# Optimizing a Trainium2 kernel written in Bass

```python
import math
import jax, jax.numpy as jnp
from jax import lax
import numpy as np

D_MODEL = 1024
BATCH = 1
SEQ = 256
DEPTH = 2

HEAD_DIM = 64
SWEEP_BLOCK = 128
RMS_EPS = 1e-6
NEG_INF = -1e30

MLA_HEADS = 8
MLA_Q_RANK = 256
MLA_KV_RANK = 128
MLA_NOPE = 64
MLA_ROPE = 32
MLA_V = 64
ROPE_THETA = 10000.0

SWA_HEADS = 8
SWA_KV_HEADS = 2
SWA_WINDOW = 128

MOBA_HEADS = 8
MOBA_BLOCK = 256
MOBA_TOPK = 3

SB_HEADS = 8

REL_BUCKETS = 32
REL_MAX_DIST = 2048
REL_HEADS = 8

N_GROUPS = 4
EXPERTS_PER_GROUP = 8
N_EXPERTS = N_GROUPS * EXPERTS_PER_GROUP
EXPERT_TOPK = 2
D_EXPERT = 256
MOE_CHUNK = 128

N_EVEN = (DEPTH + 1) // 2
N_ODD = DEPTH // 2

SWA_Q_W = SWA_HEADS * HEAD_DIM
SWA_KV_W = SWA_KV_HEADS * HEAD_DIM
IN_EVEN = MLA_Q_RANK + MLA_KV_RANK + MLA_ROPE + SWA_Q_W + 2 * SWA_KV_W
SPLIT_EVEN = (MLA_Q_RANK, MLA_Q_RANK + MLA_KV_RANK, MLA_Q_RANK + MLA_KV_RANK + MLA_ROPE,
              MLA_Q_RANK + MLA_KV_RANK + MLA_ROPE + SWA_Q_W,
              MLA_Q_RANK + MLA_KV_RANK + MLA_ROPE + SWA_Q_W + SWA_KV_W)
MIX_EVEN = MLA_HEADS * MLA_V + SWA_HEADS * HEAD_DIM
IN_ODD = 3 * (MOBA_HEADS + SB_HEADS) * HEAD_DIM
MIX_ODD = (MOBA_HEADS + SB_HEADS) * HEAD_DIM

kernel_name = "hybrid_mla_swa_moba_stickbreak_hmoe"

def rms_norm(x, g):
    xf = x.astype(jnp.float32)
    y = xf * lax.rsqrt(jnp.mean(xf * xf, axis=-1, keepdims=True) + RMS_EPS)
    return (y * g.astype(jnp.float32)).astype(x.dtype)

def rope(x):
    T, R = x.shape[1], x.shape[-1]
    freqs = ROPE_THETA ** (-jnp.arange(0, R, 2, dtype=jnp.float32) / R)
    ang = jnp.arange(T, dtype=jnp.float32)[:, None] * freqs[None, :]
    shape = (T,) + (1,) * (x.ndim - 3) + (R // 2,)
    cos, sin = jnp.cos(ang).reshape(shape), jnp.sin(ang).reshape(shape)
    xf = x.astype(jnp.float32)
    x1, x2 = xf[..., : R // 2], xf[..., R // 2:]
    return jnp.concatenate([x1 * cos - x2 * sin, x2 * cos + x1 * sin], axis=-1).astype(x.dtype)

def t5_bucket(dist):
    n = jnp.maximum(dist, 0)
    max_exact = REL_BUCKETS // 2
    nf = jnp.maximum(n, 1).astype(jnp.float32)
    large = max_exact + (jnp.log(nf / max_exact) / math.log(REL_MAX_DIST / max_exact)
                         * (REL_BUCKETS - max_exact)).astype(jnp.int32)
    large = jnp.minimum(large, REL_BUCKETS - 1)
    return jnp.where(n < max_exact, n, large)

def rel_bias(dist, table):
    return jnp.moveaxis(table[t5_bucket(dist)].astype(jnp.float32), -1, 0)

def mla_attention(q_nope, q_rope, k_nope, k_rope, v):
    B_, T, H, _ = q_nope.shape
    scale = (MLA_NOPE + MLA_ROPE) ** -0.5
    kpos = jnp.arange(T)

    def block(i):
        start = i * SWEEP_BLOCK
        qn = lax.dynamic_slice_in_dim(q_nope, start, SWEEP_BLOCK, axis=1)
        qr = lax.dynamic_slice_in_dim(q_rope, start, SWEEP_BLOCK, axis=1)
        s = (jnp.einsum('bqhd,bkhd->bhqk', qn, k_nope)
             + jnp.einsum('bqhr,bkr->bhqk', qr, k_rope)).astype(jnp.float32) * scale
        qpos = start + jnp.arange(SWEEP_BLOCK)
        s = jnp.where(kpos[None, :] <= qpos[:, None], s, NEG_INF)
        p = jax.nn.softmax(s, axis=-1).astype(v.dtype)
        return jnp.einsum('bhqk,bkhd->bqhd', p, v)

    out = lax.map(block, jnp.arange(T // SWEEP_BLOCK))
    return out.transpose(1, 0, 2, 3, 4).reshape(B_, T, H, -1)

def swa_attention(q, k, v, sinks, rel_table):
    B_, T, Hq, D = q.shape
    Hkv = k.shape[2]
    G = Hq // Hkv
    nb = T // SWEEP_BLOCK
    Q = SWEEP_BLOCK
    qb = q.reshape(B_, nb, Q, Hkv, G, D)
    pad = ((0, 0), (Q, 0), (0, 0), (0, 0))
    kb = jnp.pad(k, pad).reshape(B_, nb + 1, Q, Hkv, D)
    vb = jnp.pad(v, pad).reshape(B_, nb + 1, Q, Hkv, D)
    kw = jnp.concatenate([kb[:, :-1], kb[:, 1:]], axis=2)
    vw = jnp.concatenate([vb[:, :-1], vb[:, 1:]], axis=2)
    s = jnp.einsum('bnqhgd,bnkhd->bhgnqk', qb, kw).astype(jnp.float32) * D ** -0.5
    qpos = jnp.arange(nb)[:, None] * Q + jnp.arange(Q)[None, :]
    kpos = (jnp.arange(nb)[:, None] - 1) * Q + jnp.arange(2 * Q)[None, :]
    dist = qpos[:, :, None] - kpos[:, None, :]
    valid = (dist >= 0) & (dist < SWA_WINDOW) & (kpos[:, None, :] >= 0)
    s = s + rel_bias(dist, rel_table).reshape(Hkv, G, nb, Q, 2 * Q)
    s = jnp.where(valid, s, NEG_INF)
    sink = jnp.broadcast_to(sinks.astype(jnp.float32).reshape(1, Hkv, G, 1, 1, 1), s.shape[:-1] + (1,))
    p = jax.nn.softmax(jnp.concatenate([s, sink], axis=-1), axis=-1)[..., :-1]
    out = jnp.einsum('bhgnqk,bnkhd->bnqhgd', p.astype(v.dtype), vw)
    return out.reshape(B_, T, Hq, D)

def moba_attention(q, k, v, rel_table):
    B_, T, H, D = q.shape
    L = MOBA_BLOCK
    nkb = -(-T // L)
    Tp = nkb * L
    topk = min(MOBA_TOPK, nkb)
    scale = D ** -0.5
    qh = q.transpose(0, 2, 1, 3)
    kp = jnp.pad(k.transpose(0, 2, 1, 3), ((0, 0), (0, 0), (0, Tp - T), (0, 0)))
    vp = jnp.pad(v.transpose(0, 2, 1, 3), ((0, 0), (0, 0), (0, Tp - T), (0, 0)))
    kblk = kp.reshape(B_, H, nkb, L, D)
    vblk = vp.reshape(B_, H, nkb, L, D)
    kmean = jnp.mean(kblk.astype(jnp.float32), axis=3)
    table_h = rel_table.T
    bi = jnp.arange(B_)[:, None, None, None]
    hi = jnp.arange(H)[None, :, None, None]
    Q = SWEEP_BLOCK

    def block(i):
        start = i * Q
        own = start // L
        qc = lax.dynamic_slice_in_dim(qh, start, Q, axis=2)
        qpos = start + jnp.arange(Q)
        gsc = jnp.einsum('bhqd,bhnd->bhqn', qc.astype(jnp.float32), kmean)
        gsc = jnp.where(jnp.arange(nkb) < own, gsc, NEG_INF)
        _, sel = lax.top_k(gsc, topk)
        sel_valid = sel < own
        ks = kblk[bi, hi, sel]
        vs = vblk[bi, hi, sel]
        s_sel = jnp.einsum('bhqd,bhqkld->bhqkl', qc, ks).astype(jnp.float32) * scale
        kpos_sel = sel[..., None] * L + jnp.arange(L)
        dist_sel = qpos[:, None, None] - kpos_sel
        s_sel = s_sel + table_h[hi[..., None], t5_bucket(dist_sel)].astype(jnp.float32)
        s_sel = jnp.where(sel_valid[..., None], s_sel, NEG_INF).reshape(B_, H, Q, topk * L)
        kown = lax.dynamic_slice_in_dim(kp, own * L, L, axis=2)
        vown = lax.dynamic_slice_in_dim(vp, own * L, L, axis=2)
        s_own = jnp.einsum('bhqd,bhld->bhql', qc, kown).astype(jnp.float32) * scale
        dist_own = qpos[:, None] - (own * L + jnp.arange(L))[None, :]
        s_own = s_own + rel_bias(dist_own, rel_table)[None]
        s_own = jnp.where(dist_own >= 0, s_own, NEG_INF)
        p = jax.nn.softmax(jnp.concatenate([s_sel, s_own], axis=-1), axis=-1)
        p_sel = p[..., : topk * L].reshape(B_, H, Q, topk, L).astype(v.dtype)
        p_own = p[..., topk * L:].astype(v.dtype)
        return (jnp.einsum('bhqkl,bhqkld->bhqd', p_sel, vs)
                + jnp.einsum('bhql,bhld->bhqd', p_own, vown))

    out = lax.map(block, jnp.arange(T // Q))
    return out.transpose(1, 0, 3, 2, 4).reshape(B_, T, H, D)

def stick_breaking_attention(q, k, v):
    B_, T, H, D = q.shape
    scale = D ** -0.5
    kpos = jnp.arange(T)

    def block(i):
        start = i * SWEEP_BLOCK
        qc = lax.dynamic_slice_in_dim(q, start, SWEEP_BLOCK, axis=1)
        z = jnp.einsum('bqhd,bkhd->bhqk', qc, k).astype(jnp.float32) * scale
        qpos = start + jnp.arange(SWEEP_BLOCK)
        past = kpos[None, :] < qpos[:, None]
        log_1m = jnp.where(past, jax.nn.log_sigmoid(-z), 0.0)
        after = lax.cumsum(log_1m, axis=3, reverse=True) - log_1m
        w = jnp.where(past, jnp.exp(jax.nn.log_sigmoid(z) + after), 0.0)
        return jnp.einsum('bhqk,bkhd->bqhd', w.astype(v.dtype), v)

    out = lax.map(block, jnp.arange(T // SWEEP_BLOCK))
    return out.transpose(1, 0, 2, 3, 4).reshape(B_, T, H, D)

def even_mixer(u, w_in, g_q, g_kv, w_qb, w_kvb, sinks, w_out, rel_table):
    B_, T, _ = u.shape
    cq, ckv, kr, qs, ks, vs = jnp.split(u @ w_in, SPLIT_EVEN, axis=-1)
    q = (rms_norm(cq, g_q) @ w_qb).reshape(B_, T, MLA_HEADS, MLA_NOPE + MLA_ROPE)
    kv = (rms_norm(ckv, g_kv) @ w_kvb).reshape(B_, T, MLA_HEADS, MLA_NOPE + MLA_V)
    o_a = mla_attention(q[..., :MLA_NOPE], rope(q[..., MLA_NOPE:]),
                        kv[..., :MLA_NOPE], rope(kr), kv[..., MLA_NOPE:]).reshape(B_, T, -1)
    o_b = swa_attention(qs.reshape(B_, T, SWA_HEADS, HEAD_DIM),
                        ks.reshape(B_, T, SWA_KV_HEADS, HEAD_DIM),
                        vs.reshape(B_, T, SWA_KV_HEADS, HEAD_DIM), sinks, rel_table).reshape(B_, T, -1)
    return jnp.concatenate([o_a, o_b], axis=-1) @ w_out

def odd_mixer(u, w_in, w_out, rel_table):
    B_, T, _ = u.shape
    parts = [p.reshape(B_, T, -1, HEAD_DIM) for p in jnp.split(u @ w_in, 6, axis=-1)]
    qc, kc, vc, qd, kd, vd = parts
    o_c = moba_attention(qc, kc, vc, rel_table).reshape(B_, T, -1)
    o_d = stick_breaking_attention(qd, kd, vd).reshape(B_, T, -1)
    return jnp.concatenate([o_c, o_d], axis=-1) @ w_out

def hier_moe(u, w_group, b_group, w_router, b_router, w_gate, w_up, w_down):
    B_, T, D = u.shape
    uf = u.reshape(-1, D)
    N = uf.shape[0]
    glog = (uf @ w_group).astype(jnp.float32) + b_group.astype(jnp.float32)
    gprob = jax.nn.softmax(glog, axis=-1)
    g_sel = jnp.argmax(glog, axis=-1)
    g_gate = jnp.take_along_axis(gprob, g_sel[:, None], axis=-1)
    elog = ((uf @ w_router).astype(jnp.float32) + b_router.astype(jnp.float32)).reshape(N, N_GROUPS, EXPERTS_PER_GROUP)
    elog_g = jnp.take_along_axis(elog, g_sel[:, None, None], axis=1)[:, 0]
    top_p, top_i = lax.top_k(jax.nn.softmax(elog_g, axis=-1), EXPERT_TOPK)
    top_p = top_p / jnp.sum(top_p, axis=-1, keepdims=True)
    expert_id = g_sel[:, None] * EXPERTS_PER_GROUP + top_i
    combine = jnp.sum(jax.nn.one_hot(expert_id, N_EXPERTS, dtype=jnp.float32)
                      * (g_gate * top_p)[..., None], axis=1)

    def chunk(args):
        xc, cc = args
        h = jax.nn.silu(jnp.einsum('nd,edf->nef', xc, w_gate)) * jnp.einsum('nd,edf->nef', xc, w_up)
        h = h * cc[..., None].astype(h.dtype)
        return jnp.einsum('nef,efd->nd', h, w_down)

    y = lax.map(chunk, (uf.reshape(-1, MOE_CHUNK, D), combine.reshape(-1, MOE_CHUNK, N_EXPERTS)))
    return y.reshape(B_, T, D)

def setup_inputs(seed: int = 0) -> dict:
    key = jax.random.key(seed)
    k = jax.random.split(key, 21)
    f32 = jnp.float32
    nrm = lambda kk, shape, fan_in: jax.random.normal(kk, shape, f32) * fan_in ** -0.5
    gain = lambda kk, shape: 1.0 + 0.05 * jax.random.normal(kk, shape, f32)
    return {
        "x": jax.random.normal(k[0], (BATCH, SEQ, D_MODEL), f32),
        "norm_mix": gain(k[1], (DEPTH, D_MODEL)),
        "norm_ffn": gain(k[2], (DEPTH, D_MODEL)),
        "norm_final": gain(k[3], (D_MODEL,)),
        "rel_bias_table": 0.3 * jax.random.normal(k[4], (REL_BUCKETS, REL_HEADS), f32),
        "w_in_even": nrm(k[5], (N_EVEN, D_MODEL, IN_EVEN), D_MODEL),
        "g_mla_q": gain(k[6], (N_EVEN, MLA_Q_RANK)),
        "g_mla_kv": gain(k[7], (N_EVEN, MLA_KV_RANK)),
        "w_mla_qb": nrm(k[8], (N_EVEN, MLA_Q_RANK, MLA_HEADS * (MLA_NOPE + MLA_ROPE)), MLA_Q_RANK),
        "w_mla_kvb": nrm(k[9], (N_EVEN, MLA_KV_RANK, MLA_HEADS * (MLA_NOPE + MLA_V)), MLA_KV_RANK),
        "swa_sinks": 0.5 * jax.random.normal(k[10], (N_EVEN, SWA_HEADS), f32),
        "w_out_even": nrm(k[11], (N_EVEN, MIX_EVEN, D_MODEL), MIX_EVEN),
        "w_in_odd": nrm(k[12], (N_ODD, D_MODEL, IN_ODD), D_MODEL),
        "w_out_odd": nrm(k[13], (N_ODD, MIX_ODD, D_MODEL), MIX_ODD),
        "moe_w_group": nrm(k[14], (DEPTH, D_MODEL, N_GROUPS), D_MODEL),
        "moe_b_group": 0.01 * jax.random.normal(k[15], (DEPTH, N_GROUPS), f32),
        "moe_w_router": nrm(k[16], (DEPTH, D_MODEL, N_EXPERTS), D_MODEL),
        "moe_b_router": 0.01 * jax.random.normal(k[17], (DEPTH, N_EXPERTS), f32),
        "moe_w_gate": nrm(k[18], (DEPTH, N_EXPERTS, D_MODEL, D_EXPERT), D_MODEL),
        "moe_w_up": nrm(k[19], (DEPTH, N_EXPERTS, D_MODEL, D_EXPERT), D_MODEL),
        "moe_w_down": nrm(k[20], (DEPTH, N_EXPERTS, D_EXPERT, D_MODEL), D_EXPERT),
    }

def reference(x, norm_mix, norm_ffn, norm_final, rel_bias_table, w_in_even, g_mla_q, g_mla_kv,
              w_mla_qb, w_mla_kvb, swa_sinks, w_out_even, w_in_odd, w_out_odd, moe_w_group,
              moe_b_group, moe_w_router, moe_b_router, moe_w_gate, moe_w_up, moe_w_down):
    h = x
    for layer in range(DEPTH):
        j = layer // 2
        u = rms_norm(h, norm_mix[layer])
        if layer % 2 == 0:
            h = h + even_mixer(u, w_in_even[j], g_mla_q[j], g_mla_kv[j], w_mla_qb[j], w_mla_kvb[j],
                               swa_sinks[j], w_out_even[j], rel_bias_table)
        else:
            h = h + odd_mixer(u, w_in_odd[j], w_out_odd[j], rel_bias_table)
        u = rms_norm(h, norm_ffn[layer])
        h = h + hier_moe(u, moe_w_group[layer], moe_b_group[layer], moe_w_router[layer], moe_b_router[layer],
                         moe_w_gate[layer], moe_w_up[layer], moe_w_down[layer])
    return rms_norm(h, norm_final)


_drawn_inputs = setup_inputs


def setup_inputs(seed=0):
    import zlib

    import numpy as np

    out = dict(_drawn_inputs(seed))
    spreads = {}
    factors = {'moe_b_group': 8.0, 'moe_b_router': 2.816}
    for name, (base, spread) in spreads.items():
        noise = np.random.default_rng([zlib.crc32(name.encode()), seed]).standard_normal(out[name].shape)
        drawn = base * np.exp(spread * noise) if base else spread * noise
        out[name] = __import__('jax').numpy.asarray(drawn.astype(out[name].dtype))
    for name, factor in factors.items():
        out[name] = (out[name] * factor).astype(out[name].dtype)
    return out
```

```python
from contextlib import ExitStack

import numpy as np

import concourse.bass as bass
from concourse import mybir

F32 = mybir.dt.float32
I32 = mybir.dt.int32
ALU = mybir.AluOpType
ACT = mybir.ActivationFunctionType
AX = mybir.AxisListType

P = 128
T = 256
TT = T // P
D = 1024
KD = D // P
HALF = D // 2
HEADS = 8
HD = 64
DEPTH = 2
EPS = 1e-6
NEG = -1e30
MLA_QR, MLA_KVR, ROPE = 256, 128, 32
MLA_SCALE = float(HD + ROPE) ** -0.5
HEAD_SCALE = float(HD) ** -0.5
WINDOW = 128
BUCKETS, MAX_DIST = 32, 2048
GROUPS, PER_GROUP = 4, 8
EXPERTS = GROUPS * PER_GROUP
FE = 256
SLOTS = 32
LOT = P // SLOTS
LOTS = EXPERTS // LOT
ROUNDS = T // SLOTS
BUILDS = LOTS + 1
RING = 6
SLOT_COLS = KD * HALF
BLK = T + P


def shape_constants():
    p = np.arange(P)[:, None]
    q = np.arange(P)
    t = np.arange(T)
    parts = {}
    parts["ident"] = (p == q[None]).astype(np.float32)
    parts["earlier"] = (p < q[None]).astype(np.float32)
    parts["ones"] = np.ones((P, P), np.float32)
    parts["stack"] = (p % SLOTS == np.arange(SLOTS)[None]).astype(np.float32)
    parts["iota"] = np.broadcast_to(q.astype(np.float32), (P, P))
    parts["first4"] = np.broadcast_to(np.arange(GROUPS, 0, -1, dtype=np.float32), (P, GROUPS))
    parts["first32"] = np.broadcast_to(np.arange(EXPERTS, 0, -1, dtype=np.float32), (P, EXPERTS))
    parts["slot0"] = np.broadcast_to(SLOTS * np.arange(EXPERTS, dtype=np.float32), (P, EXPERTS))
    parts["limits"] = np.broadcast_to(SLOTS * np.arange(1, ROUNDS, dtype=np.float32), (P, ROUNDS - 1))
    freqs = (np.float32(10000.0) ** (-np.arange(0, ROPE, 2, dtype=np.float32) / np.float32(ROPE))).astype(np.float32)
    ang = np.arange(T, dtype=np.float32)[None, :] * freqs[:, None]
    cos, sin = np.cos(ang).astype(np.float32), np.sin(ang).astype(np.float32)
    one = np.ones((HD, T), np.float32)
    parts["qrope"] = np.concatenate([one, cos, cos, sin, -sin])
    parts["kcos"] = np.concatenate([one, cos, cos, cos, cos])
    parts["ksin"] = np.concatenate([one, -sin, sin, sin, -sin])
    k2, k1 = t[None, :], q[None, :]
    parts["causal"] = np.concatenate([np.where(k2 <= p + P, 0.0, NEG), np.where(k1 <= p, 0.0, NEG)], 1)
    parts["strict"] = np.concatenate([np.where(k2 < p + P, 0.0, NEG), np.where(k1 < p, 0.0, NEG)], 1)
    carry = np.ones((P, BLK))
    carry[:, [T - 1, BLK - 1]] = 0.0
    parts["carry"] = carry
    at, n = {}, 0
    for name, a in parts.items():
        at[name] = (n, n + a.shape[1])
        n += a.shape[1]
    return np.ascontiguousarray(np.concatenate([np.asarray(a, np.float32) for a in parts.values()], 1)), at


def distance_constants():
    dist = T - 1 - np.arange(BLK)
    n = np.maximum(dist, 0)
    exact = BUCKETS // 2
    nf = np.maximum(n, 1).astype(np.float32)
    large = exact + (np.log(nf / np.float32(exact)) / np.float32(np.log(MAX_DIST / exact))
                     * np.float32(BUCKETS - exact)).astype(np.int32)
    bucket = np.where(n < exact, n, np.minimum(large, BUCKETS - 1))
    onehot = (np.arange(BUCKETS)[:, None] == bucket[None]).astype(np.float32)
    window = np.where((dist >= 0) & (dist < WINDOW), 0.0, NEG)
    causal = np.where(dist >= 0, 0.0, NEG)
    masks = np.broadcast_to(np.stack([window, causal]), (HEADS, 2, BLK)).astype(np.float32)
    return np.ascontiguousarray(onehot), np.ascontiguousarray(masks)


PAR = {}
_n = 0
for _name, _w in (("gmix0", KD), ("gmix1", KD), ("gffn0", KD), ("gffn1", KD), ("gq", 2), ("gkv", 1),
                  ("sinks", HEADS), ("rbias0", GROUPS + EXPERTS), ("rbias1", GROUPS + EXPERTS), ("gfinal", D)):
    PAR[_name] = (_n, _n + _w)
    _n += _w
PAR_COLS = _n


class Banks:

    def __init__(self, nc, ctx):
        self.t = [ctx.enter_context(nc.psum_tensor(f"bank{i}", [P, 512], F32)) for i in range(8)]
        self.full = [ctx.enter_context(nc.semaphore(f"bank{i}_full")) for i in range(8)]
        self.free = [ctx.enter_context(nc.semaphore(f"bank{i}_free")) for i in range(8)]
        self.uses = [0] * 8
        self.at = {}

    def plan(self, key, bank):
        self.at[key] = (bank, self.uses[bank])
        self.uses[bank] += 1

    def begin(self, pe, key):
        b, n = self.at[key]
        if n:
            pe.wait_ge(self.free[b], n)
        return self.t[b]

    def written(self, ins, key):
        ins.then_inc(self.full[self.at[key][0]], 1)

    def read(self, eng, key):
        b, n = self.at[key]
        eng.wait_ge(self.full[b], n + 1)
        return self.t[b]

    def taken(self, eng, key):
        b, n = self.at[key]
        eng.wait_ge(self.free[b], n + 1)

    def release(self, ins, key):
        ins.then_inc(self.free[self.at[key][0]], 1)


class Steps:

    def __init__(self, sem):
        self.sem, self.n = sem, 0

    def __call__(self, eng, ins):
        self.n += 1
        ins.then_inc(self.sem, 1)
        eng.wait_ge(self.sem, self.n)


def trunk(nc, x, stream, kvb, router_w, params, table, consts, onehot, masks, w_gate, w_up, w_down, out, at):
    ctx = ExitStack()
    with ctx:
        def sb(name, shape, dt=F32):
            return ctx.enter_context(nc.sbuf_tensor(name, shape, dt))

        sems = {}

        def sem(name):
            if name not in sems:
                sems[name] = ctx.enter_context(nc.semaphore(name))
            return sems[name]

        B = Banks(nc, ctx)
        bank = B.t
        bias_rows = nc.dram_tensor("bias_rows", [2, HEADS, P * (BLK + 1)], F32, kind="Internal").ap()

        ring = sb("ring", [P, RING, SLOT_COLS])
        con = sb("con", [P, consts.shape[1]])
        par = sb("par", [P, PAR_COLS])
        rw = sb("rw", [P, DEPTH, KD, GROUPS + EXPERTS])
        tab = sb("tab", [BUCKETS, HEADS])
        hot = sb("hot", [BUCKETS, BLK])
        msk = sb("msk", [HEADS, 2, BLK])
        rows = sb("rows", [HEADS, 2, BLK])
        h = sb("h", [P, TT, D])
        u = sb("u", [P, TT, D])
        uT = sb("uT", [P, KD, T])
        qT = sb("qT", [P, HEADS, T])
        kT = sb("kT", [P, HEADS, T])
        swq = sb("swq", [P, 4, T])
        swk = sb("swk", [P, T])
        v1 = sb("v1", [P, TT, 512])
        v2 = sb("v2", [P, TT, 512])
        bias = sb("bias", [P, HEADS, BLK])
        sc = sb("sc", [P, 3, BLK])
        pr = sb("pr", [P, 3, BLK])
        cs = sb("cs", [P, 2, BLK])
        pt = sb("pt", [P, 2, BLK])
        nm = sb("nm", [P, 3, 8])
        nsink = sb("nsink", [P, HEADS])
        st = sb("st", [P, 16])
        lg = sb("lg", [P, TT, GROUPS + EXPERTS])
        mem = sb("mem", [P, TT, EXPERTS])
        nrounds = sb("nrounds", [P, 1], I32)
        rank = sb("rank", [P, TT, 2])
        base = sb("base", [P, TT, 2])
        gate = sb("gate", [P, TT, 2])
        cur = sb("cur", [P, TT, 2])
        sil = sb("sil", [P, 2, P])
        hT = sb("hT", [P, 2, P])

        def view(tile, a, shape):
            flat = tile[:, :, :].rearrange("p a b -> p (a b)")[:, a:a + int(np.prod(shape))]
            names = " ".join("abc"[:len(shape)])
            sizes = dict(zip("abc"[1:], shape[1:]))
            return flat.rearrange(f"p ({names}) -> p {names}", **sizes) if len(shape) > 1 else flat

        junk = view(kT, 0, [D])
        oT = view(u, 0, [KD, T])
        low, lowsq = sc[:, :, 0:T], pr[:, :, 0:T]
        lowr, krt = cs[:, :, 0:T], pt[:, :, 0:T]
        rt = view(v1, 0, [16, TT, EXPERTS])
        sel = view(v2, 0, [TT, P])
        wsel = view(v2, TT * P, [TT * 2, P])
        wT = view(v2, 3 * TT * P, [T])
        xg = view(bias, 0, [KD, P])
        part = view(bias, D, [2, 512])
        ys = view(bias, 2 * D, [2, HALF])

        def c(name, rows_=slice(0, P)):
            return con[rows_, at[name][0]:at[name][1]]

        def pcol(name, k=None):
            a, b = PAR[name]
            return par[:, a:b] if k is None else par[:, a + k:a + k + 1]

        ident, ones = c("ident"), c("ones")

        def win(s):
            return ring[:, s, :].rearrange("p (k n) -> p k n", k=KD)

        B.plan("rows", 7)
        upto = []
        for l in range(DEPTH):
            for b in range(4):
                B.plan(("uT", l, "mix", b), b)
            if l == 0:
                for i, b in enumerate((4, 5, 6, 7)):
                    B.plan(("low", i), b)
                for i in range(2):
                    B.plan(("swq", i), i)
                B.plan("swk", 2)
                B.plan("ssq", 4)
                B.plan("swv", 3)
                for i in range(4):
                    B.plan(("mq", i), (0, 1, 5, 6)[i])
                for i in range(4):
                    B.plan(("mk", i), (7, 2, 3, 4)[i])
                for i in range(TT):
                    B.plan(("mv", i), i)
            else:
                for i in range(12):
                    B.plan(("in1", i), (4 + i) % 8)
            for n in range(2 * HEADS):
                B.plan(("s", l, n), n % 3)
                B.plan(("t", l, n), 3 + n % 2)
                if n % 2 == 0:
                    B.plan(("o", l, n // 2), 5 + (n // 2) % 3)
            for i in range(4):
                B.plan(("out", l, i), i)
            for b in range(4):
                B.plan(("uT", l, "ffn", b), 4 + b)
            B.plan(("route", l), 0)
            B.plan(("rank", l), 1)
            upto.append(list(B.uses))

        slot_use = {("in", 0): 0, ("moe", 0): 1, ("in", 1): 1 + LOTS, ("out", 1): 2 + LOTS}
        moe1 = [3 + LOTS] * 2 + [2 + LOTS] * 4
        moe0 = [1] * RING

        def landed(eng, s, n):
            eng.wait_ge(sem(f"slot{s}_landed"), 16 * (n + 1))

        land = {("in", 0): [0] * RING, ("moe", 0): [16] * RING,
                ("in", 1): [16 + 32 * LOTS] * RING, ("out", 1): [32 + 32 * LOTS] * RING,
                ("moe", 1): [48 + 32 * LOTS] * 2 + [32 + 32 * LOTS] * 4}

        def arrived(eng, phase, s):
            eng.wait_ge(sem(f"slot{s}_landed"), land[phase][s] + 16)

        class Set:

            def __init__(self, name, l, ring_base, land_base, own):
                self.name, self.l, self.free_base, self.land_base = name, l, ring_base, land_base
                self.sel_built = sem(f"{name}_sel_built")
                self.sel_step = sem(f"{name}_sel_step")
                self.gathered = sem(f"{name}_gathered")
                self.x_ready = sem(f"{name}_x_ready")
                self.w_turned = sem(f"{name}_w_turned")
                self.w_ready = sem(f"{name}_w_ready")
                self.part_ready = sem(f"{name}_part_ready")
                self.summed = sem(f"{name}_summed")
                self.silu_ready = sem(f"{name}_silu_ready")
                self.h_ready = sem(f"{name}_h_ready")
                self.y_done = sem(f"{name}_y_done")
                self.y0_ready = sem(f"{name}_y0_ready")
                self.y1_ready = sem(f"{name}_y1_ready")
                self.combined = sem(f"{name}_combined")
                self.added = sem(f"{name}_added")
                self.landed = [sem(f"{'more' + str(l) + '_' if own else ''}slot{s}_landed") for s in range(RING)]
                self.freed = [sem(f"{'more' + str(l) + '_' if own else ''}slot{s}_freed") for s in range(RING)]

        main = [Set("moe", l, [n - LOTS * l for n in (moe0, moe1)[l]],
                    [n - 32 * LOTS * l for n in land[("moe", l)]], False) for l in range(DEPTH)]
        more = [Set(f"more{l}", l, [1] * RING, [0] * RING, True) for l in range(DEPTH)]

        PLACING = 6
        def h_complete(eng, i):
            if i == 0:
                eng.wait_ge(sem("x_loaded"), 16)
            elif i % 2:
                for b in range(4):
                    B.taken(eng, ("out", i // 2, b))
            else:
                eng.wait_ge(sem(f"moe_added{i // 2 - 1}"), 1)

        def pv_done(eng, l, n):
            if n % 2 == 0:
                eng.wait_ge(sem(f"pv_even{l}"), n // 2 + 1)
            else:
                B.read(eng, ("o", l, n // 2))

        def swa_head(n):
            return (n - HEADS) // 2 + 4 * (n % 2)

        def in1_reads(eng, e, which):
            dst = ([qT[:, 2 * i:2 * i + 2, :] for i in (0, 1)] + [kT[:, 2 * i:2 * i + 2, :] for i in (0, 1)]
                   + [v1[:, i, :] for i in range(TT)]
                   + [qT[:, 4 + 2 * i:6 + 2 * i, :] for i in (0, 1)] + [kT[:, 4 + 2 * i:6 + 2 * i, :] for i in (0, 1)]
                   + [v2[:, i, :] for i in range(TT)])
            for i in range(12):
                if i % 2 == which:
                    src = B.read(eng, ("in1", i))
                    o = dst[i]
                    s = src[:, :] if i in (4, 5, 10, 11) else src[:, :].rearrange("p (c t) -> p c t", c=2)
                    if which:
                        ins = e.activation(o, s, ACT.Copy)
                    else:
                        ins = e.tensor_copy(o, s)
                    B.release(ins, ("in1", i))

        def act_lot(act, q, it):
            for e in range(LOT):
                act.wait_ge(q.freed[e], q.free_base[e] + 1 + it)
                if e >= 2:
                    act.wait_ge(q.summed, it * LOT + (e - 1))
                nc.scalar.activation(part[:, e % 2, :], bank[e % 2][:, :], ACT.Copy).then_inc(q.part_ready, 1)
            act.wait_ge(q.summed, it * LOT + LOT)
            nc.scalar.activation(sil[:, :, :], bank[2][:, 0:2 * P].rearrange("p (j s) -> p j s", j=2),
                                 ACT.Silu).then_inc(q.silu_ready, 1)
            act.wait_ge(q.y_done, it + 1)
            nc.scalar.activation(ys[:, 0, :], bank[4][:, :], ACT.Copy).then_inc(q.y0_ready, 1)

        def route(dve, V, l, step):
            NG = GROUPS

            def wide(a, n):
                return a.unsqueeze(2).broadcast_to([P, TT, n])

            src = B.read(dve, ("route", l))
            rb = pcol(f"rbias{l}").unsqueeze(1).broadcast_to([P, TT, NG + EXPERTS])
            ins = V.tensor_tensor(lg[:, :, :], src[:, 0:TT * (NG + EXPERTS)].rearrange("p (t n) -> p t n", t=TT),
                                  rb, ALU.add)
            B.release(ins, ("route", l))
            B.taken(dve, ("route", l))
            G, E = lg[:, :, 0:NG], lg[:, :, NG:]
            best = rt[:, 0, :, 0:8]

            def col(i):
                return best[:, :, i]

            step(dve, V.tensor_reduce(col(0), G, AX.X, ALU.max))
            V.tensor_tensor(rt[:, 1, :, 0:NG], G, wide(col(0), NG), ALU.subtract).then_inc(sem(f"glog_ready{l}"), 1)

            def first_max(x_, top, order, n_, tmp, mark):
                step(dve, V.tensor_tensor(tmp, x_, wide(top, n_), ALU.is_equal))
                step(dve, V.tensor_tensor(tmp, tmp, order.unsqueeze(1).broadcast_to([P, TT, n_]), ALU.mult))
                step(dve, V.tensor_reduce(col(1), tmp, AX.X, ALU.max))
                step(dve, V.tensor_tensor(mark, tmp, wide(col(1), n_), ALU.is_equal))

            first_max(G, col(0), c("first4"), NG, rt[:, 2, :, 0:NG], rt[:, 3, :, 0:NG])
            step(dve, V.tensor_scalar(rt[:, 2, :, 0:NG], rt[:, 3, :, 0:NG], 1.0, -NEG, ALU.subtract, ALU.mult))
            step(dve, V.tensor_tensor(rt[:, 4, :, :].rearrange("p t (g e) -> p t g e", g=NG),
                                      E.rearrange("p t (g e) -> p t g e", g=NG),
                                      rt[:, 2, :, 0:NG].unsqueeze(3).broadcast_to([P, TT, NG, PER_GROUP]), ALU.add))
            step(dve, V.tensor_reduce(col(2), rt[:, 4, :, :], AX.X, ALU.max))
            first_max(rt[:, 4, :, :], col(2), c("first32"), EXPERTS, rt[:, 5, :, :], rt[:, 6, :, :])
            step(dve, V.scalar_tensor_tensor(out=rt[:, 4, :, :], in0=rt[:, 6, :, :], scalar=3.0 * NEG,
                                             in1=rt[:, 4, :, :], op0=ALU.mult, op1=ALU.add))
            step(dve, V.tensor_reduce(col(3), rt[:, 4, :, :], AX.X, ALU.max))
            first_max(rt[:, 4, :, :], col(3), c("first32"), EXPERTS, rt[:, 5, :, :], rt[:, 7, :, :])
            V.tensor_tensor(mem[:, :, :], rt[:, 6, :, :], rt[:, 7, :, :], ALU.add).then_inc(sem("members"), 1)
            V.tensor_tensor(st[:, 10:12], col(3), col(2), ALU.subtract).then_inc(sem(f"gap_ready{l}"), 1)
            dve.wait_ge(sem(f"gexp_ready{l}"), 1)
            step(dve, V.tensor_reduce(col(4), rt[:, 1, :, 0:NG], AX.X, ALU.add))
            dve.wait_ge(sem(f"gapexp_ready{l}"), 1)
            step(dve, V.scalar_tensor_tensor(out=col(5), in0=st[:, 12:14], scalar=1.0, in1=col(4),
                                             op0=ALU.add, op1=ALU.mult))
            step(dve, V.reciprocal(gate[:, :, 0], col(5)))
            step(dve, V.tensor_tensor(gate[:, :, 1], gate[:, :, 0], st[:, 12:14], ALU.mult))
            src = B.read(dve, ("rank", l))
            for i in range(2):
                mark = rt[:, 6 + i, :, :]
                step(dve, V.tensor_tensor(rt[:, 8 + i, :, :], mark,
                                          src[:, 0:TT * EXPERTS].rearrange("p (t e) -> p t e", t=TT), ALU.mult))
                step(dve, V.tensor_reduce(rank[:, :, i], rt[:, 8 + i, :, :], AX.X, ALU.add))
                step(dve, V.tensor_tensor(rt[:, 8 + i, :, :], mark,
                                          c("slot0").unsqueeze(1).broadcast_to([P, TT, EXPERTS]), ALU.mult))
                step(dve, V.tensor_reduce(base[:, :, i], rt[:, 8 + i, :, :], AX.X, ALU.add))
            ins = V.tensor_reduce(st[:, 14:15], src[:, TT * EXPERTS:(TT + 1) * EXPERTS], AX.X, ALU.max)
            B.release(ins, ("rank", l))
            B.taken(dve, ("rank", l))
            step(dve, V.tensor_scalar(rt[:, 10, 0, 0:ROUNDS - 1], c("limits"), st[:, 14:15], None, ALU.is_lt))
            step(dve, V.tensor_reduce(st[:, 15:16], rt[:, 10, 0, 0:ROUNDS - 1], AX.X, ALU.add))
            V.tensor_scalar(nrounds[:, :], st[:, 15:16], 1.0, None, ALU.add).then_inc(sem(f"rounds_known{l}"), 1)

        def placing(V):
            ok, pos = rt[:, 11, :, 0:2], rt[:, 12, :, 0:2]
            lo = rt[:, 13, :, 0:2]
            yield V.tensor_scalar(ok, rank[:, :, :], 0.0, None, ALU.is_ge)
            yield V.tensor_scalar(lo, rank[:, :, :], float(SLOTS), None, ALU.is_lt)
            yield V.tensor_tensor(ok, ok, lo, ALU.mult)
            yield V.tensor_tensor(pos, base[:, :, :], rank[:, :, :], ALU.add)
            yield V.scalar_tensor_tensor(out=pos, in0=pos, scalar=1.0, in1=ok, op0=ALU.add, op1=ALU.mult)
            yield V.tensor_scalar(cur[:, :, :], pos, 1.0, None, ALU.subtract)

        def place(dve, V, step):
            for ins in placing(V):
                step(dve, ins)

        def next_round(dve, V, l, r):
            s = sem(f"round_step{l}")
            n = (r - 1) * (PLACING + 1)
            V.tensor_scalar(rank[:, :, :], rank[:, :, :], float(SLOTS), None, ALU.subtract).then_inc(s, 1)
            dve.wait_ge(s, n + 1)
            for k, ins in enumerate(placing(V)):
                ins.then_inc(s, 1)
                dve.wait_ge(s, n + k + 2)

        def pick(dve, V, q, n):
            for tt in range(TT):
                V.tensor_scalar(sel[:, tt, :], c("iota"), cur[:, tt, 0:1], None, ALU.is_equal).then_inc(q.sel_step, 1)
                for i in range(2):
                    V.tensor_scalar(wsel[:, 2 * tt + i, :], c("iota"), cur[:, tt, i:i + 1], gate[:, tt, i:i + 1],
                                    ALU.is_equal, ALU.mult)
            dve.wait_ge(q.sel_step, n * 5 + 2)
            for tt in range(TT):
                V.scalar_tensor_tensor(out=sel[:, tt, :], in0=c("iota"), scalar=cur[:, tt, 1:2], in1=sel[:, tt, :],
                                       op0=ALU.is_equal, op1=ALU.add).then_inc(q.sel_step, 1)
            dve.wait_ge(q.sel_step, n * 5 + 4)
            V.tensor_scalar(cur[:, :, :], cur[:, :, :], float(P), None, ALU.subtract).then_inc(q.sel_step, 1)
            dve.wait_ge(q.sel_step, n * 5 + 5)
            V.memset(st[:, 9:10], 0.0).then_inc(q.sel_built, 1)

        def pick_first(dve, V, q, n):
            pick(dve, V, q, n)

        def dve_lot(dve, V, q, it, n):
            l = q.l
            gain = par[:, PAR[f"gffn{l}"][0]:PAR[f"gffn{l}"][1]]
            for hf in range(2):
                dve.wait_ge(q.gathered, it * 2 + (hf + 1))
                ks = slice(4 * hf, 4 * hf + 4)
                V.tensor_tensor(xg[:, ks, :], bank[(3, 2)[hf]][:, :].rearrange("p (k s) -> p k s", k=4),
                                gain[:, ks].unsqueeze(2).broadcast_to([P, 4, P]), ALU.mult).then_inc(q.x_ready, 1)
            dve.wait_ge(q.w_turned, it + 1)
            V.tensor_copy(wT[:, :], bank[4][:, 0:T]).then_inc(q.w_ready, 1)
            pick(dve, V, q, n)
            dve.wait_ge(q.silu_ready, it + 1)
            V.tensor_tensor(hT[:, :, :], sil[:, :, :], bank[2][:, 2 * P:4 * P].rearrange("p (j s) -> p j s", j=2),
                            ALU.mult).then_inc(q.h_ready, 1)
            dve.wait_ge(q.freed[RING - 1], q.free_base[RING - 1] + 1 + it)
            V.tensor_copy(ys[:, 1, :], bank[5][:, :]).then_inc(q.y1_ready, 1)
            for hf in range(2):
                for tt in range(TT):
                    dve.wait_ge(q.combined, it * 4 + (2 * hf + tt + 1))
                    if hf == 0 and tt == 0:
                        pass
                    dst = h[:, tt, hf * HALF:(hf + 1) * HALF]
                    V.tensor_tensor(dst, dst, bank[6 + tt][:, :], ALU.add).then_inc(q.added, 1)

        def pe_lot(pe, q, it, n):
            def mm(o, lhsT, rhs, start, stop, **kw):
                return nc.tensor.matmul(o, lhsT, rhs, start=start, stop=stop, **kw)

            pe.wait_ge(q.sel_built, n + 1)
            for hf in range(2):
                for k in range(4):
                    for tt in range(TT):
                        src = u[:, tt, :].rearrange("p (d k) -> p k d", k=KD)[:, 4 * hf + k, :]
                        ins = mm(bank[(3, 2)[hf]][:, k * P:(k + 1) * P], src, sel[:, tt, :], tt == 0, tt == TT - 1)
                ins.then_inc(q.gathered, 1)
            for tt in range(TT):
                for i in range(2):
                    ins = mm(bank[4][:, tt * P:(tt + 1) * P], wsel[:, 2 * tt + i, :], ident, i == 0, i == 1)
            ins.then_inc(q.w_turned, 1)

            def total(e):
                pe.wait_ge(q.part_ready, it * LOT + (e + 1))
                for j in range(4):
                    ins = mm(bank[2][:, j * P + e * SLOTS:j * P + (e + 1) * SLOTS],
                             part[:, e % 2, j * P:(j + 1) * P], c("stack"), True, True)
                ins.then_inc(q.summed, 1)

            pe.wait_ge(q.x_ready, it * 2 + 2)
            for e in range(LOT):
                pe.wait_ge(q.landed[e], q.land_base[e] + (it + 1) * 32)
                if e >= 2:
                    pe.wait_ge(q.part_ready, it * LOT + (e - 1))
                w = ring[:, e, :].rearrange("p (w k f) -> p k w f", w=2, k=KD)
                for k in range(KD):
                    cg = SLOTS * (k % 4)
                    ins = mm(bank[e % 2][cg:cg + SLOTS, :].rearrange("p (w f) -> p w f", w=2),
                             xg[:, k, e * SLOTS:(e + 1) * SLOTS], w[:, k], k < 4, k >= 4)
                ins.then_inc(q.freed[e], 1)
                if e:
                    total(e - 1)
            total(LOT - 1)
            pe.wait_ge(q.h_ready, it + 1)
            pe.wait_ge(q.w_ready, it + 1)
            for pair in range(2):
                s = LOT + pair
                pe.wait_ge(q.landed[s], q.land_base[s] + (it + 1) * 32)
            for hf in range(2):
                for j in range(2):
                    for e in range(LOT):
                        w = ring[:, LOT + e // 2, :].rearrange("p (e j n) -> p e j n", e=2, j=2)
                        ins = mm(bank[4 + hf][e * SLOTS:(e + 1) * SLOTS, :], hT[:, j, e * SLOTS:(e + 1) * SLOTS],
                                 w[:, e % 2, j, hf * HALF:(hf + 1) * HALF], j == 0, j == 1)
                        if hf == 1 and j == 1 and e in (1, 3):
                            ins.then_inc(q.freed[LOT + e // 2], 1)
                if hf == 0:
                    ins.then_inc(q.y_done, 1)
            for hf in range(2):
                pe.wait_ge((q.y0_ready, q.y1_ready)[hf], it + 1)
                for tt in range(TT):
                    if hf:
                        pe.wait_ge(q.added, it * 4 + (tt + 1))
                    mm(bank[6 + tt][:, :], wT[:, tt * P:(tt + 1) * P], ys[:, hf, :], True, True)\
                        .then_inc(q.combined, 1)

        block = ctx.enter_context(nc.Block())

        @block.sync
        def _(sp):
            def expert_loads(q, it, g):
                for e in range(LOT):
                    sp.wait_ge(q.freed[e], q.free_base[e] + it)
                    half = ring[:, e, :].rearrange("p (w n) -> p w n", w=2)
                    for w, src in enumerate((w_gate, w_up)):
                        one = src[q.l, bass.ds(g * LOT + e, 1)].rearrange("e (p k) f -> p (e k f)", k=KD)
                        sp.dma_start(half[:, w, :], one).then_inc(q.landed[e], 16)
                for pair in range(LOT // 2):
                    s = LOT + pair
                    sp.wait_ge(q.freed[s], q.free_base[s] + it)
                    half = ring[:, s, :].rearrange("p (e j n) -> p e j n", e=2, j=2)
                    for e in range(2):
                        one = w_down[q.l, bass.ds(g * LOT + 2 * pair + e, 1)]
                        sp.dma_start(half[:, e], one.rearrange("e (j p) d -> p (e j) d", p=P))\
                          .then_inc(q.landed[s], 16)

            def more_rounds(l):
                sp.wait_ge(sem(f"rounds_known{l}"), 1)
                r_end = sp.value_load(nrounds[0:1, 0:1], min_val=1, max_val=ROUNDS)
                with sp.If(r_end > 1):
                    for s in range(RING):
                        sp.wait_ge(main[l].freed[s], main[l].free_base[s] + LOTS * (l + 1))
                    with sp.Fori(1, r_end) as r:
                        with sp.Fori(0, LOTS) as g:
                            expert_loads(more[l], (r - 1) * LOTS + g, g)
                    sp.wait_ge(sem(f"moe_added{l}"), 1)
                with sp.Else():
                    sp.nop()

            for s in range(3):
                sp.dma_start(ring[:, s, :], stream[s]).then_inc(sem(f"slot{s}_landed"), 16)
                if s == 1:
                    sp.dma_start(ring[:, 5, 0:1024], kvb).then_inc(sem("slot5_landed"), 16)
            for s in (3, 4):
                sp.dma_start(ring[:, s, :], stream[s]).then_inc(sem(f"slot{s}_landed"), 16)
            with sp.Fori(0, LOTS) as g:
                expert_loads(main[0], g, g)
            more_rounds(0)
            for s in range(RING):
                sp.wait_ge(sem(f"slot{s}_freed"), moe0[s] + LOTS)
                sp.dma_start(ring[:, s, :], stream[5 + s]).then_inc(sem(f"slot{s}_landed"), 16)
            for s in range(2):
                sp.wait_ge(sem(f"slot{s}_freed"), moe0[s] + LOTS + 1)
                sp.dma_start(ring[:, s, :], stream[11 + s]).then_inc(sem(f"slot{s}_landed"), 16)
            with sp.Fori(0, LOTS) as g:
                expert_loads(main[1], LOTS + g, g)
            more_rounds(1)
            for tt in range(TT):
                sp.wait_ge(sem("final_ready"), tt + 1)
                sp.dma_start(out[0, tt * P:(tt + 1) * P, :], u[:, tt, :]).then_inc(sem("stored"), 16)
            sp.wait_ge(sem("stored"), 16 * TT)

        @block.gpsimd
        def _(pool):
            pool.wait_ge(sem("rows_step"), 1)
            B.taken(pool, "rows")
            for w in range(2):
                skewed = bias_rows[w].rearrange("h (q x) -> h q x", q=P)[:, :, 0:BLK]
                pool.dma_start(skewed, rows[:, w, :].unsqueeze(1).broadcast_to([HEADS, P, BLK]))\
                    .then_inc(sem("rows_stored"), 16)
            pool.wait_ge(sem("rows_stored"), 32)

            def spread(w):
                for seg, (a, n) in enumerate(((0, T), (T, P))):
                    src_ap = bass.AP(bias_rows.tensor, w * HEADS * P * (BLK + 1) + P - 1 + seg * P,
                                     [[BLK, P], [P * (BLK + 1), HEADS], [1, n]])
                    pool.dma_start(bias[:, :, a:a + n], src_ap).then_inc(sem("bias_ready"), 16)

            spread(0)
            pool.wait_ge(sem("kr_parts"), 1)
            B.taken(pool, ("low", 3))
            src = [krt[HD:P, i, :].unsqueeze(1).broadcast_to([HD, HEADS, T]) for i in range(2)]
            nc.gpsimd.tensor_tensor(kT[HD:P, :, :], src[0], src[1], ALU.add).then_inc(sem("kr_ready"), 1)
            pool.wait_ge(sem("moe_added0"), 1)
            spread(1)

        @block.scalar
        def _(act):
            step = Steps(sem("act_step"))
            act.dma_start(h[:, :, :], x[0].rearrange("(t p) d -> p t d", p=P)).then_inc(sem("x_loaded"), 16)
            act.dma_start(con[:, :], consts).then_inc(sem("con_loaded"), 16)
            act.dma_start(par[:, :], params).then_inc(sem("par_loaded"), 16)
            act.dma_start(rw[:, :, :, :], router_w).then_inc(sem("par_loaded"), 16)
            act.dma_start(tab[:, :], table).then_inc(sem("tab_loaded"), 16)
            act.dma_start(hot[:, :], onehot).then_inc(sem("tab_loaded"), 16)
            act.dma_start(msk[:, :, :], masks).then_inc(sem("tab_loaded"), 16)

            def norm_half(i):
                h_complete(act, i)
                act.wait_ge(sem("h_read"), i)
                nc.scalar.activation(junk[:, :], h[:, 0, :], ACT.Square,
                                     accum_out=st[:, 0:1]).then_inc(sem("ss_act"), 1)
                act.wait_ge(sem("ss_act"), i + 1)
                act.wait_ge(sem("ss_dve"), i + 1)
                act.wait_ge(sem("eps_ready"), 1)
                nc.scalar.activation(st[:, 2:4], st[:, 0:2], ACT.Sqrt, bias=st[:, 8:9],
                                     scale=1.0 / D).then_inc(sem("std_ready"), 1)

            def uT_banks(l, which):
                for b in (0, 2):
                    src = B.read(act, ("uT", l, which, b))
                    for j in range(2):
                        k = 2 * b + j
                        ins = nc.scalar.activation(uT[:, k, :], src[:, j * T:(j + 1) * T], ACT.Copy,
                                                   scale=pcol(f"g{which}{l}", k))
                    B.release(ins, ("uT", l, which, b))

            act.wait_ge(sem("con_loaded"), 16)
            act.wait_ge(sem("par_loaded"), 32)

            for l in range(DEPTH):
                norm_half(2 * l)
                uT_banks(l, "mix")
                if l == 0:
                    for i in range(2):
                        src = B.read(act, ("swq", i))
                        ins = nc.scalar.activation(swq[:, 2 * i:2 * i + 2, :],
                                                   src[:, :].rearrange("p (c t) -> p c t", c=2), ACT.Copy)
                        B.release(ins, ("swq", i))
                    src = B.read(act, "ssq")
                    nc.scalar.activation(lowr[:, 0, :], src[:, 0:T], ACT.Sqrt, bias=st[:, 8:9], scale=1.0 / MLA_QR)
                    ins = nc.scalar.activation(lowr[:, 1, :], src[:, T:2 * T], ACT.Sqrt, bias=st[:, 8:9],
                                               scale=1.0 / MLA_KVR)
                    B.release(ins, "ssq")
                    for i in range(4):
                        src = B.read(act, ("mk", i))
                        ins = nc.scalar.activation(kT[0:HD, 2 * i:2 * i + 2, :],
                                                   src[0:HD, :].rearrange("p (c t) -> p c t", c=2), ACT.Copy)
                        B.release(ins, ("mk", i))
                else:
                    in1_reads(act, nc.scalar, 1)

                for i in range(2 * HEADS + 2):
                    if i < 2 * HEADS:
                        j = i % 3
                        if l == 0 or i < HEADS:
                            act.wait_ge(sem(f"max_ready{l}"), i + 1)
                            if i >= 3:
                                B.read(act, ("t", l, i - 3))
                            nc.scalar.activation(pr[:, j, 0:T], sc[:, j, 0:T], ACT.Exp, bias=nm[:, j, 0:1],
                                                 accum_out=nm[:, j, 2:3])
                            ins = nc.scalar.activation(pr[:, j, T:BLK], sc[:, j, T:BLK], ACT.Exp,
                                                       bias=nm[:, j, 1:2], accum_out=nm[:, j, 3:4])
                            if l == 0 and i >= HEADS:
                                hh = swa_head(i)
                                ins = nc.scalar.activation(nm[:, j, 4:6], nm[:, j, 0:2], ACT.Exp,
                                                           bias=pcol("sinks", hh))
                            ins.then_inc(sem(f"exp_ready{l}"), 1)
                        else:
                            m = i - HEADS
                            B.taken(act, ("s", l, i))
                            B.read(act, ("t", l, i - 3))
                            step(act, nc.scalar.activation(pr[:, j, :], sc[:, j, :], ACT.Abs))
                            step(act, nc.scalar.activation(pr[:, j, :], pr[:, j, :], ACT.Exp, scale=-1.0))
                            nc.scalar.activation(pr[:, j, :], pr[:, j, :], ACT.Ln, bias=1.0)\
                              .then_inc(sem("ln_ready"), 1)
                    if l == 1 and HEADS <= i - 1 < 2 * HEADS:
                        n = i - 1
                        act.wait_ge(sem("tail_ready"), n - HEADS + 1)
                        nc.scalar.activation(pr[:, n % 3, :], sc[:, n % 3, :], ACT.Exp)\
                          .then_inc(sem("sb_ready"), 1)
                    if i >= 2:
                        n = i - 2
                        src = B.read(act, ("t", l, n))
                        if n >= 2:
                            pv_done(act, l, n - 2)
                        ins = nc.scalar.activation(pt[:, n % 2, :], src[:, 0:BLK], ACT.Copy)
                        B.release(ins, ("t", l, n))

                norm_half(2 * l + 1)
                uT_banks(l, "ffn")
                act.wait_ge(sem(f"glog_ready{l}"), 1)
                nc.scalar.activation(rt[:, 1, :, 0:GROUPS], rt[:, 1, :, 0:GROUPS], ACT.Exp)\
                  .then_inc(sem(f"gexp_ready{l}"), 1)
                act.wait_ge(sem(f"gap_ready{l}"), 1)
                nc.scalar.activation(st[:, 12:14], st[:, 10:12], ACT.Exp).then_inc(sem(f"gapexp_ready{l}"), 1)

                act.wait_ge(sem(f"rounds_known{l}"), 1)
                r_end = act.value_load(nrounds[0:1, 0:1], min_val=1, max_val=ROUNDS)
                with act.Fori(0, LOTS) as g:
                    act_lot(act, main[l], LOTS * l + g)
                with act.If(r_end > 1):
                    with act.Fori(1, r_end) as r:
                        with act.Fori(0, LOTS) as g:
                            act_lot(act, more[l], (r - 1) * LOTS + g)
                with act.Else():
                    act.nop()
            norm_half(2 * DEPTH)

        @block.vector
        def _(dve):
            step = Steps(sem("dve_step"))
            V = nc.vector
            step(dve, V.memset(st[:, 8:9], EPS))
            V.memset(st[:, 9:10], 0.0).then_inc(sem("eps_ready"), 1)
            dve.wait_ge(sem("con_loaded"), 16)
            dve.wait_ge(sem("par_loaded"), 32)
            dve.wait_ge(sem("tab_loaded"), 48)
            step(dve, V.tensor_scalar(nsink[:, :], pcol("sinks"), -1.0, None, ALU.mult))
            src = B.read(dve, "rows")
            for w in range(2):
                ins = V.tensor_tensor(rows[:, w, :], src[0:HEADS, 0:BLK], msk[:, w, :], ALU.add)
                if w == 0:
                    ins.then_inc(sem("rows_step"), 1)
            B.release(ins, "rows")

            def norm(i):
                h_complete(dve, i)
                V.tensor_tensor_reduce(u[:, 1, :], h[:, 1, :], h[:, 1, :], 1.0, 0.0, ALU.mult, ALU.add,
                                       st[:, 1:2]).then_inc(sem("ss_dve"), 1)
                dve.wait_ge(sem("std_ready"), i + 1)
                step(dve, V.reciprocal(st[:, 4:6], st[:, 2:4]))
                dve.wait_ge(sem("ss_dve"), i + 1)
                for tt in range(TT):
                    V.tensor_scalar(u[:, tt, :], h[:, tt, :], st[:, 4 + tt:5 + tt], None, ALU.mult)\
                     .then_inc(sem("u_ready"), 1)

            def norm_turn(i, l, which):
                norm(i)
                for b in (1, 3):
                    src = B.read(dve, ("uT", l, which, b))
                    for j in range(2):
                        k = 2 * b + j
                        ins = V.tensor_scalar(uT[:, k, :], src[:, j * T:(j + 1) * T], pcol(f"g{which}{l}", k),
                                              None, ALU.mult)
                    B.release(ins, ("uT", l, which, b))
                dve.wait_ge(sem("u_ready"), 2 * (i + 1))
                dve.sem_inc(sem("h_read"), 1)

            for l in range(DEPTH):
                norm_turn(2 * l, l, "mix")
                if l == 0:
                    for i in range(3):
                        src = B.read(dve, ("low", i))
                        ins = V.tensor_copy(low[:, i, :], src[:, 0:T])
                        B.release(ins, ("low", i))
                        B.taken(dve, ("low", i))
                        V.tensor_tensor(lowsq[:, i, :], low[:, i, :], low[:, i, :], ALU.mult)\
                         .then_inc(sem("lowsq_ready"), 1)
                    src = B.read(dve, ("low", 3))
                    V.tensor_tensor(krt[HD:P, 0, :], src[HD:P, 0:T], c("kcos", slice(HD, P)), ALU.mult)\
                     .then_inc(sem("kr_parts"), 1)
                    ins = V.tensor_tensor(krt[HD:P, 1, :], src[HD:P, T:2 * T], c("ksin", slice(HD, P)), ALU.mult)
                    B.release(ins, ("low", 3))
                    src = B.read(dve, "swk")
                    ins = V.tensor_copy(swk[:, :], src[:, 0:T])
                    B.release(ins, "swk")
                    src = B.read(dve, "swv")
                    ins = V.tensor_copy(v2[:, :, 0:P], src[:, 0:2 * P].rearrange("p (t n) -> p t n", t=TT))
                    B.release(ins, "swv")
                    B.taken(dve, "ssq")
                    step(dve, V.reciprocal(lowr[:, :, :], lowr[:, :, :]))
                    for i in range(3):
                        g = pcol("gkv", 0) if i == 2 else pcol("gq", i)
                        V.scalar_tensor_tensor(out=low[:, i, :], in0=low[:, i, :], scalar=g,
                                               in1=lowr[:, i // 2, :], op0=ALU.mult, op1=ALU.mult)\
                         .then_inc(sem("lown_ready"), 1)
                    for i in range(4):
                        src = B.read(dve, ("mq", i))
                        ins = V.tensor_tensor(qT[:, 2 * i:2 * i + 2, :], src[:, :].rearrange("p (c t) -> p c t", c=2),
                                              c("qrope").unsqueeze(1).broadcast_to([P, 2, T]), ALU.mult)
                        B.release(ins, ("mq", i))
                    for i in range(TT):
                        src = B.read(dve, ("mv", i))
                        ins = V.tensor_copy(v1[:, i, :], src[:, :])
                        B.release(ins, ("mv", i))
                else:
                    in1_reads(dve, V, 0)

                for i in range(2 * HEADS + 6):
                    if i < 2 * HEADS:
                        j = i % 3
                        src = B.read(dve, ("s", l, i))
                        if i >= 3 and (l == 0 or i - 3 < HEADS):
                            dve.wait_ge(sem(f"exp_ready{l}"), i - 2)
                        elif i >= 3:
                            dve.wait_ge(sem("sb_ready"), i - 2 - HEADS)
                        if l == 0 and i < HEADS:
                            scale, add = MLA_SCALE, c("causal")
                        elif l == 0:
                            scale, add = HEAD_SCALE, bias[:, swa_head(i), :]
                            dve.wait_ge(sem("bias_ready"), 32)
                        elif i < HEADS:
                            scale, add = HEAD_SCALE, bias[:, i, :]
                            dve.wait_ge(sem("bias_ready"), 64)
                        else:
                            scale, add = HEAD_SCALE, c("strict")
                        ins = V.scalar_tensor_tensor(out=sc[:, j, :], in0=src[:, 0:BLK], scalar=scale, in1=add,
                                                     op0=ALU.mult, op1=ALU.add)
                        B.release(ins, ("s", l, i))
                        if l == 0 or i < HEADS:
                            B.taken(dve, ("s", l, i))
                            V.tensor_reduce(nm[:, j, 0:1], sc[:, j, 0:T], AX.X, ALU.max, negate=True)
                            ins = V.tensor_reduce(nm[:, j, 1:2], sc[:, j, T:BLK], AX.X, ALU.max, negate=True)
                            if l == 0 and i >= HEADS:
                                step(dve, ins)
                                hh = swa_head(i)
                                ins = V.tensor_scalar(nm[:, j, 0:2], nm[:, j, 0:2], nsink[:, hh:hh + 1], None, ALU.min)
                            ins.then_inc(sem(f"max_ready{l}"), 1)
                    n = i - 1
                    if 0 <= n < 2 * HEADS:
                        j = n % 3
                        if l == 1 and n >= HEADS:
                            m = n - HEADS
                            dve.wait_ge(sem("ln_ready"), m + 1)
                            step(dve, V.scalar_tensor_tensor(out=cs[:, 0, :], in0=sc[:, j, :], scalar=0.0,
                                                             in1=pr[:, j, :], op0=ALU.max, op1=ALU.add))
                            step(dve, V.tensor_tensor_scan(cs[:, 1, ::-1], c("carry")[:, ::-1], cs[:, 0, ::-1], 0.0,
                                                           ALU.mult, ALU.add))
                            V.tensor_tensor(sc[:, j, :], sc[:, j, :], cs[:, 1, :], ALU.subtract)\
                             .then_inc(sem("tail_ready"), 1)
                        else:
                            dve.wait_ge(sem(f"exp_ready{l}"), n + 1)
                            if l == 0 and n >= HEADS:
                                step(dve, V.tensor_tensor(nm[:, j, 2:4], nm[:, j, 2:4], nm[:, j, 4:6], ALU.add))
                            step(dve, V.reciprocal(nm[:, j, 6:8], nm[:, j, 2:4]))
                            V.tensor_scalar(pr[:, j, 0:T], pr[:, j, 0:T], nm[:, j, 6:7], None, ALU.mult)\
                             .then_inc(sem(f"p_ready{l}"), 1)
                            V.tensor_scalar(pr[:, j, T:BLK], pr[:, j, T:BLK], nm[:, j, 7:8], None, ALU.mult)\
                             .then_inc(sem(f"p_ready{l}"), 1)
                    n = i - 4
                    if n >= 1 and n % 2 == 1 and n < 2 * HEADS:
                        src = B.read(dve, ("o", l, n // 2))
                        ins = V.tensor_copy(oT[:, n // 2, :], src[:, 0:T])
                        B.release(ins, ("o", l, n // 2))

                for i in range(4):
                    src = B.read(dve, ("out", l, i))
                    tt, hf = i // 2, i % 2
                    dst = h[:, tt, hf * HALF:(hf + 1) * HALF]
                    ins = V.tensor_tensor(dst, dst, src[:, :], ALU.add)
                    B.release(ins, ("out", l, i))

                norm_turn(2 * l + 1, l, "ffn")
                route(dve, V, l, step)
                place(dve, V, step)
                pick_first(dve, V, main[l], BUILDS * l)
                with dve.Fori(0, LOTS) as g:
                    dve_lot(dve, V, main[l], LOTS * l + g, BUILDS * l + g + 1)
                dve.wait_ge(sem(f"rounds_known{l}"), 1)
                r_end = dve.value_load(nrounds[0:1, 0:1], min_val=1, max_val=ROUNDS)
                with dve.If(r_end > 1):
                    with dve.Fori(1, r_end) as r:
                        next_round(dve, V, l, r)
                        pick_first(dve, V, more[l], (r - 1) * BUILDS)
                        with dve.Fori(0, LOTS) as g:
                            dve_lot(dve, V, more[l], (r - 1) * LOTS + g, (r - 1) * BUILDS + g + 1)
                        dve.wait_ge(more[l].added, r * (LOTS * 4))
                    V.memset(st[:, 9:10], 0.0).then_inc(sem(f"moe_added{l}"), 1)
                with dve.Else():
                    dve.wait_ge(main[l].added, LOTS * (l + 1) * 4)
                    V.memset(st[:, 9:10], 0.0).then_inc(sem(f"moe_added{l}"), 1)

            norm(2 * DEPTH)
            dve.wait_ge(sem("u_ready"), 2 * (2 * DEPTH + 1))
            for tt in range(TT):
                V.tensor_tensor(u[:, tt, :], u[:, tt, :], pcol("gfinal"), ALU.mult).then_inc(sem("final_ready"), 1)


        @block.tensor
        def _(pe):
            spent = []

            def carry(ins):
                if spent:
                    ins.then_inc(sem(f"slot{spent.pop()}_freed"), 1)
                return ins

            def mm(o, lhsT, rhs, start, stop, **kw):
                return carry(nc.tensor.matmul(o, lhsT, rhs, start=start, stop=stop, **kw))

            pe.wait_ge(sem("tab_loaded"), 48)
            o = B.begin(pe, "rows")
            B.written(mm(o[0:HEADS, 0:BLK], tab[:, :], hot[:, :], True, True), "rows")
            pe.wait_ge(sem("con_loaded"), 16)

            def turn_u(i, l, which):
                pe.wait_ge(sem("u_ready"), 2 * i + 2)
                for b in range(4):
                    o = B.begin(pe, ("uT", l, which, b))
                    for j in range(2):
                        for tt in range(TT):
                            src = u[:, tt, :].rearrange("p (d k) -> p k d", k=KD)[:, 2 * b + j, :]
                            ins = carry(nc.tensor.transpose(o[:, j * T + tt * P:j * T + (tt + 1) * P], src, ident))
                    B.written(ins, ("uT", l, which, b))
                for b in range(4):
                    B.taken(pe, ("uT", l, which, b))

            def featured(o, w, cols, M, p0=0):
                for k in range(KD):
                    ins = mm(o[p0:p0 + M, :], w[:, k, cols:cols + M], uT[:, k, :], k == 0, k == KD - 1)
                return ins

            def tokened(o, w, tt, cols, n):
                for k in range(KD):
                    ins = mm(o, uT[:, k, tt * P:(tt + 1) * P], w[:, k, cols:cols + n], k == 0, k == KD - 1)
                return ins

            def slot_freed(s):
                spent.append(s)

            for l in range(DEPTH):
                turn_u(2 * l, l, "mix")
                if l == 0:
                    arrived(pe, ("in", 0), 0)
                    w = win(0)
                    for i in range(3):
                        o = B.begin(pe, ("low", i))
                        B.written(featured(o[:, 0:T], w, i * P, P), ("low", i))
                    o = B.begin(pe, ("low", 3))
                    featured(o[:, 0:T], w, 3 * P, HD, HD)
                    ins = featured(o[:, T:2 * T], w, 3 * P + HD, HD, HD)
                    B.written(ins, ("low", 3))
                    slot_freed(0)
                    arrived(pe, ("in", 0), 1)
                    w = win(1)
                    for i in range(2):
                        o = B.begin(pe, ("swq", i))
                        for j in range(2):
                            ins = featured(o[:, j * T:(j + 1) * T], w, (2 * i + j) * P, P)
                        B.written(ins, ("swq", i))
                    slot_freed(1)
                    arrived(pe, ("in", 0), 2)
                    w = ring[:, 2, 0:KD * T].rearrange("p (k n) -> p k n", k=KD)
                    o = B.begin(pe, "swk")
                    B.written(featured(o[:, 0:T], w, 0, P), "swk")
                    pe.wait_ge(sem("lowsq_ready"), 3)
                    o = B.begin(pe, "ssq")
                    mm(o[:, 0:T], ones, lowsq[:, 0, :], True, False)
                    mm(o[:, 0:T], ones, lowsq[:, 1, :], False, True)
                    B.written(mm(o[:, T:2 * T], ones, lowsq[:, 2, :], True, True), "ssq")
                    o = B.begin(pe, "swv")
                    for tt in range(TT):
                        ins = tokened(o[:, tt * P:(tt + 1) * P], w, tt, P, P)
                    B.written(ins, "swv")
                    wq = ring[:, 2, KD * T:].rearrange("p (k n) -> p k n", k=2)
                    pe.wait_ge(sem("lown_ready"), 2)
                    for i in range(4):
                        o = B.begin(pe, ("mq", i))
                        for j in range(2):
                            hh = 2 * i + j
                            for k in range(2):
                                ins = mm(o[:, j * T:(j + 1) * T], wq[:, k, hh * P:(hh + 1) * P], low[:, k, :],
                                         k == 0, k == 1)
                        B.written(ins, ("mq", i))
                    slot_freed(2)
                    arrived(pe, ("in", 0), 5)
                    pe.wait_ge(sem("lown_ready"), 3)
                    for i in range(4):
                        o = B.begin(pe, ("mk", i))
                        for j in range(2):
                            hh = 2 * i + j
                            ins = mm(o[0:HD, j * T:(j + 1) * T], ring[:, 5, hh * HD:(hh + 1) * HD], low[:, 2, :],
                                     True, True)
                        B.written(ins, ("mk", i))
                    for tt in range(TT):
                        o = B.begin(pe, ("mv", tt))
                        ins = mm(o[:, :], low[:, 2, tt * P:(tt + 1) * P], ring[:, 5, 512:1024], True, True)
                        B.written(ins, ("mv", tt))
                    slot_freed(5)
                    pe.wait_ge(sem("kr_ready"), 1)
                    for key in ([(name, i) for name in ("mk", "mq") for i in range(4)]
                                + [("swq", 0), ("swq", 1), ("mv", 0), ("mv", 1), "swk", "swv"]):
                        B.taken(pe, key)
                else:
                    n = 0
                    for s in range(RING):
                        arrived(pe, ("in", 1), s)
                        w = win(s)
                        for i in range(2):
                            o = B.begin(pe, ("in1", n))
                            if s % 3 == 2:
                                ins = tokened(o[:, :], w, i, 0, 512)
                            else:
                                for j in range(2):
                                    ins = featured(o[:, j * T:(j + 1) * T], w, (2 * i + j) * P, P)
                            B.written(ins, ("in1", n))
                            n += 1
                        slot_freed(s)
                    for i in range(12):
                        B.taken(pe, ("in1", i))

                def operands(n):
                    if l == 0 and n < HEADS:
                        return qT[:, n, :], kT[:, n, :]
                    p0 = HD * (n % 2)
                    if l == 0:
                        return swq[p0:p0 + HD, (n - HEADS) // 2, :], swk[p0:p0 + HD, :]
                    return qT[p0:p0 + HD, n // 2, :], kT[p0:p0 + HD, n // 2, :]

                def values(n, tt):
                    if l == 0 and n >= HEADS:
                        return v2[:, tt, HD * (n % 2):HD * (n % 2) + HD]
                    return (v1 if n < HEADS else v2)[:, tt, (n % HEADS) * HD:(n % HEADS + 1) * HD]

                for i in range(2 * HEADS + 3):
                    if i < 2 * HEADS:
                        q_, k_ = operands(i)
                        o = B.begin(pe, ("s", l, i))
                        mm(o[:, 0:T], q_[:, P:T], k_, True, True)
                        B.written(mm(o[:, T:BLK], q_[:, 0:P], k_[:, 0:P], True, True), ("s", l, i))
                    n = i - 2
                    if 0 <= n < 2 * HEADS:
                        j = n % 3
                        if l == 0 or n < HEADS:
                            pe.wait_ge(sem(f"p_ready{l}"), 2 * n + 2)
                        else:
                            pe.wait_ge(sem("sb_ready"), n - HEADS + 1)
                        o = B.begin(pe, ("t", l, n))
                        nc.tensor.transpose(o[:, 0:P], pr[:, j, T:BLK], ident)
                        nc.tensor.transpose(o[:, P:2 * P], pr[:, j, 0:P], ident)
                        ins = nc.tensor.transpose(o[:, 2 * P:3 * P], pr[:, j, P:2 * P], ident)
                        B.written(ins, ("t", l, n))
                    n = i - 3
                    if n >= 0:
                        B.taken(pe, ("t", l, n))
                        p0 = HD * (n % 2)
                        o = B.begin(pe, ("o", l, n // 2)) if n % 2 == 0 else bank[B.at[("o", l, n // 2)][0]]
                        mm(o[p0:p0 + HD, 0:T], values(n, 0), pt[:, n % 2, 0:T], True, True)
                        ins = mm(o[p0:p0 + HD, P:T], values(n, 1), pt[:, n % 2, T:BLK], False, True,
                                 skip_group_check=True)
                        if n % 2 == 0:
                            ins.then_inc(sem(f"pv_even{l}"), 1)
                        else:
                            B.written(ins, ("o", l, n // 2))

                for n in range(HEADS):
                    B.taken(pe, ("o", l, n))
                for i in range(4):
                    tt, hf = i // 2, i % 2
                    s = (3, 0)[l] + hf
                    if tt == 0:
                        arrived(pe, ("in", 0) if l == 0 else ("out", 1), s)
                    o = B.begin(pe, ("out", l, i))
                    for k in range(KD):
                        ins = mm(o[:, :], oT[:, k, tt * P:(tt + 1) * P], win(s)[:, k, :], k == 0, k == KD - 1)
                    B.written(ins, ("out", l, i))
                    if tt == 1:
                        slot_freed(s)

                turn_u(2 * l + 1, l, "ffn")
                o = B.begin(pe, ("route", l))
                NR = GROUPS + EXPERTS
                for tt in range(TT):
                    for k in range(KD):
                        ins = mm(o[:, tt * NR:(tt + 1) * NR], uT[:, k, tt * P:(tt + 1) * P], rw[:, l, k, :],
                                 k == 0, k == KD - 1)
                B.written(ins, ("route", l))
                pe.wait_ge(sem("members"), l + 1)
                o = B.begin(pe, ("rank", l))
                mm(o[:, 0:EXPERTS], c("earlier"), mem[:, 0, :], True, True)
                mm(o[:, EXPERTS:2 * EXPERTS], ones, mem[:, 0, :], True, False)
                mm(o[:, EXPERTS:2 * EXPERTS], c("earlier"), mem[:, 1, :], False, True)
                mm(o[:, 2 * EXPERTS:3 * EXPERTS], ones, mem[:, 0, :], True, False)
                ins = mm(o[:, 2 * EXPERTS:3 * EXPERTS], ones, mem[:, 1, :], False, True)
                B.written(ins, ("rank", l))
                for b in range(8):
                    pe.wait_ge(B.free[b], upto[l][b])

                with pe.Fori(0, LOTS) as g:
                    pe_lot(pe, main[l], LOTS * l + g, BUILDS * l + g)
                pe.wait_ge(sem(f"rounds_known{l}"), 1)
                r_end = pe.value_load(nrounds[0:1, 0:1], min_val=1, max_val=ROUNDS)
                with pe.If(r_end > 1):
                    for s in range(RING):
                        pe.sem_inc(more[l].freed[s], 1)
                    pe.wait_ge(main[l].added, LOTS * (l + 1) * 4)
                    with pe.Fori(1, r_end) as r:
                        with pe.Fori(0, LOTS) as g:
                            pe_lot(pe, more[l], (r - 1) * LOTS + g, (r - 1) * BUILDS + g)
                with pe.Else():
                    pe.nop()
                pe.wait_ge(sem(f"moe_added{l}"), 1)

def _stream(inp):
    def cols(w, parts):
        return np.ascontiguousarray(np.concatenate([w[:, a:b] for a, b in parts], 1)).reshape(P, -1)

    w0 = inp["w_in_even"][0]
    kr = MLA_QR + MLA_KVR
    half = ROPE // 2
    a, b = (kr, kr + half), (kr + half, kr + ROPE)
    qs = kr + ROPE
    slots = [cols(w0, [(0, kr), a, b, b, a, b, a, a, b])]
    heads = [(qs + HD * n, qs + HD * (n + 1)) for i in range(4) for n in (i, 4 + i)]
    slots.append(cols(w0, heads))
    ks = qs + HEADS * HD
    wq = inp["w_mla_qb"][0].reshape(2, P, HEADS, HD + ROPE)
    wq = np.concatenate([wq, wq[..., HD:]], -1).transpose(1, 0, 2, 3).reshape(P, -1)
    slots.append(np.concatenate([cols(w0, [(ks, ks + 256)]), wq], 1))
    wo = inp["w_out_even"][0].reshape(16, HD, D)
    order = list(range(8)) + [n for i in range(4) for n in (8 + i, 12 + i)]
    wo = wo[order].reshape(KD, P, D).transpose(1, 0, 2)
    slots += [wo[:, :, i * HALF:(i + 1) * HALF].reshape(P, -1) for i in range(2)]
    w1 = inp["w_in_odd"][0]
    slots += [cols(w1, [(512 * i, 512 * i + 512)]) for i in range(6)]
    wo = inp["w_out_odd"][0].reshape(KD, P, D).transpose(1, 0, 2)
    slots += [wo[:, :, i * HALF:(i + 1) * HALF].reshape(P, -1) for i in range(2)]
    return np.ascontiguousarray(np.stack(slots))


def kernel(**inputs):
    import concourse.bacc as bacc
    from concourse.bass_utils import run_bass_kernel_spmd

    inp = {k: np.asarray(v) for k, v in inputs.items()}
    consts, at = shape_constants()
    onehot, masks = distance_constants()
    kv = inp["w_mla_kvb"][0].reshape(P, HEADS, 2 * HD)
    par = np.empty((P, PAR_COLS), np.float32)

    def put(name, v):
        par[:, PAR[name][0]:PAR[name][1]] = v

    for l in range(DEPTH):
        put(f"gmix{l}", inp["norm_mix"][l].reshape(P, KD))
        put(f"gffn{l}", inp["norm_ffn"][l].reshape(P, KD))
        put(f"rbias{l}", np.concatenate([inp["moe_b_group"][l], inp["moe_b_router"][l]])[None])
    put("gq", inp["g_mla_q"][0].reshape(2, P).T)
    put("gkv", inp["g_mla_kv"][0].reshape(1, P).T)
    put("sinks", inp["swa_sinks"][0][None])
    put("gfinal", inp["norm_final"][None])
    rw = np.concatenate([inp["moe_w_group"], inp["moe_w_router"]], -1).reshape(DEPTH, P, KD, GROUPS + EXPERTS)
    arrays = {
        "in_x": inp["x"], "in_stream": _stream(inp),
        "in_kvb": np.ascontiguousarray(np.concatenate([kv[:, :, :HD].reshape(P, -1), kv[:, :, HD:].reshape(P, -1)], 1)),
        "in_router": np.ascontiguousarray(rw.transpose(1, 0, 2, 3)), "in_params": par,
        "in_table": inp["rel_bias_table"], "in_consts": consts, "in_onehot": onehot, "in_masks": masks,
        "in_gate": inp["moe_w_gate"], "in_up": inp["moe_w_up"], "in_down": inp["moe_w_down"],
    }
    arrays = {k: np.ascontiguousarray(v) for k, v in arrays.items()}
    nc = bacc.Bacc("TRN2", target_bir_lowering=False, num_devices=1)
    args = [nc.dram_tensor(k, v.shape, mybir.dt.from_np(v.dtype), kind="ExternalInput").ap() for k, v in arrays.items()]
    out = nc.dram_tensor("out", (1, T, D), F32, kind="ExternalOutput").ap()
    trunk(nc, *args, out, at)
    r = run_bass_kernel_spmd(nc, [arrays], core_ids=[0])
    return r.results[0]["out"]
```

```python
from contextlib import ExitStack

import numpy as np

import concourse.bass as bass
from concourse import mybir

F32 = mybir.dt.float32
I32 = mybir.dt.int32
ALU = mybir.AluOpType
ACT = mybir.ActivationFunctionType
AX = mybir.AxisListType

P = 128
T = 256
TT = T // P
D = 1024
KD = D // P
HALF = D // 2
HEADS = 8
HD = 64
DEPTH = 2
EPS = 1e-6
NEG = -1e30
MLA_QR, MLA_KVR, ROPE = 256, 128, 32
MLA_SCALE = float(HD + ROPE) ** -0.5
HEAD_SCALE = float(HD) ** -0.5
WINDOW = 128
BUCKETS, MAX_DIST = 32, 2048
GROUPS, PER_GROUP = 4, 8
EXPERTS = GROUPS * PER_GROUP
NR = GROUPS + EXPERTS
FE = 256
SLOTS = 32
LOT = P // SLOTS
LOTS = EXPERTS // LOT
ROUNDS = T // SLOTS
BUILDS = LOTS + 1
RING = 6
SLOT_COLS = KD * HALF
BLK = T + P


def shape_constants():
    p = np.arange(P)[:, None]
    q = np.arange(P)
    t = np.arange(T)
    parts = {}
    parts["ident"] = (p == q[None]).astype(np.float32)
    parts["earlier"] = (p < q[None]).astype(np.float32)
    parts["ones"] = np.ones((P, P), np.float32)
    parts["stack"] = (p % SLOTS == np.arange(SLOTS)[None]).astype(np.float32)
    parts["iota"] = np.broadcast_to(q.astype(np.float32), (P, P))
    parts["first4"] = np.broadcast_to(np.arange(GROUPS, 0, -1, dtype=np.float32), (P, GROUPS))
    parts["first32"] = np.broadcast_to(np.arange(EXPERTS, 0, -1, dtype=np.float32), (P, EXPERTS))
    parts["slot0"] = np.broadcast_to(SLOTS * np.arange(EXPERTS, dtype=np.float32), (P, EXPERTS))
    parts["limits"] = np.broadcast_to(SLOTS * np.arange(1, ROUNDS, dtype=np.float32), (P, ROUNDS - 1))
    freqs = (np.float32(10000.0) ** (-np.arange(0, ROPE, 2, dtype=np.float32) / np.float32(ROPE))).astype(np.float32)
    ang = np.arange(T, dtype=np.float32)[None, :] * freqs[:, None]
    cos, sin = np.cos(ang).astype(np.float32), np.sin(ang).astype(np.float32)
    one = np.ones((HD, T), np.float32)
    parts["qrope"] = np.concatenate([one, cos, cos, sin, -sin])
    parts["kcos"] = np.concatenate([one, cos, cos, cos, cos])
    parts["ksin"] = np.concatenate([one, -sin, sin, sin, -sin])
    k2, k1 = t[None, :], q[None, :]
    parts["causal"] = np.concatenate([np.where(k2 <= p + P, 0.0, NEG), np.where(k1 <= p, 0.0, NEG)], 1)
    parts["strict"] = np.concatenate([np.where(k2 < p + P, 0.0, NEG), np.where(k1 < p, 0.0, NEG)], 1)
    restart = np.zeros((P, BLK))
    restart[:, [T - 1, BLK - 1]] = 1.0
    parts["restart"] = restart
    at, n = {}, 0
    for name, a in parts.items():
        at[name] = (n, n + a.shape[1])
        n += a.shape[1]
    return np.ascontiguousarray(np.concatenate([np.asarray(a, np.float32) for a in parts.values()], 1)), at


def distance_constants():
    dist = T - 1 - np.arange(BLK)
    n = np.maximum(dist, 0)
    exact = BUCKETS // 2
    nf = np.maximum(n, 1).astype(np.float32)
    large = exact + (np.log(nf / np.float32(exact)) / np.float32(np.log(MAX_DIST / exact))
                     * np.float32(BUCKETS - exact)).astype(np.int32)
    bucket = np.where(n < exact, n, np.minimum(large, BUCKETS - 1))
    onehot = (np.arange(BUCKETS)[:, None] == bucket[None]).astype(np.float32)
    window = np.where((dist >= 0) & (dist < WINDOW), 0.0, NEG)
    causal = np.where(dist >= 0, 0.0, NEG)
    masks = np.broadcast_to(np.stack([window, causal]), (HEADS, 2, BLK)).astype(np.float32)
    return np.ascontiguousarray(onehot), np.ascontiguousarray(masks)


PAR = {}
_n = 0
for _name, _w in (("gmix0", KD), ("gmix1", KD), ("gffn0", KD), ("gffn1", KD), ("gq", 2), ("gkv", 1),
                  ("sinks", HEADS), ("rbias0", GROUPS + EXPERTS), ("rbias1", GROUPS + EXPERTS), ("gfinal", D)):
    PAR[_name] = (_n, _n + _w)
    _n += _w
PAR_COLS = _n


class Banks:

    def __init__(self, nc, ctx):
        self.t = [ctx.enter_context(nc.psum_tensor(f"bank{i}", [P, 512], F32)) for i in range(8)]
        self.full = [ctx.enter_context(nc.semaphore(f"bank{i}_full")) for i in range(8)]
        self.free = [ctx.enter_context(nc.semaphore(f"bank{i}_free")) for i in range(8)]
        self.uses = [0] * 8
        self.at = {}

    def plan(self, key, bank):
        self.at[key] = (bank, self.uses[bank])
        self.uses[bank] += 1

    def begin(self, pe, key):
        b, n = self.at[key]
        if n:
            pe.wait_ge(self.free[b], n)
        return self.t[b]

    def written(self, ins, key):
        ins.then_inc(self.full[self.at[key][0]], 1)

    def read(self, eng, key):
        b, n = self.at[key]
        eng.wait_ge(self.full[b], n + 1)
        return self.t[b]

    def taken(self, eng, key):
        b, n = self.at[key]
        eng.wait_ge(self.free[b], n + 1)

    def release(self, ins, key):
        ins.then_inc(self.free[self.at[key][0]], 1)


class Steps:

    def __init__(self, sem):
        self.sem, self.n = sem, 0

    def __call__(self, eng, ins):
        self.n += 1
        ins.then_inc(self.sem, 1)
        eng.wait_ge(self.sem, self.n)


def trunk(nc, x, stream, kvb, router_w, params, table, consts, onehot, masks, w_gate, w_up, w_down, out, at):
    ctx = ExitStack()
    with ctx:
        def sb(name, shape, dt=F32):
            return ctx.enter_context(nc.sbuf_tensor(name, shape, dt))

        sems = {}

        def sem(name):
            if name not in sems:
                sems[name] = ctx.enter_context(nc.semaphore(name))
            return sems[name]

        B = Banks(nc, ctx)
        bank = B.t
        bias_rows = nc.dram_tensor("bias_rows", [2, HEADS, P * (BLK + 1)], F32, kind="Internal").ap()

        ring = sb("ring", [P, RING, SLOT_COLS])
        con = sb("con", [P, consts.shape[1]])
        par = sb("par", [P, PAR_COLS])
        rw = sb("rw", [P, DEPTH, KD, GROUPS + EXPERTS])
        tab = sb("tab", [BUCKETS, HEADS])
        hot = sb("hot", [BUCKETS, BLK])
        msk = sb("msk", [HEADS, 2, BLK])
        rows = sb("rows", [HEADS, 2, BLK])
        h = sb("h", [P, TT, D])
        u = sb("u", [P, TT, D])
        uT = sb("uT", [P, KD, T])
        qT = sb("qT", [P, HEADS, T])
        kT = sb("kT", [P, HEADS, T])
        swq = sb("swq", [P, 4, T])
        swk = sb("swk", [P, T])
        v1 = sb("v1", [P, TT, 512])
        v2 = sb("v2", [P, TT, 512])
        bias = sb("bias", [P, HEADS, BLK])
        sc = sb("sc", [P, 3, BLK])
        pr = sb("pr", [P, 3, BLK])
        cs = sb("cs", [P, 2, BLK])
        pt = sb("pt", [P, 2, BLK])
        nm = sb("nm", [P, 3, 8])
        nsink = sb("nsink", [P, HEADS])
        st = sb("st", [P, 16])
        lg = sb("lg", [P, TT, GROUPS + EXPERTS])
        mem = sb("mem", [P, TT, EXPERTS])
        nrounds = sb("nrounds", [P, 1], I32)
        rank = sb("rank", [P, TT, 2])
        base = sb("base", [P, TT, 2])
        gate = sb("gate", [P, TT, 2])
        cur = sb("cur", [P, TT, 2])
        sil = sb("sil", [P, 2, P])
        hT = sb("hT", [P, 2, P])

        def view(tile, a, shape):
            flat = tile[:, :, :].rearrange("p a b -> p (a b)")[:, a:a + int(np.prod(shape))]
            names = " ".join("abc"[:len(shape)])
            sizes = dict(zip("abc"[1:], shape[1:]))
            return flat.rearrange(f"p ({names}) -> p {names}", **sizes) if len(shape) > 1 else flat

        junk = view(kT, 0, [D])
        oT = view(u, 0, [KD, T])
        low, lowsq = sc[:, :, 0:T], pr[:, :, 0:T]
        lowr, krt = cs[:, :, 0:T], pt[:, :, 0:T]
        rt = view(v1, 0, [16, TT, EXPERTS])
        sel = view(v2, 0, [TT, P])
        wsel = view(v2, TT * P, [TT * 2, P])
        wT = view(v2, 3 * TT * P, [T])
        xg = view(bias, 0, [KD, P])
        part = view(bias, D, [2, 512])
        ys = view(bias, 2 * D, [2, HALF])
        after = view(cs, 0, [BLK + 1])

        def c(name, rows_=slice(0, P)):
            return con[rows_, at[name][0]:at[name][1]]

        def pcol(name, k=None):
            a, b = PAR[name]
            return par[:, a:b] if k is None else par[:, a + k:a + k + 1]

        ident, ones = c("ident"), c("ones")

        def win(s):
            return ring[:, s, :].rearrange("p (k n) -> p k n", k=KD)

        B.plan("rows", 7)
        upto = []
        for l in range(DEPTH):
            for b in range(4):
                B.plan(("uT", l, "mix", b), b)
            if l == 0:
                for i, b in enumerate((4, 5, 6, 7)):
                    B.plan(("low", i), b)
                for i in range(2):
                    B.plan(("swq", i), i)
                B.plan("swk", 2)
                B.plan("ssq", 4)
                B.plan("swv", 3)
                for i in range(4):
                    B.plan(("mq", i), (0, 1, 5, 6)[i])
                for i in range(4):
                    B.plan(("mk", i), (7, 2, 3, 4)[i])
                for i in range(TT):
                    B.plan(("mv", i), i)
            else:
                for i in range(12):
                    B.plan(("in1", i), (4 + i) % 8)
            for n in range(2 * HEADS):
                B.plan(("s", l, n), n % 3)
                B.plan(("t", l, n), 3 + n % 2)
                if n % 2 == 0:
                    B.plan(("o", l, n // 2), 5 + (n // 2) % 3)
            for i in range(4):
                B.plan(("out", l, i), i)
            for b in range(4):
                B.plan(("uT", l, "ffn", b), 4 + b)
            B.plan(("route parts", l), 1)
            B.plan(("route", l), 0)
            B.plan(("rank", l), 2)
            upto.append(list(B.uses))

        moe1 = [2 + LOTS] * 4 + [3 + LOTS] * 2
        moe0 = [1] * RING

        land = {("in", 0): [0] * RING, ("moe", 0): [16] * RING,
                ("in", 1): [16 + 32 * LOTS] * RING, ("out", 1): [32 + 32 * LOTS] * RING,
                ("moe", 1): [32 + 32 * LOTS] * 4 + [48 + 32 * LOTS] * 2}

        def arrived(eng, phase, s):
            eng.wait_ge(sem(f"slot{s}_landed"), land[phase][s] + 16)

        class Set:

            def __init__(self, name, l, ring_base, land_base, own):
                self.name, self.l, self.free_base, self.land_base = name, l, ring_base, land_base
                self.sel_built = sem(f"{name}_sel_built")
                self.wsel_built = sem(f"{name}_wsel_built")
                self.sel_step = sem(f"{name}_sel_step")
                self.gathered = sem(f"{name}_gathered")
                self.x_ready = sem(f"{name}_x_ready")
                self.w_turned = sem(f"{name}_w_turned")
                self.w_ready = sem(f"{name}_w_ready")
                self.part_ready = sem(f"{name}_part_ready")
                self.summed = sem(f"{name}_summed")
                self.silu_ready = sem(f"{name}_silu_ready")
                self.h_ready = sem(f"{name}_h_ready")
                self.y_done = sem(f"{name}_y_done")
                self.y0_ready = sem(f"{name}_y0_ready")
                self.y1_ready = sem(f"{name}_y1_ready")
                self.combined = sem(f"{name}_combined")
                self.added = sem(f"{name}_added")
                self.landed = [sem(f"{'more' + str(l) + '_' if own else ''}slot{s}_landed") for s in range(RING)]
                self.freed = [sem(f"{'more' + str(l) + '_' if own else ''}slot{s}_freed") for s in range(RING)]

        main = [Set("moe", l, [n - LOTS * l for n in (moe0, moe1)[l]],
                    [n - 32 * LOTS * l for n in land[("moe", l)]], False) for l in range(DEPTH)]
        more = [Set(f"more{l}", l, [1] * RING, [0] * RING, True) for l in range(DEPTH)]

        PLACING = 3
        AWAY = -65536.0

        def h_complete(eng, i):
            if i == 0:
                eng.wait_ge(sem("x_loaded"), 16 * TT)
            elif i % 2:
                for b in range(4):
                    B.taken(eng, ("out", i // 2, b))
            else:
                eng.wait_ge(sem(f"moe_added{i // 2 - 1}"), 1)

        def pv_done(eng, l, n):
            if n % 2 == 0:
                eng.wait_ge(sem(f"pv_even{l}"), n // 2 + 1)
            else:
                B.read(eng, ("o", l, n // 2))

        def is_sb(l, n):
            return l == 1 and n >= HEADS

        def swa_head(n):
            return (n - HEADS) // 2 + 4 * (n % 2)

        def in1_reads(eng, e, which):
            dst = ([qT[:, 2 * i:2 * i + 2, :] for i in (0, 1)] + [kT[:, 2 * i:2 * i + 2, :] for i in (0, 1)]
                   + [v1[:, i, :] for i in range(TT)]
                   + [qT[:, 4 + 2 * i:6 + 2 * i, :] for i in (0, 1)] + [kT[:, 4 + 2 * i:6 + 2 * i, :] for i in (0, 1)]
                   + [v2[:, i, :] for i in range(TT)])
            for i in range(12):
                if i % 2 == which:
                    src = B.read(eng, ("in1", i))
                    o = dst[i]
                    s = src[:, :] if i in (4, 5, 10, 11) else src[:, :].rearrange("p (c t) -> p c t", c=2)
                    if which:
                        ins = e.activation(o, s, ACT.Copy)
                    else:
                        ins = e.tensor_copy(o, s)
                    B.release(ins, ("in1", i))

        def act_lot(act, q, it):
            for e in range(LOT):
                act.wait_ge(q.freed[e], q.free_base[e] + 1 + it)
                if e >= 2:
                    act.wait_ge(q.summed, it * LOT + (e - 1))
                nc.scalar.activation(part[:, e % 2, :], bank[e % 2][:, :], ACT.Copy).then_inc(q.part_ready, 1)
            act.wait_ge(q.summed, it * LOT + LOT)
            nc.scalar.activation(sil[:, :, :], bank[2][:, 0:2 * P].rearrange("p (j s) -> p j s", j=2),
                                 ACT.Silu).then_inc(q.silu_ready, 1)
            act.wait_ge(q.y_done, it + 1)
            nc.scalar.activation(ys[:, 0, :], bank[4][:, :], ACT.Copy).then_inc(q.y0_ready, 1)

        def route(dve, V, l, step):
            NG = GROUPS

            def wide(a, n):
                return a.unsqueeze(2).broadcast_to([P, TT, n])

            src = B.read(dve, ("route parts", l))
            V.tensor_copy(part[0:NR, 0, 0:T], src[0:NR, 0:T]).then_inc(sem("logits0_ready"), 1)
            src = B.read(dve, ("route", l))
            dve.sem_inc(B.free[B.at[("route parts", l)][0]], 1)
            rb = pcol(f"rbias{l}").unsqueeze(1).broadcast_to([P, TT, NR])
            ins = V.tensor_tensor(lg[:, :, :], src[:, 0:TT * HD].rearrange("p (t n) -> p t n", t=TT)[:, :, 0:NR],
                                  rb, ALU.add)
            B.release(ins, ("route", l))
            B.taken(dve, ("route", l))
            G, E = lg[:, :, 0:NG], lg[:, :, NG:]
            best = rt[:, 0, :, 0:8]

            def col(i):
                return best[:, :, i]

            step(dve, V.tensor_reduce(col(0), G, AX.X, ALU.max))
            V.tensor_tensor(rt[:, 1, :, 0:NG], G, wide(col(0), NG), ALU.subtract).then_inc(sem(f"glog_ready{l}"), 1)

            def first_max(x_, top, order, n_, tmp, mark):
                for tt in range(TT):
                    ins = V.scalar_tensor_tensor(out=tmp[:, tt, :], in0=x_[:, tt, :], scalar=best[:, tt, top:top + 1],
                                                 in1=order, op0=ALU.is_equal, op1=ALU.mult)
                step(dve, ins)
                step(dve, V.tensor_reduce(col(1), tmp, AX.X, ALU.max))
                step(dve, V.tensor_tensor(mark, tmp, wide(col(1), n_), ALU.is_equal))

            first_max(G, 0, c("first4"), NG, rt[:, 2, :, 0:NG], rt[:, 3, :, 0:NG])
            step(dve, V.tensor_scalar(rt[:, 2, :, 0:NG], rt[:, 3, :, 0:NG], 1.0, -NEG, ALU.subtract, ALU.mult))
            step(dve, V.tensor_tensor(rt[:, 4, :, :].rearrange("p t (g e) -> p t g e", g=NG),
                                      E.rearrange("p t (g e) -> p t g e", g=NG),
                                      rt[:, 2, :, 0:NG].unsqueeze(3).broadcast_to([P, TT, NG, PER_GROUP]), ALU.add))
            step(dve, V.tensor_reduce(col(2), rt[:, 4, :, :], AX.X, ALU.max))
            first_max(rt[:, 4, :, :], 2, c("first32"), EXPERTS, rt[:, 5, :, :], rt[:, 6, :, :])
            step(dve, V.scalar_tensor_tensor(out=rt[:, 4, :, :], in0=rt[:, 6, :, :], scalar=3.0 * NEG,
                                             in1=rt[:, 4, :, :], op0=ALU.mult, op1=ALU.add))
            step(dve, V.tensor_reduce(col(3), rt[:, 4, :, :], AX.X, ALU.max))
            first_max(rt[:, 4, :, :], 3, c("first32"), EXPERTS, rt[:, 5, :, :], rt[:, 7, :, :])
            V.tensor_tensor(mem[:, :, :], rt[:, 6, :, :], rt[:, 7, :, :], ALU.add).then_inc(sem("members"), 1)
            V.tensor_tensor(st[:, 10:12], col(3), col(2), ALU.subtract).then_inc(sem(f"gap_ready{l}"), 1)


            def marked(dst, i, values):
                for tt in range(TT):
                    ins = V.tensor_tensor_reduce(rt[:, 8 + i, tt, :], rt[:, 6 + i, tt, :], values(tt), 1.0, 0.0,
                                                 ALU.mult, ALU.add, dst[:, tt, i:i + 1])
                return ins

            for i in range(2):
                ins = marked(base, i, lambda tt: c("slot0"))
            step(dve, ins)
            dve.wait_ge(sem(f"gexp_ready{l}"), 1)
            step(dve, V.tensor_reduce(col(4), rt[:, 1, :, 0:NG], AX.X, ALU.add))
            dve.wait_ge(sem(f"gapexp_ready{l}"), 1)
            step(dve, V.scalar_tensor_tensor(out=col(5), in0=st[:, 12:14], scalar=1.0, in1=col(4),
                                             op0=ALU.add, op1=ALU.mult))
            step(dve, V.reciprocal(gate[:, :, 0], col(5)))
            step(dve, V.tensor_tensor(gate[:, :, 1], gate[:, :, 0], st[:, 12:14], ALU.mult))
            src = B.read(dve, ("rank", l))
            for i in range(2):
                marked(rank, i, lambda tt: src[:, tt * EXPERTS:(tt + 1) * EXPERTS])
            ins = V.tensor_reduce(st[:, 14:15], src[:, TT * EXPERTS:(TT + 1) * EXPERTS], AX.X, ALU.max)
            B.release(ins, ("rank", l))
            B.taken(dve, ("rank", l))

        def count_rounds(dve, V, l, step):
            step(dve, V.tensor_scalar(rt[:, 10, 0, 0:ROUNDS - 1], c("limits"), st[:, 14:15], None, ALU.is_lt))
            step(dve, V.tensor_reduce(st[:, 15:16], rt[:, 10, 0, 0:ROUNDS - 1], AX.X, ALU.add))
            V.tensor_scalar(nrounds[:, :], st[:, 15:16], 1.0, None, ALU.add).then_inc(sem(f"rounds_known{l}"), 1)

        def placing(V, later):
            over, pos, under = rt[:, 11, :, 0:2], rt[:, 12, :, 0:2], rt[:, 13, :, 0:2]
            V.tensor_scalar(over, rank[:, :, :], float(SLOTS), AWAY, ALU.is_ge, ALU.mult)
            ins = V.tensor_tensor(pos, base[:, :, :], rank[:, :, :], ALU.add)
            if later:
                yield V.tensor_scalar(under, rank[:, :, :], 0.0, AWAY, ALU.is_lt, ALU.mult)
                yield V.tensor_tensor(over, over, under, ALU.add)
            else:
                yield ins
            yield V.tensor_tensor(cur[:, :, :], pos, over, ALU.add)

        def place(dve, V, step):
            for ins in placing(V, False):
                step(dve, ins)

        def next_round(dve, V, l, r):
            s = sem(f"round_step{l}")
            n = (r - 1) * (PLACING + 1)
            V.tensor_scalar(rank[:, :, :], rank[:, :, :], float(SLOTS), None, ALU.subtract).then_inc(s, 1)
            dve.wait_ge(s, n + 1)
            for k, ins in enumerate(placing(V, True)):
                ins.then_inc(s, 1)
                dve.wait_ge(s, n + k + 2)

        def pick(dve, V, q, n):
            for tt in range(TT):
                ins = V.tensor_scalar(sel[:, tt, :], c("iota"), cur[:, tt, 0:1], None, ALU.is_equal)
            ins.then_inc(q.sel_step, 1)
            dve.wait_ge(q.sel_step, n * 2 + 1)
            for tt in range(TT):
                ins = V.scalar_tensor_tensor(out=sel[:, tt, :], in0=c("iota"), scalar=cur[:, tt, 1:2],
                                             in1=sel[:, tt, :], op0=ALU.is_equal, op1=ALU.add)
            ins.then_inc(q.sel_built, 1)
            for tt in range(TT):
                for i in range(2):
                    ins = V.tensor_scalar(wsel[:, 2 * tt + i, :], c("iota"), cur[:, tt, i:i + 1],
                                          gate[:, tt, i:i + 1], ALU.is_equal, ALU.mult)
            ins.then_inc(q.wsel_built, 1)
            dve.wait_ge(q.wsel_built, n + 1)
            V.tensor_scalar(cur[:, :, :], cur[:, :, :], float(P), None, ALU.subtract).then_inc(q.sel_step, 1)
            dve.wait_ge(q.sel_step, n * 2 + 2)
            V.memset(st[:, 9:10], 0.0)

        def dve_lot(dve, V, q, it, n):
            l = q.l
            gain = par[:, PAR[f"gffn{l}"][0]:PAR[f"gffn{l}"][1]]
            for hf in range(2):
                dve.wait_ge(q.gathered, it * 2 + (hf + 1))
                ks = slice(4 * hf, 4 * hf + 4)
                V.tensor_tensor(xg[:, ks, :], bank[(3, 2)[hf]][:, :].rearrange("p (k s) -> p k s", k=4),
                                gain[:, ks].unsqueeze(2).broadcast_to([P, 4, P]), ALU.mult).then_inc(q.x_ready, 1)
            dve.wait_ge(q.w_turned, it + 1)
            V.tensor_copy(wT[:, :], bank[4][:, 0:T]).then_inc(q.w_ready, 1)
            pick(dve, V, q, n)
            dve.wait_ge(q.silu_ready, it + 1)
            V.tensor_tensor(hT[:, :, :], sil[:, :, :], bank[2][:, 2 * P:4 * P].rearrange("p (j s) -> p j s", j=2),
                            ALU.mult).then_inc(q.h_ready, 1)
            dve.wait_ge(q.freed[RING - 1], q.free_base[RING - 1] + 1 + it)
            V.tensor_copy(ys[:, 1, :], bank[5][:, :]).then_inc(q.y1_ready, 1)
            for hf in range(2):
                for tt in range(TT):
                    dve.wait_ge(q.combined, it * 4 + (2 * hf + tt + 1))
                    dst = h[:, tt, hf * HALF:(hf + 1) * HALF]
                    V.tensor_tensor(dst, dst, bank[6 + tt][:, :], ALU.add).then_inc(q.added, 1)

        def pe_lot(pe, q, it, n):
            def mm(o, lhsT, rhs, start, stop, **kw):
                return nc.tensor.matmul(o, lhsT, rhs, start=start, stop=stop, **kw)

            pe.wait_ge(q.sel_built, n + 1)
            for hf in range(2):
                for k in range(4):
                    for tt in range(TT):
                        src = u[:, tt, :].rearrange("p (d k) -> p k d", k=KD)[:, 4 * hf + k, :]
                        ins = mm(bank[(3, 2)[hf]][:, k * P:(k + 1) * P], src, sel[:, tt, :], tt == 0, tt == TT - 1)
                ins.then_inc(q.gathered, 1)
            pe.wait_ge(q.wsel_built, n + 1)
            for tt in range(TT):
                for i in range(2):
                    ins = mm(bank[4][:, tt * P:(tt + 1) * P], wsel[:, 2 * tt + i, :], ident, i == 0, i == 1)
            ins.then_inc(q.w_turned, 1)

            def total(e):
                pe.wait_ge(q.part_ready, it * LOT + (e + 1))
                for j in range(4):
                    ins = mm(bank[2][:, j * P + e * SLOTS:j * P + (e + 1) * SLOTS],
                             part[:, e % 2, j * P:(j + 1) * P], c("stack"), True, True)
                ins.then_inc(q.summed, 1)

            for e in range(LOT):
                pe.wait_ge(q.landed[e], q.land_base[e] + (it + 1) * 32)
                if e >= 2:
                    pe.wait_ge(q.part_ready, it * LOT + (e - 1))
                w = ring[:, e, :].rearrange("p (w k f) -> p k w f", w=2, k=KD)
                for k in range(KD):
                    if e == 0 and k % 4 == 0:
                        pe.wait_ge(q.x_ready, it * 2 + (k // 4 + 1))
                    cg = SLOTS * (k % 4)
                    ins = mm(bank[e % 2][cg:cg + SLOTS, :].rearrange("p (w f) -> p w f", w=2),
                             xg[:, k, e * SLOTS:(e + 1) * SLOTS], w[:, k], k < 4, k >= 4)
                ins.then_inc(q.freed[e], 1)
                if e:
                    total(e - 1)
            total(LOT - 1)
            pe.wait_ge(q.h_ready, it + 1)
            pe.wait_ge(q.w_ready, it + 1)
            for pair in range(2):
                s = LOT + pair
                pe.wait_ge(q.landed[s], q.land_base[s] + (it + 1) * 32)
            for hf in range(2):
                for j in range(2):
                    for e in range(LOT):
                        w = ring[:, LOT + e // 2, :].rearrange("p (e j n) -> p e j n", e=2, j=2)
                        ins = mm(bank[4 + hf][e * SLOTS:(e + 1) * SLOTS, :], hT[:, j, e * SLOTS:(e + 1) * SLOTS],
                                 w[:, e % 2, j, hf * HALF:(hf + 1) * HALF], j == 0, j == 1)
                        if hf == 1 and j == 1 and e in (1, 3):
                            ins.then_inc(q.freed[LOT + e // 2], 1)
                if hf == 0:
                    ins.then_inc(q.y_done, 1)
            for hf in range(2):
                pe.wait_ge((q.y0_ready, q.y1_ready)[hf], it + 1)
                for tt in range(TT):
                    if hf:
                        pe.wait_ge(q.added, it * 4 + (tt + 1))
                    mm(bank[6 + tt][:, :], wT[:, tt * P:(tt + 1) * P], ys[:, hf, :], True, True)\
                        .then_inc(q.combined, 1)

        block = ctx.enter_context(nc.Block())

        @block.sync
        def _(sp):
            def up_loads(q, it, g):
                for e in range(LOT):
                    sp.wait_ge(q.freed[e], q.free_base[e] + it)
                    half = ring[:, e, :].rearrange("p (w n) -> p w n", w=2)
                    for w, src in enumerate((w_gate, w_up)):
                        one = src[q.l, bass.ds(g * LOT + e, 1)].rearrange("e (p k) f -> p (e k f)", k=KD)
                        sp.dma_start(half[:, w, :], one).then_inc(q.landed[e], 16)

            def down_loads(q, it, g):
                for pair in range(LOT // 2):
                    s = LOT + pair
                    sp.wait_ge(q.freed[s], q.free_base[s] + it)
                    half = ring[:, s, :].rearrange("p (e j n) -> p e j n", e=2, j=2)
                    for e in range(2):
                        one = w_down[q.l, bass.ds(g * LOT + 2 * pair + e, 1)]
                        sp.dma_start(half[:, e], one.rearrange("e (j p) d -> p (e j) d", p=P))\
                          .then_inc(q.landed[s], 16)

            def expert_loads(q, it, g):
                up_loads(q, it, g)
                down_loads(q, it, g)

            def more_rounds(l):
                sp.wait_ge(sem(f"rounds_known{l}"), 1)
                r_end = sp.value_load(nrounds[0:1, 0:1], min_val=1, max_val=ROUNDS)
                with sp.If(r_end > 1):
                    for s in range(RING):
                        sp.wait_ge(main[l].freed[s], main[l].free_base[s] + LOTS * (l + 1))
                    with sp.Fori(1, r_end) as r:
                        with sp.Fori(0, LOTS) as g:
                            expert_loads(more[l], (r - 1) * LOTS + g, g)
                    sp.wait_ge(sem(f"moe_added{l}"), 1)
                with sp.Else():
                    sp.nop()

            for tt in range(TT):
                sp.dma_start(h[:, tt, :], x[0, tt * P:(tt + 1) * P, :]).then_inc(sem("x_loaded"), 16)
            sp.dma_start(par[:, 0:PAR_COLS - D], params[:, 0:PAR_COLS - D]).then_inc(sem("par_loaded"), 16)
            sp.dma_start(con[:, :], consts).then_inc(sem("con_loaded"), 16)
            for s in range(3):
                sp.dma_start(ring[:, s, :], stream[s]).then_inc(sem(f"slot{s}_landed"), 16)
                if s == 1:
                    sp.dma_start(ring[:, 3, 0:1024], kvb).then_inc(sem("slot3_landed"), 16)
            for s in range(LOT, RING):
                sp.dma_start(ring[:, s, :], stream[s - 1]).then_inc(sem(f"slot{s}_landed"), 16)
            sp.dma_start(par[:, PAR_COLS - D:], params[:, PAR_COLS - D:]).then_inc(sem("gfinal_loaded"), 16)
            up_loads(main[0], 0, 0)
            down_loads(main[0], 0, 0)
            with sp.Fori(1, LOTS) as g:
                expert_loads(main[0], g, g)
            more_rounds(0)
            for s in range(RING):
                sp.wait_ge(sem(f"slot{s}_freed"), moe0[s] + LOTS)
                sp.dma_start(ring[:, s, :], stream[5 + s]).then_inc(sem(f"slot{s}_landed"), 16)
            up_loads(main[1], LOTS, 0)
            for s in range(LOT, RING):
                sp.wait_ge(sem(f"slot{s}_freed"), moe0[s] + LOTS + 1)
                sp.dma_start(ring[:, s, :], stream[11 + s - LOT]).then_inc(sem(f"slot{s}_landed"), 16)
            down_loads(main[1], LOTS, 0)
            with sp.Fori(1, LOTS) as g:
                expert_loads(main[1], LOTS + g, g)
            more_rounds(1)
            for tt in range(TT):
                sp.wait_ge(sem("final_ready"), tt + 1)
                sp.dma_start(out[0, tt * P:(tt + 1) * P, :], u[:, tt, :]).then_inc(sem("stored"), 16)
            sp.wait_ge(sem("stored"), 16 * TT)

        @block.gpsimd
        def _(pool):
            pool.wait_ge(sem("rows_step"), 1)
            B.taken(pool, "rows")
            for w in range(2):
                skewed = bias_rows[w].rearrange("h (q x) -> h q x", q=P)[:, :, 0:BLK]
                pool.dma_start(skewed, rows[:, w, :].unsqueeze(1).broadcast_to([HEADS, P, BLK]))\
                    .then_inc(sem("rows_stored"), 16)
            pool.wait_ge(sem("rows_stored"), 32)

            def spread(w):
                for seg, (a, n) in enumerate(((0, T), (T, P))):
                    src_ap = bass.AP(bias_rows.tensor, w * HEADS * P * (BLK + 1) + P - 1 + seg * P,
                                     [[BLK, P], [P * (BLK + 1), HEADS], [1, n]])
                    pool.dma_start(bias[:, :, a:a + n], src_ap).then_inc(sem("bias_ready"), 16)

            spread(0)
            pool.wait_ge(sem("kr_parts"), 1)
            B.taken(pool, ("low", 3))
            src = [krt[HD:P, i, :].unsqueeze(1).broadcast_to([HD, HEADS, T]) for i in range(2)]
            nc.gpsimd.tensor_tensor(kT[HD:P, :, :], src[0], src[1], ALU.add).then_inc(sem("kr_ready"), 1)
            pool.wait_ge(sem("moe_added0"), 1)
            spread(1)

        @block.scalar
        def _(act):
            step = Steps(sem("act_step"))
            act.dma_start(tab[:, :], table).then_inc(sem("tab_loaded"), 16)
            act.dma_start(hot[:, :], onehot).then_inc(sem("tab_loaded"), 16)
            act.dma_start(msk[:, :, :], masks).then_inc(sem("tab_loaded"), 16)
            act.dma_start(rw[:, :, :, :], router_w).then_inc(sem("par_loaded"), 16)

            def norm_half(i):
                act.wait_ge(sem("eps_ready"), 1)
                nc.scalar.activation(st[:, 6:7], st[:, 8:9], ACT.Sqrt)
                h_complete(act, i)
                act.wait_ge(sem("h_read"), i)
                nc.scalar.activation(junk[:, :], h[:, 0, :], ACT.Square,
                                     accum_out=st[:, 0:1]).then_inc(sem("ss_act"), 1)
                act.wait_ge(sem("ss_act"), i + 1)
                act.wait_ge(sem("ss_dve"), i + 1)
                nc.scalar.activation(st[:, 2:4], st[:, 0:2], ACT.Sqrt, bias=st[:, 8:9],
                                     scale=1.0 / D).then_inc(sem("std_ready"), 1)

            def normed_tile0(i):
                act.wait_ge(sem("rstd_ready"), i + 1)
                nc.scalar.activation(u[:, 0, :], h[:, 0, :], ACT.Copy, scale=st[:, 4:5])\
                  .then_inc(sem("u0_ready"), 1)

            def uT_banks(l, which):
                for b in (0, 2):
                    src = B.read(act, ("uT", l, which, b))
                    for j in range(2):
                        k = 2 * b + j
                        ins = nc.scalar.activation(uT[:, k, :], src[:, j * T:(j + 1) * T], ACT.Copy,
                                                   scale=pcol(f"g{which}{l}", k))
                    B.release(ins, ("uT", l, which, b))

            for l in range(DEPTH):
                norm_half(2 * l)
                normed_tile0(2 * l)
                if l == 0:
                    act.wait_ge(sem("con_loaded"), 16)
                    act.wait_ge(sem("par_loaded"), 32)
                uT_banks(l, "mix")
                if l == 0:
                    for i in range(2):
                        src = B.read(act, ("swq", i))
                        ins = nc.scalar.activation(swq[:, 2 * i:2 * i + 2, :],
                                                   src[:, :].rearrange("p (c t) -> p c t", c=2), ACT.Copy)
                        B.release(ins, ("swq", i))
                    src = B.read(act, "ssq")
                    nc.scalar.activation(lowr[:, 0, :], src[:, 0:T], ACT.Sqrt, bias=st[:, 8:9], scale=1.0 / MLA_QR)
                    ins = nc.scalar.activation(lowr[:, 1, :], src[:, T:2 * T], ACT.Sqrt, bias=st[:, 8:9],
                                               scale=1.0 / MLA_KVR)
                    B.release(ins, "ssq")
                    for i in range(4):
                        src = B.read(act, ("mk", i))
                        ins = nc.scalar.activation(kT[0:HD, 2 * i:2 * i + 2, :],
                                                   src[0:HD, :].rearrange("p (c t) -> p c t", c=2), ACT.Copy)
                        B.release(ins, ("mk", i))
                else:
                    in1_reads(act, nc.scalar, 1)

                for i in range(2 * HEADS + 2):
                    if i < 2 * HEADS:
                        j = i % 3
                        if not is_sb(l, i):
                            act.wait_ge(sem(f"max_ready{l}"), i + 1)
                            if i >= 3:
                                B.read(act, ("t", l, i - 3))
                            nc.scalar.activation(pr[:, j, 0:T], sc[:, j, 0:T], ACT.Exp, bias=nm[:, j, 0:1],
                                                 accum_out=nm[:, j, 2:3])
                            ins = nc.scalar.activation(pr[:, j, T:BLK], sc[:, j, T:BLK], ACT.Exp,
                                                       bias=nm[:, j, 1:2], accum_out=nm[:, j, 3:4])
                            if l == 0 and i >= HEADS:
                                hh = swa_head(i)
                                ins = nc.scalar.activation(nm[:, j, 4:6], nm[:, j, 0:2], ACT.Exp,
                                                           bias=pcol("sinks", hh))
                            ins.then_inc(sem(f"exp_ready{l}"), 1)
                        else:
                            B.taken(act, ("s", l, i))
                            B.read(act, ("t", l, i - 3))
                            nc.scalar.activation(pr[:, j, :], sc[:, j, :], ACT.Sigmoid, scale=-1.0)\
                              .then_inc(sem("left_ready"), 1)
                            nc.scalar.activation(sc[:, j, :], sc[:, j, :], ACT.Sigmoid)\
                              .then_inc(sem("share_ready"), 1)
                    if i >= 2:
                        n = i - 2
                        src = B.read(act, ("t", l, n))
                        if n >= 2:
                            pv_done(act, l, n - 2)
                        ins = nc.scalar.activation(pt[:, n % 2, :], src[:, 0:BLK], ACT.Copy)
                        B.release(ins, ("t", l, n))

                norm_half(2 * l + 1)
                normed_tile0(2 * l + 1)
                uT_banks(l, "ffn")
                src = B.read(act, ("route parts", l))
                nc.scalar.activation(part[0:NR, 0, T:2 * T], src[HD:HD + NR, 0:T], ACT.Copy)\
                  .then_inc(sem("logits1_ready"), 1)
                act.wait_ge(sem(f"glog_ready{l}"), 1)
                nc.scalar.activation(rt[:, 1, :, 0:GROUPS], rt[:, 1, :, 0:GROUPS], ACT.Exp)\
                  .then_inc(sem(f"gexp_ready{l}"), 1)
                act.wait_ge(sem(f"gap_ready{l}"), 1)
                nc.scalar.activation(st[:, 12:14], st[:, 10:12], ACT.Exp).then_inc(sem(f"gapexp_ready{l}"), 1)

                with act.Fori(0, LOTS) as g:
                    act_lot(act, main[l], LOTS * l + g)
                act.wait_ge(sem(f"rounds_known{l}"), 1)
                r_end = act.value_load(nrounds[0:1, 0:1], min_val=1, max_val=ROUNDS)
                with act.If(r_end > 1):
                    with act.Fori(1, r_end) as r:
                        with act.Fori(0, LOTS) as g:
                            act_lot(act, more[l], (r - 1) * LOTS + g)
                with act.Else():
                    act.nop()
            norm_half(2 * DEPTH)

        @block.vector
        def _(dve):
            step = Steps(sem("dve_step"))
            V = nc.vector
            step(dve, V.memset(st[:, 8:9], EPS))
            V.memset(st[:, 9:10], 0.0).then_inc(sem("eps_ready"), 1)

            def bias_over_distances():
                dve.wait_ge(sem("con_loaded"), 16)
                dve.wait_ge(sem("par_loaded"), 32)
                dve.wait_ge(sem("tab_loaded"), 48)
                step(dve, V.tensor_scalar(nsink[:, :], pcol("sinks"), -1.0, None, ALU.mult))
                src = B.read(dve, "rows")
                for w in range(2):
                    ins = V.tensor_tensor(rows[:, w, :], src[0:HEADS, 0:BLK], msk[:, w, :], ALU.add)
                    if w == 0:
                        ins.then_inc(sem("rows_step"), 1)
                B.release(ins, "rows")

            def roots(i):
                h_complete(dve, i)
                V.tensor_tensor_reduce(u[:, 1, :], h[:, 1, :], h[:, 1, :], 1.0, 0.0, ALU.mult, ALU.add,
                                       st[:, 1:2]).then_inc(sem("ss_dve"), 1)
                dve.wait_ge(sem("std_ready"), i + 1)
                V.reciprocal(st[:, 4:6], st[:, 2:4]).then_inc(sem("rstd_ready"), 1)
                dve.wait_ge(sem("rstd_ready"), i + 1)
                dve.wait_ge(sem("ss_dve"), i + 1)

            def norm_turn(i, l, which):
                roots(i)
                V.tensor_scalar(u[:, 1, :], h[:, 1, :], st[:, 5:6], None, ALU.mult).then_inc(sem("u1_ready"), 1)
                if i == 0:
                    bias_over_distances()
                for b in (1, 3):
                    src = B.read(dve, ("uT", l, which, b))
                    for j in range(2):
                        k = 2 * b + j
                        ins = V.tensor_scalar(uT[:, k, :], src[:, j * T:(j + 1) * T], pcol(f"g{which}{l}", k),
                                              None, ALU.mult)
                    B.release(ins, ("uT", l, which, b))
                dve.wait_ge(sem("u0_ready"), i + 1)
                dve.wait_ge(sem("u1_ready"), i + 1)
                dve.sem_inc(sem("h_read"), 1)

            for l in range(DEPTH):
                norm_turn(2 * l, l, "mix")
                if l == 0:
                    for i in range(3):
                        src = B.read(dve, ("low", i))
                        ins = V.tensor_copy(low[:, i, :], src[:, 0:T])
                        B.release(ins, ("low", i))
                        B.taken(dve, ("low", i))
                        V.tensor_tensor(lowsq[:, i, :], low[:, i, :], low[:, i, :], ALU.mult)\
                         .then_inc(sem("lowsq_ready"), 1)
                    src = B.read(dve, ("low", 3))
                    V.tensor_tensor(krt[HD:P, 0, :], src[HD:P, 0:T], c("kcos", slice(HD, P)), ALU.mult)\
                     .then_inc(sem("kr_parts"), 1)
                    ins = V.tensor_tensor(krt[HD:P, 1, :], src[HD:P, T:2 * T], c("ksin", slice(HD, P)), ALU.mult)
                    B.release(ins, ("low", 3))
                    src = B.read(dve, "swk")
                    ins = V.tensor_copy(swk[:, :], src[:, 0:T])
                    B.release(ins, "swk")
                    src = B.read(dve, "swv")
                    ins = V.tensor_copy(v2[:, :, 0:P], src[:, 0:2 * P].rearrange("p (t n) -> p t n", t=TT))
                    B.release(ins, "swv")
                    B.taken(dve, "ssq")
                    step(dve, V.reciprocal(lowr[:, :, :], lowr[:, :, :]))
                    for i in range(3):
                        g = pcol("gkv", 0) if i == 2 else pcol("gq", i)
                        V.scalar_tensor_tensor(out=low[:, i, :], in0=low[:, i, :], scalar=g,
                                               in1=lowr[:, i // 2, :], op0=ALU.mult, op1=ALU.mult)\
                         .then_inc(sem("lown_ready"), 1)
                    for i in range(4):
                        src = B.read(dve, ("mq", i))
                        ins = V.tensor_tensor(qT[:, 2 * i:2 * i + 2, :], src[:, :].rearrange("p (c t) -> p c t", c=2),
                                              c("qrope").unsqueeze(1).broadcast_to([P, 2, T]), ALU.mult)
                        B.release(ins, ("mq", i))
                    for i in range(TT):
                        src = B.read(dve, ("mv", i))
                        ins = V.tensor_copy(v1[:, i, :], src[:, :])
                        B.release(ins, ("mv", i))
                else:
                    in1_reads(dve, V, 0)

                for i in range(2 * HEADS + 6):
                    if i < 2 * HEADS:
                        j = i % 3
                        src = B.read(dve, ("s", l, i))
                        if i >= 3 and not is_sb(l, i - 3):
                            dve.wait_ge(sem(f"exp_ready{l}"), i - 2)
                        if l == 0 and i < HEADS:
                            scale, add = MLA_SCALE, c("causal")
                        elif l == 0:
                            scale, add = HEAD_SCALE, bias[:, swa_head(i), :]
                            dve.wait_ge(sem("bias_ready"), 32)
                        elif i < HEADS:
                            scale, add = HEAD_SCALE, bias[:, i, :]
                            dve.wait_ge(sem("bias_ready"), 64)
                        else:
                            scale, add = HEAD_SCALE, c("strict")
                        ins = V.scalar_tensor_tensor(out=sc[:, j, :], in0=src[:, 0:BLK], scalar=scale, in1=add,
                                                     op0=ALU.mult, op1=ALU.add)
                        B.release(ins, ("s", l, i))
                        if not is_sb(l, i):
                            B.taken(dve, ("s", l, i))
                            V.tensor_reduce(nm[:, j, 0:1], sc[:, j, 0:T], AX.X, ALU.max, negate=True)
                            ins = V.tensor_reduce(nm[:, j, 1:2], sc[:, j, T:BLK], AX.X, ALU.max, negate=True)
                            if l == 0 and i >= HEADS:
                                step(dve, ins)
                                hh = swa_head(i)
                                ins = V.tensor_scalar(nm[:, j, 0:2], nm[:, j, 0:2], nsink[:, hh:hh + 1], None, ALU.min)
                            ins.then_inc(sem(f"max_ready{l}"), 1)
                    n = i - 1
                    if is_sb(l, n) and n < 2 * HEADS:
                        j = n % 3
                        if n == HEADS:
                            step(dve, V.memset(after[:, BLK:BLK + 1], 1.0))
                        dve.wait_ge(sem("left_ready"), n - HEADS + 1)
                        if n > HEADS:
                            dve.wait_ge(sem("sb_ready"), n - HEADS)
                        step(dve, V.tensor_tensor_scan(after[:, 0:BLK][:, ::-1], pr[:, j, ::-1],
                                                       c("restart")[:, ::-1], 1.0, ALU.mult, ALU.max))
                        dve.wait_ge(sem("share_ready"), n - HEADS + 1)
                        V.tensor_tensor(pr[:, j, :], sc[:, j, :], after[:, 1:BLK + 1], ALU.mult)\
                         .then_inc(sem("sb_ready"), 1)
                    elif 0 <= n < 2 * HEADS:
                        j = n % 3
                        dve.wait_ge(sem(f"exp_ready{l}"), n + 1)
                        if l == 0 and n >= HEADS:
                            step(dve, V.tensor_tensor(nm[:, j, 2:4], nm[:, j, 2:4], nm[:, j, 4:6], ALU.add))
                        step(dve, V.reciprocal(nm[:, j, 6:8], nm[:, j, 2:4]))
                        V.tensor_scalar(pr[:, j, 0:T], pr[:, j, 0:T], nm[:, j, 6:7], None, ALU.mult)
                        V.tensor_scalar(pr[:, j, T:BLK], pr[:, j, T:BLK], nm[:, j, 7:8], None, ALU.mult)\
                         .then_inc(sem(f"p_ready{l}"), 1)
                    n = i - 4
                    if n >= 1 and n % 2 == 1 and n < 2 * HEADS:
                        src = B.read(dve, ("o", l, n // 2))
                        ins = V.tensor_copy(oT[:, n // 2, :], src[:, 0:T])
                        B.release(ins, ("o", l, n // 2))

                for i in range(4):
                    src = B.read(dve, ("out", l, i))
                    tt, hf = i // 2, i % 2
                    dst = h[:, tt, hf * HALF:(hf + 1) * HALF]
                    ins = V.tensor_tensor(dst, dst, src[:, :], ALU.add)
                    B.release(ins, ("out", l, i))

                norm_turn(2 * l + 1, l, "ffn")
                route(dve, V, l, step)
                place(dve, V, step)
                pick(dve, V, main[l], BUILDS * l)
                count_rounds(dve, V, l, step)
                with dve.Fori(0, LOTS) as g:
                    dve_lot(dve, V, main[l], LOTS * l + g, BUILDS * l + g + 1)
                dve.wait_ge(sem(f"rounds_known{l}"), 1)
                r_end = dve.value_load(nrounds[0:1, 0:1], min_val=1, max_val=ROUNDS)
                with dve.If(r_end > 1):
                    with dve.Fori(1, r_end) as r:
                        next_round(dve, V, l, r)
                        pick(dve, V, more[l], (r - 1) * BUILDS)
                        with dve.Fori(0, LOTS) as g:
                            dve_lot(dve, V, more[l], (r - 1) * LOTS + g, (r - 1) * BUILDS + g + 1)
                        dve.wait_ge(more[l].added, r * (LOTS * 4))
                    V.memset(st[:, 9:10], 0.0).then_inc(sem(f"moe_added{l}"), 1)
                with dve.Else():
                    dve.wait_ge(main[l].added, LOTS * (l + 1) * 4)
                    V.memset(st[:, 9:10], 0.0).then_inc(sem(f"moe_added{l}"), 1)

            roots(2 * DEPTH)
            dve.wait_ge(sem("gfinal_loaded"), 16)
            for tt in range(TT):
                V.scalar_tensor_tensor(out=u[:, tt, :], in0=h[:, tt, :], scalar=st[:, 4 + tt:5 + tt],
                                       in1=pcol("gfinal"), op0=ALU.mult, op1=ALU.mult)\
                 .then_inc(sem("final_ready"), 1)


        @block.tensor
        def _(pe):
            spent = []

            def carry(ins):
                if spent:
                    ins.then_inc(sem(f"slot{spent.pop()}_freed"), 1)
                return ins

            def mm(o, lhsT, rhs, start, stop, **kw):
                return carry(nc.tensor.matmul(o, lhsT, rhs, start=start, stop=stop, **kw))

            pe.wait_ge(sem("tab_loaded"), 48)
            o = B.begin(pe, "rows")
            B.written(mm(o[0:HEADS, 0:BLK], tab[:, :], hot[:, :], True, True), "rows")

            def turn_u(i, l, which):
                for tt in range(TT):
                    pe.wait_ge(sem(f"u{tt}_ready"), i + 1)
                    if i == 0 and tt == 0:
                        pe.wait_ge(sem("con_loaded"), 16)
                    for b in range(4):
                        o = B.begin(pe, ("uT", l, which, b)) if tt == 0 else bank[B.at[("uT", l, which, b)][0]]
                        for j in range(2):
                            src = u[:, tt, :].rearrange("p (d k) -> p k d", k=KD)[:, 2 * b + j, :]
                            ins = carry(nc.tensor.transpose(o[:, j * T + tt * P:j * T + (tt + 1) * P], src, ident))
                        if tt == TT - 1:
                            B.written(ins, ("uT", l, which, b))

            def turned(l, which, k):
                if k % 2 == 0:
                    B.taken(pe, ("uT", l, which, k // 2))

            def featured(o, w, cols, M, p0=0, first=None):
                for k in range(KD):
                    if first is not None:
                        turned(first, "mix", k)
                    ins = mm(o[p0:p0 + M, :], w[:, k, cols:cols + M], uT[:, k, :], k == 0, k == KD - 1)
                return ins

            def tokened(o, w, tt, cols, n):
                for k in range(KD):
                    ins = mm(o, uT[:, k, tt * P:(tt + 1) * P], w[:, k, cols:cols + n], k == 0, k == KD - 1)
                return ins

            def slot_freed(s):
                spent.append(s)

            for l in range(DEPTH):
                turn_u(2 * l, l, "mix")
                if l == 0:
                    arrived(pe, ("in", 0), 0)
                    w = win(0)
                    for i in range(3):
                        o = B.begin(pe, ("low", i))
                        B.written(featured(o[:, 0:T], w, i * P, P, first=0 if i == 0 else None), ("low", i))
                    o = B.begin(pe, ("low", 3))
                    featured(o[:, 0:T], w, 3 * P, HD, HD)
                    ins = featured(o[:, T:2 * T], w, 3 * P + HD, HD, HD)
                    B.written(ins, ("low", 3))
                    slot_freed(0)
                    arrived(pe, ("in", 0), 1)
                    w = win(1)
                    for i in range(2):
                        o = B.begin(pe, ("swq", i))
                        for j in range(2):
                            ins = featured(o[:, j * T:(j + 1) * T], w, (2 * i + j) * P, P)
                        B.written(ins, ("swq", i))
                    slot_freed(1)
                    arrived(pe, ("in", 0), 2)
                    w = ring[:, 2, 0:KD * T].rearrange("p (k n) -> p k n", k=KD)
                    o = B.begin(pe, "swk")
                    B.written(featured(o[:, 0:T], w, 0, P), "swk")
                    pe.wait_ge(sem("lowsq_ready"), 3)
                    o = B.begin(pe, "ssq")
                    mm(o[:, 0:T], ones, lowsq[:, 0, :], True, False)
                    mm(o[:, 0:T], ones, lowsq[:, 1, :], False, True)
                    B.written(mm(o[:, T:2 * T], ones, lowsq[:, 2, :], True, True), "ssq")
                    o = B.begin(pe, "swv")
                    for tt in range(TT):
                        ins = tokened(o[:, tt * P:(tt + 1) * P], w, tt, P, P)
                    B.written(ins, "swv")
                    wq = ring[:, 2, KD * T:].rearrange("p (k n) -> p k n", k=2)
                    pe.wait_ge(sem("lown_ready"), 2)
                    for i in range(4):
                        o = B.begin(pe, ("mq", i))
                        for j in range(2):
                            hh = 2 * i + j
                            for k in range(2):
                                ins = mm(o[:, j * T:(j + 1) * T], wq[:, k, hh * P:(hh + 1) * P], low[:, k, :],
                                         k == 0, k == 1)
                        B.written(ins, ("mq", i))
                    slot_freed(2)
                    arrived(pe, ("in", 0), 3)
                    pe.wait_ge(sem("lown_ready"), 3)
                    for i in range(4):
                        o = B.begin(pe, ("mk", i))
                        for j in range(2):
                            hh = 2 * i + j
                            ins = mm(o[0:HD, j * T:(j + 1) * T], ring[:, 3, hh * HD:(hh + 1) * HD], low[:, 2, :],
                                     True, True)
                        B.written(ins, ("mk", i))
                    for tt in range(TT):
                        o = B.begin(pe, ("mv", tt))
                        ins = mm(o[:, :], low[:, 2, tt * P:(tt + 1) * P], ring[:, 3, 512:1024], True, True)
                        B.written(ins, ("mv", tt))
                    slot_freed(3)
                    pe.wait_ge(sem("kr_ready"), 1)
                    for key in ([(name, i) for name in ("mk", "mq") for i in range(4)]
                                + [("swq", 0), ("swq", 1), ("mv", 0), ("mv", 1), "swk", "swv"]):
                        B.taken(pe, key)
                else:
                    n = 0
                    for s in range(RING):
                        arrived(pe, ("in", 1), s)
                        w = win(s)
                        for i in range(2):
                            o = B.begin(pe, ("in1", n))
                            if s % 3 == 2:
                                ins = tokened(o[:, :], w, i, 0, 512)
                            else:
                                for j in range(2):
                                    ins = featured(o[:, j * T:(j + 1) * T], w, (2 * i + j) * P, P,
                                                   first=l if n == 0 and j == 0 else None)
                            B.written(ins, ("in1", n))
                            n += 1
                        slot_freed(s)
                    for i in range(12):
                        B.taken(pe, ("in1", i))

                def operands(n):
                    if l == 0 and n < HEADS:
                        return qT[:, n, :], kT[:, n, :]
                    p0 = HD * (n % 2)
                    if l == 0:
                        return swq[p0:p0 + HD, (n - HEADS) // 2, :], swk[p0:p0 + HD, :]
                    return qT[p0:p0 + HD, n // 2, :], kT[p0:p0 + HD, n // 2, :]

                def values(n, tt):
                    if l == 0 and n >= HEADS:
                        return v2[:, tt, HD * (n % 2):HD * (n % 2) + HD]
                    return (v1 if n < HEADS else v2)[:, tt, (n % HEADS) * HD:(n % HEADS + 1) * HD]

                for i in range(2 * HEADS + 3):
                    if i < 2 * HEADS:
                        q_, k_ = operands(i)
                        o = B.begin(pe, ("s", l, i))
                        mm(o[:, 0:T], q_[:, P:T], k_, True, True)
                        B.written(mm(o[:, T:BLK], q_[:, 0:P], k_[:, 0:P], True, True), ("s", l, i))
                    n = i - 2
                    if 0 <= n < 2 * HEADS:
                        if is_sb(l, n):
                            pe.wait_ge(sem("sb_ready"), n - HEADS + 1)
                        else:
                            pe.wait_ge(sem(f"p_ready{l}"), n + 1)
                        w = pr[:, n % 3, :]
                        o = B.begin(pe, ("t", l, n))
                        nc.tensor.transpose(o[:, 0:P], w[:, T:BLK], ident)
                        nc.tensor.transpose(o[:, P:2 * P], w[:, 0:P], ident)
                        ins = nc.tensor.transpose(o[:, 2 * P:3 * P], w[:, P:2 * P], ident)
                        B.written(ins, ("t", l, n))
                    n = i - 3
                    if n >= 0:
                        B.taken(pe, ("t", l, n))
                        p0 = HD * (n % 2)
                        o = B.begin(pe, ("o", l, n // 2)) if n % 2 == 0 else bank[B.at[("o", l, n // 2)][0]]
                        mm(o[p0:p0 + HD, 0:T], values(n, 0), pt[:, n % 2, 0:T], True, True)
                        ins = mm(o[p0:p0 + HD, P:T], values(n, 1), pt[:, n % 2, T:BLK], False, True,
                                 skip_group_check=True)
                        if n % 2 == 0:
                            ins.then_inc(sem(f"pv_even{l}"), 1)
                        else:
                            B.written(ins, ("o", l, n // 2))

                for n in range(HEADS):
                    B.taken(pe, ("o", l, n))
                for i in range(4):
                    tt, hf = i // 2, i % 2
                    s = LOT + hf
                    if tt == 0:
                        arrived(pe, ("in", 0) if l == 0 else ("out", 1), s)
                    o = B.begin(pe, ("out", l, i))
                    for k in range(KD):
                        ins = mm(o[:, :], oT[:, k, tt * P:(tt + 1) * P], win(s)[:, k, :], k == 0, k == KD - 1)
                    B.written(ins, ("out", l, i))
                    if tt == 1:
                        slot_freed(s)

                turn_u(2 * l + 1, l, "ffn")
                o = B.begin(pe, ("route parts", l))
                for k in range(KD):
                    turned(l, "ffn", k)
                    p0 = HD * (k % 2)
                    ins = mm(o[p0:p0 + NR, 0:T], rw[:, l, k, :], uT[:, k, :], k < 2, k >= KD - 2)
                B.written(ins, ("route parts", l))
                o = B.begin(pe, ("route", l))
                pe.wait_ge(sem("logits0_ready"), l + 1)
                pe.wait_ge(sem("logits1_ready"), l + 1)
                for tt in range(TT):
                    for which in range(2):
                        ins = mm(o[:, tt * HD:tt * HD + NR], part[0:NR, 0, which * T + tt * P:which * T + (tt + 1) * P],
                                 ident[0:NR, 0:NR], which == 0, which == 1)
                B.written(ins, ("route", l))
                pe.wait_ge(sem("members"), l + 1)
                o = B.begin(pe, ("rank", l))
                both = mem[:, :, :].rearrange("p t e -> p (t e)")
                mm(o[:, 0:2 * EXPERTS], c("earlier"), both, True, False)
                mm(o[:, EXPERTS:2 * EXPERTS], ones, mem[:, 0, :], False, True)
                mm(o[:, 2 * EXPERTS:3 * EXPERTS], ones, mem[:, 0, :], True, False)
                ins = mm(o[:, 2 * EXPERTS:3 * EXPERTS], ones, mem[:, 1, :], False, True)
                B.written(ins, ("rank", l))
                for b in range(8):
                    pe.wait_ge(B.free[b], upto[l][b])

                with pe.Fori(0, LOTS) as g:
                    pe_lot(pe, main[l], LOTS * l + g, BUILDS * l + g)
                pe.wait_ge(sem(f"rounds_known{l}"), 1)
                r_end = pe.value_load(nrounds[0:1, 0:1], min_val=1, max_val=ROUNDS)
                with pe.If(r_end > 1):
                    for s in range(RING):
                        pe.sem_inc(more[l].freed[s], 1)
                    pe.wait_ge(main[l].added, LOTS * (l + 1) * 4)
                    with pe.Fori(1, r_end) as r:
                        with pe.Fori(0, LOTS) as g:
                            pe_lot(pe, more[l], (r - 1) * LOTS + g, (r - 1) * BUILDS + g)
                with pe.Else():
                    pe.nop()
                pe.wait_ge(sem(f"moe_added{l}"), 1)

def _stream(inp):
    def cols(w, parts):
        return np.ascontiguousarray(np.concatenate([w[:, a:b] for a, b in parts], 1)).reshape(P, -1)

    w0 = inp["w_in_even"][0]
    kr = MLA_QR + MLA_KVR
    half = ROPE // 2
    a, b = (kr, kr + half), (kr + half, kr + ROPE)
    qs = kr + ROPE
    slots = [cols(w0, [(0, kr), a, b, b, a, b, a, a, b])]
    heads = [(qs + HD * n, qs + HD * (n + 1)) for i in range(4) for n in (i, 4 + i)]
    slots.append(cols(w0, heads))
    ks = qs + HEADS * HD
    wq = inp["w_mla_qb"][0].reshape(2, P, HEADS, HD + ROPE)
    wq = np.concatenate([wq, wq[..., HD:]], -1).transpose(1, 0, 2, 3).reshape(P, -1)
    slots.append(np.concatenate([cols(w0, [(ks, ks + 256)]), wq], 1))
    wo = inp["w_out_even"][0].reshape(16, HD, D)
    order = list(range(8)) + [n for i in range(4) for n in (8 + i, 12 + i)]
    wo = wo[order].reshape(KD, P, D).transpose(1, 0, 2)
    slots += [wo[:, :, i * HALF:(i + 1) * HALF].reshape(P, -1) for i in range(2)]
    w1 = inp["w_in_odd"][0]
    slots += [cols(w1, [(512 * i, 512 * i + 512)]) for i in range(6)]
    wo = inp["w_out_odd"][0].reshape(KD, P, D).transpose(1, 0, 2)
    slots += [wo[:, :, i * HALF:(i + 1) * HALF].reshape(P, -1) for i in range(2)]
    return np.ascontiguousarray(np.stack(slots))


def kernel(**inputs):
    import concourse.bacc as bacc
    from concourse.bass_utils import run_bass_kernel_spmd

    inp = {k: np.asarray(v) for k, v in inputs.items()}
    consts, at = shape_constants()
    onehot, masks = distance_constants()
    kv = inp["w_mla_kvb"][0].reshape(P, HEADS, 2 * HD)
    par = np.empty((P, PAR_COLS), np.float32)

    def put(name, v):
        par[:, PAR[name][0]:PAR[name][1]] = v

    for l in range(DEPTH):
        put(f"gmix{l}", inp["norm_mix"][l].reshape(P, KD))
        put(f"gffn{l}", inp["norm_ffn"][l].reshape(P, KD))
        put(f"rbias{l}", np.concatenate([inp["moe_b_group"][l], inp["moe_b_router"][l]])[None])
    put("gq", inp["g_mla_q"][0].reshape(2, P).T)
    put("gkv", inp["g_mla_kv"][0].reshape(1, P).T)
    put("sinks", inp["swa_sinks"][0][None])
    put("gfinal", inp["norm_final"][None])
    rw = np.concatenate([inp["moe_w_group"], inp["moe_w_router"]], -1).reshape(DEPTH, P, KD, GROUPS + EXPERTS)
    arrays = {
        "in_x": inp["x"], "in_stream": _stream(inp),
        "in_kvb": np.ascontiguousarray(np.concatenate([kv[:, :, :HD].reshape(P, -1), kv[:, :, HD:].reshape(P, -1)], 1)),
        "in_router": np.ascontiguousarray(rw.transpose(1, 0, 2, 3)), "in_params": par,
        "in_table": inp["rel_bias_table"], "in_consts": consts, "in_onehot": onehot, "in_masks": masks,
        "in_gate": inp["moe_w_gate"], "in_up": inp["moe_w_up"], "in_down": inp["moe_w_down"],
    }
    arrays = {k: np.ascontiguousarray(v) for k, v in arrays.items()}
    nc = bacc.Bacc("TRN2", target_bir_lowering=False, num_devices=1)
    args = [nc.dram_tensor(k, v.shape, mybir.dt.from_np(v.dtype), kind="ExternalInput").ap() for k, v in arrays.items()]
    out = nc.dram_tensor("out", (1, T, D), F32, kind="ExternalOutput").ap()
    trunk(nc, *args, out, at)
    r = run_bass_kernel_spmd(nc, [arrays], core_ids=[0])
    return r.results[0]["out"]
```

```python
from contextlib import ExitStack

import numpy as np

import concourse.bass as bass
from concourse import mybir

F32 = mybir.dt.float32
I32 = mybir.dt.int32
ALU = mybir.AluOpType
ACT = mybir.ActivationFunctionType
AX = mybir.AxisListType

P = 128
T = 256
TT = T // P
D = 1024
KD = D // P
HALF = D // 2
HEADS = 8
HD = 64
DEPTH = 2
EPS = 1e-6
NEG = -1e30
MLA_QR, MLA_KVR, ROPE = 256, 128, 32
MLA_SCALE = float(HD + ROPE) ** -0.5
HEAD_SCALE = float(HD) ** -0.5
WINDOW = 128
BUCKETS, MAX_DIST = 32, 2048
GROUPS, PER_GROUP = 4, 8
EXPERTS = GROUPS * PER_GROUP
NR = GROUPS + EXPERTS
FE = 256
SLOTS = 32
LOT = P // SLOTS
LOTS = EXPERTS // LOT
ROUNDS = T // SLOTS
BUILDS = LOTS + 1
RING = 6
SLOT_COLS = KD * HALF
BLK = T + P


def shape_constants():
    p = np.arange(P)[:, None]
    q = np.arange(P)
    t = np.arange(T)
    parts = {}
    parts["ident"] = (p == q[None]).astype(np.float32)
    parts["earlier"] = (p < q[None]).astype(np.float32)
    parts["ones"] = np.ones((P, P), np.float32)
    parts["stack"] = (p % SLOTS == np.arange(SLOTS)[None]).astype(np.float32)
    parts["iota"] = np.broadcast_to(q.astype(np.float32), (P, P))
    parts["first4"] = np.broadcast_to(np.arange(GROUPS, 0, -1, dtype=np.float32), (P, GROUPS))
    parts["first32"] = np.broadcast_to(np.arange(EXPERTS, 0, -1, dtype=np.float32), (P, EXPERTS))
    parts["slot0"] = np.broadcast_to(SLOTS * np.arange(EXPERTS, dtype=np.float32), (P, EXPERTS))
    parts["limits"] = np.broadcast_to(SLOTS * np.arange(1, ROUNDS, dtype=np.float32), (P, ROUNDS - 1))
    freqs = (np.float32(10000.0) ** (-np.arange(0, ROPE, 2, dtype=np.float32) / np.float32(ROPE))).astype(np.float32)
    ang = np.arange(T, dtype=np.float32)[None, :] * freqs[:, None]
    cos, sin = np.cos(ang).astype(np.float32), np.sin(ang).astype(np.float32)
    one = np.ones((HD, T), np.float32)
    parts["qrope"] = np.concatenate([one, cos, cos, sin, -sin])
    parts["kcos"] = np.concatenate([one, cos, cos, cos, cos])
    parts["ksin"] = np.concatenate([one, -sin, sin, sin, -sin])
    k2, k1 = t[None, :], q[None, :]
    parts["causal"] = np.concatenate([np.where(k2 <= p + P, 0.0, NEG), np.where(k1 <= p, 0.0, NEG)], 1)
    parts["strict"] = np.concatenate([np.where(k2 < p + P, 0.0, NEG), np.where(k1 < p, 0.0, NEG)], 1)
    restart = np.zeros((P, BLK))
    restart[:, [T - 1, BLK - 1]] = 1.0
    parts["restart"] = restart
    at, n = {}, 0
    for name, a in parts.items():
        at[name] = (n, n + a.shape[1])
        n += a.shape[1]
    return np.ascontiguousarray(np.concatenate([np.asarray(a, np.float32) for a in parts.values()], 1)), at


def distance_constants():
    dist = T - 1 - np.arange(BLK)
    n = np.maximum(dist, 0)
    exact = BUCKETS // 2
    nf = np.maximum(n, 1).astype(np.float32)
    large = exact + (np.log(nf / np.float32(exact)) / np.float32(np.log(MAX_DIST / exact))
                     * np.float32(BUCKETS - exact)).astype(np.int32)
    bucket = np.where(n < exact, n, np.minimum(large, BUCKETS - 1))
    onehot = (np.arange(BUCKETS)[:, None] == bucket[None]).astype(np.float32)
    window = np.where((dist >= 0) & (dist < WINDOW), 0.0, NEG)
    causal = np.where(dist >= 0, 0.0, NEG)
    masks = np.broadcast_to(np.stack([window, causal]), (HEADS, 2, BLK)).astype(np.float32)
    return np.ascontiguousarray(onehot), np.ascontiguousarray(masks)


PAR = {}
_n = 0
for _name, _w in (("gmix0", KD), ("gmix1", KD), ("gffn0", KD), ("gffn1", KD), ("gq", 2), ("gkv", 1),
                  ("sinks", HEADS), ("rbias0", GROUPS + EXPERTS), ("rbias1", GROUPS + EXPERTS), ("gfinal", D)):
    PAR[_name] = (_n, _n + _w)
    _n += _w
PAR_COLS = _n


class Banks:

    def __init__(self, nc, ctx):
        self.t = [ctx.enter_context(nc.psum_tensor(f"bank{i}", [P, 512], F32)) for i in range(8)]
        self.full = [ctx.enter_context(nc.semaphore(f"bank{i}_full")) for i in range(8)]
        self.free = [ctx.enter_context(nc.semaphore(f"bank{i}_free")) for i in range(8)]
        self.uses = [0] * 8
        self.at = {}

    def plan(self, key, bank):
        self.at[key] = (bank, self.uses[bank])
        self.uses[bank] += 1

    def begin(self, pe, key):
        b, n = self.at[key]
        if n:
            pe.wait_ge(self.free[b], n)
        return self.t[b]

    def written(self, ins, key):
        ins.then_inc(self.full[self.at[key][0]], 1)

    def read(self, eng, key):
        b, n = self.at[key]
        eng.wait_ge(self.full[b], n + 1)
        return self.t[b]

    def taken(self, eng, key):
        b, n = self.at[key]
        eng.wait_ge(self.free[b], n + 1)

    def release(self, ins, key):
        ins.then_inc(self.free[self.at[key][0]], 1)


class Steps:

    def __init__(self, sem):
        self.sem, self.n = sem, 0

    def __call__(self, eng, ins):
        self.n += 1
        ins.then_inc(self.sem, 1)
        eng.wait_ge(self.sem, self.n)


def trunk(nc, x, stream, kvb, router_w, params, table, consts, onehot, masks, w_gate, w_up, w_down, out, at):
    ctx = ExitStack()
    with ctx:
        def sb(name, shape, dt=F32):
            return ctx.enter_context(nc.sbuf_tensor(name, shape, dt))

        sems = {}

        def sem(name):
            if name not in sems:
                sems[name] = ctx.enter_context(nc.semaphore(name))
            return sems[name]

        B = Banks(nc, ctx)
        bank = B.t
        bias_rows = nc.dram_tensor("bias_rows", [2, HEADS, P * (BLK + 1)], F32, kind="Internal").ap()

        ring = sb("ring", [P, RING, SLOT_COLS])
        con = sb("con", [P, consts.shape[1]])
        par = sb("par", [P, PAR_COLS])
        rw = sb("rw", [P, DEPTH, KD, GROUPS + EXPERTS])
        tab = sb("tab", [BUCKETS, HEADS])
        hot = sb("hot", [BUCKETS, BLK])
        msk = sb("msk", [HEADS, 2, BLK])
        rows = sb("rows", [HEADS, 2, BLK])
        h = sb("h", [P, TT, D])
        u = sb("u", [P, TT, D])
        uT = sb("uT", [P, KD, T])
        qk = sb("qk", [P, 2 * HEADS, T])
        qT, kT = qk[:, 0:HEADS, :], qk[:, HEADS:, :]
        swq = sb("swq", [P, 4, T])
        swk = sb("swk", [P, T])
        v1 = sb("v1", [P, TT, 512])
        v2 = sb("v2", [P, TT, 512])
        bias = sb("bias", [P, HEADS, BLK])
        sc = sb("sc", [P, 3, BLK])
        pr = sb("pr", [P, 3, BLK])
        cs = sb("cs", [P, 2, BLK])
        pt = sb("pt", [P, 2, BLK])
        nm = sb("nm", [P, 3, 10])
        nsink = sb("nsink", [P, HEADS])
        st = sb("st", [P, 16])
        lg = sb("lg", [P, TT, GROUPS + EXPERTS])
        mem = sb("mem", [P, TT, EXPERTS])
        nrounds = sb("nrounds", [P, 1], I32)
        rank = sb("rank", [P, TT, 2])
        base = sb("base", [P, TT, 2])
        gate = sb("gate", [P, TT, 2])
        cur = sb("cur", [P, TT, 2])
        sil = sb("sil", [P, 2, P])
        hT = sb("hT", [P, 2, P])

        def view(tile, a, shape):
            flat = tile[:, :, :].rearrange("p a b -> p (a b)")[:, a:a + int(np.prod(shape))]
            names = " ".join("abc"[:len(shape)])
            sizes = dict(zip("abc"[1:], shape[1:]))
            return flat.rearrange(f"p ({names}) -> p {names}", **sizes) if len(shape) > 1 else flat

        junk = view(sc, 0, [D])
        oT = view(u, 0, [KD, T])
        low, lowsq = sc[:, :, 0:T], pr[:, :, 0:T]
        lowr, krt = cs[:, :, 0:T], pt[:, :, 0:T]
        rt = view(v1, 0, [16, TT, EXPERTS])
        sel = view(v2, 0, [TT, P])
        wsel = view(v2, TT * P, [TT * 2, P])
        wT = view(v2, 3 * TT * P, [T])
        xg = view(bias, 0, [KD, P])
        part = view(bias, D, [2, 512])
        ys = view(bias, 2 * D, [2, HALF])
        after = view(cs, 0, [BLK + 1])

        def c(name, rows_=slice(0, P)):
            return con[rows_, at[name][0]:at[name][1]]

        def pcol(name, k=None):
            a, b = PAR[name]
            return par[:, a:b] if k is None else par[:, a + k:a + k + 1]

        ident, ones = c("ident"), c("ones")

        def gate_up(e, odd):
            return view(qk, 0, [SLOT_COLS]) if odd and e == 0 else ring[:, e, :]

        def win(s):
            return ring[:, s, :].rearrange("p (k n) -> p k n", k=KD)

        B.plan("rows", 7)
        upto = []
        for l in range(DEPTH):
            for b in range(4):
                B.plan(("uT", l, "mix", b), b)
            if l == 0:
                for i, b in enumerate((4, 5, 6, 7)):
                    B.plan(("low", i), b)
                for i in range(2):
                    B.plan(("swq", i), i)
                B.plan("swk", 2)
                B.plan("ssq", 4)
                B.plan("swv", 3)
                for i in range(4):
                    B.plan(("mk", i), (7, 2, 3, 4)[i])
                for i in range(TT):
                    B.plan(("mv", i), i)
                for i in range(4):
                    B.plan(("mq", i), (5, 6, 0, 1)[i])
            else:
                for i in range(12):
                    B.plan(("in1", i), (4 + i) % 8)
            for n in range(2 * HEADS):
                B.plan(("s", l, n), n % 3)
                B.plan(("t", l, n), 3 + n % 2)
                if n % 2 == 0:
                    B.plan(("o", l, n // 2), 5 + (n // 2) % 3)
            for i in range(4):
                B.plan(("out", l, i), i)
            for b in range(4):
                B.plan(("uT", l, "ffn", b), 4 + b)
            B.plan(("route parts", l), 1)
            B.plan(("route", l), 0)
            B.plan(("rank", l), 2)
            upto.append(list(B.uses))

        runs = [LOTS // 2] + [LOTS] * (RING - 1) + [LOTS // 2]
        moe0 = [1] * RING + [0]
        moe1 = [moe0[s] + runs[s] + (1, 1, 1, 1, 2, 2, 0)[s] for s in range(RING + 1)]

        land = {("in", 0): [0] * RING, ("moe", 0): [16] * RING + [0],
                ("in", 1): [16 + 32 * n for n in runs[:RING]], ("out", 1): [32 + 32 * n for n in runs[:RING]]}
        land[("moe", 1)] = [land[("in", 1)][s] + (16, 16, 16, 16, 32, 32)[s] for s in range(RING)] + [32 * runs[RING]]

        def arrived(eng, phase, s):
            eng.wait_ge(sem(f"slot{s}_landed"), land[phase][s] + 16)

        class Set:

            def use(self, e, odd, it, it2):
                return (RING if odd else 0, it2) if e == 0 else (e, it)

            def __init__(self, name, l, ring_base, land_base, own):
                self.name, self.l, self.free_base, self.land_base = name, l, ring_base, land_base
                self.sel_built = sem(f"{name}_sel_built")
                self.wsel_built = sem(f"{name}_wsel_built")
                self.sel_step = sem(f"{name}_sel_step")
                self.gathered = sem(f"{name}_gathered")
                self.x_ready = sem(f"{name}_x_ready")
                self.w_turned = sem(f"{name}_w_turned")
                self.w_ready = sem(f"{name}_w_ready")
                self.part_ready = sem(f"{name}_part_ready")
                self.summed = sem(f"{name}_summed")
                self.silu_ready = sem(f"{name}_silu_ready")
                self.h_ready = sem(f"{name}_h_ready")
                self.y_done = sem(f"{name}_y_done")
                self.y0_ready = sem(f"{name}_y0_ready")
                self.y1_ready = sem(f"{name}_y1_ready")
                self.combined = sem(f"{name}_combined")
                self.added = sem(f"{name}_added")
                self.landed = [sem(f"{'more' + str(l) + '_' if own else ''}slot{s}_landed") for s in range(RING + 1)]
                self.freed = [sem(f"{'more' + str(l) + '_' if own else ''}slot{s}_freed") for s in range(RING + 1)]

        main = [Set("moe", l, [a - n * l for a, n in zip((moe0, moe1)[l], runs)],
                    [a - 32 * n * l for a, n in zip(land[("moe", l)], runs)], False) for l in range(DEPTH)]
        more = [Set(f"more{l}", l, [1] * (RING + 1), [0] * (RING + 1), True) for l in range(DEPTH)]

        PLACING = 3
        AWAY = -65536.0

        def h_complete(eng, i):
            if i == 0:
                eng.wait_ge(sem("x_loaded"), 16 * TT)
            elif i % 2:
                for b in range(4):
                    B.taken(eng, ("out", i // 2, b))
            else:
                eng.wait_ge(sem("experts_added"), i // 2)

        def pv_done(eng, l, n):
            if n % 2 == 0:
                eng.wait_ge(sem("pv_even"), HEADS * l + n // 2 + 1)
            else:
                B.read(eng, ("o", l, n // 2))

        def is_sb(l, n):
            return l == 1 and n >= HEADS

        def swa_head(n):
            return (n - HEADS) // 2 + 4 * (n % 2)

        def in1_reads(eng, e, which):
            dst = ([qT[:, 2 * i:2 * i + 2, :] for i in (0, 1)] + [kT[:, 2 * i:2 * i + 2, :] for i in (0, 1)]
                   + [v1[:, i, :] for i in range(TT)]
                   + [qT[:, 4 + 2 * i:6 + 2 * i, :] for i in (0, 1)] + [kT[:, 4 + 2 * i:6 + 2 * i, :] for i in (0, 1)]
                   + [v2[:, i, :] for i in range(TT)])
            for i in range(12):
                if i % 2 == which:
                    src = B.read(eng, ("in1", i))
                    o = dst[i]
                    s = src[:, :] if i in (4, 5, 10, 11) else src[:, :].rearrange("p (c t) -> p c t", c=2)
                    if which:
                        ins = e.activation(o, s, ACT.Copy)
                    else:
                        ins = e.tensor_copy(o, s)
                    B.release(ins, ("in1", i))

        def act_lot(act, q, it, it2, odd):
            for e in range(LOT):
                s, n = q.use(e, odd, it, it2)
                act.wait_ge(q.freed[s], q.free_base[s] + 1 + n)
                if e >= 2:
                    act.wait_ge(q.summed, it * LOT + (e - 1))
                nc.scalar.activation(part[:, e % 2, :], bank[e % 2][:, :], ACT.Copy).then_inc(q.part_ready, 1)
            act.wait_ge(q.summed, it * LOT + LOT)
            nc.scalar.activation(sil[:, :, :], bank[2][:, 0:2 * P].rearrange("p (j s) -> p j s", j=2),
                                 ACT.Silu).then_inc(q.silu_ready, 1)
            act.wait_ge(q.y_done, it + 1)
            nc.scalar.activation(ys[:, 0, :], bank[4][:, :], ACT.Copy).then_inc(q.y0_ready, 1)

        def route(dve, V, l, step):
            NG = GROUPS

            def wide(a, n):
                return a.unsqueeze(2).broadcast_to([P, TT, n])

            src = B.read(dve, ("route parts", l))
            V.tensor_copy(part[0:NR, 0, 0:T], src[0:NR, 0:T]).then_inc(sem("logits0_ready"), 1)
            src = B.read(dve, ("route", l))
            dve.sem_inc(B.free[B.at[("route parts", l)][0]], 1)
            rb = pcol(f"rbias{l}").unsqueeze(1).broadcast_to([P, TT, NR])
            ins = V.tensor_tensor(lg[:, :, :], src[:, 0:TT * HD].rearrange("p (t n) -> p t n", t=TT)[:, :, 0:NR],
                                  rb, ALU.add)
            B.release(ins, ("route", l))
            B.taken(dve, ("route", l))
            G, E = lg[:, :, 0:NG], lg[:, :, NG:]
            best = rt[:, 0, :, 0:8]

            def col(i):
                return best[:, :, i]

            step(dve, V.tensor_reduce(col(0), G, AX.X, ALU.max))
            V.tensor_tensor(rt[:, 1, :, 0:NG], G, wide(col(0), NG), ALU.subtract).then_inc(sem("glog_ready"), 1)

            def first_max(x_, top, order, n_, tmp, mark):
                for tt in range(TT):
                    ins = V.scalar_tensor_tensor(out=tmp[:, tt, :], in0=x_[:, tt, :], scalar=best[:, tt, top:top + 1],
                                                 in1=order, op0=ALU.is_equal, op1=ALU.mult)
                step(dve, ins)
                step(dve, V.tensor_reduce(col(1), tmp, AX.X, ALU.max))
                step(dve, V.tensor_tensor(mark, tmp, wide(col(1), n_), ALU.is_equal))

            first_max(G, 0, c("first4"), NG, rt[:, 2, :, 0:NG], rt[:, 3, :, 0:NG])
            step(dve, V.tensor_scalar(rt[:, 2, :, 0:NG], rt[:, 3, :, 0:NG], 1.0, -NEG, ALU.subtract, ALU.mult))
            step(dve, V.tensor_tensor(rt[:, 4, :, :].rearrange("p t (g e) -> p t g e", g=NG),
                                      E.rearrange("p t (g e) -> p t g e", g=NG),
                                      rt[:, 2, :, 0:NG].unsqueeze(3).broadcast_to([P, TT, NG, PER_GROUP]), ALU.add))
            step(dve, V.tensor_reduce(col(2), rt[:, 4, :, :], AX.X, ALU.max))
            first_max(rt[:, 4, :, :], 2, c("first32"), EXPERTS, rt[:, 5, :, :], rt[:, 6, :, :])
            step(dve, V.scalar_tensor_tensor(out=rt[:, 4, :, :], in0=rt[:, 6, :, :], scalar=3.0 * NEG,
                                             in1=rt[:, 4, :, :], op0=ALU.mult, op1=ALU.add))
            step(dve, V.tensor_reduce(col(3), rt[:, 4, :, :], AX.X, ALU.max))
            first_max(rt[:, 4, :, :], 3, c("first32"), EXPERTS, rt[:, 5, :, :], rt[:, 7, :, :])
            V.tensor_tensor(mem[:, :, :], rt[:, 6, :, :], rt[:, 7, :, :], ALU.add).then_inc(sem("members"), 1)
            V.tensor_tensor(st[:, 10:12], col(3), col(2), ALU.subtract).then_inc(sem("gap_ready"), 1)


            def marked(dst, i, values):
                for tt in range(TT):
                    ins = V.tensor_tensor_reduce(rt[:, 8 + i, tt, :], rt[:, 6 + i, tt, :], values(tt), 1.0, 0.0,
                                                 ALU.mult, ALU.add, dst[:, tt, i:i + 1])
                return ins

            for i in range(2):
                ins = marked(base, i, lambda tt: c("slot0"))
            step(dve, ins)
            dve.wait_ge(sem("gexp_ready"), l + 1)
            step(dve, V.tensor_reduce(col(4), rt[:, 1, :, 0:NG], AX.X, ALU.add))
            dve.wait_ge(sem("gapexp_ready"), l + 1)
            step(dve, V.scalar_tensor_tensor(out=col(5), in0=st[:, 12:14], scalar=1.0, in1=col(4),
                                             op0=ALU.add, op1=ALU.mult))
            step(dve, V.reciprocal(gate[:, :, 0], col(5)))
            step(dve, V.tensor_tensor(gate[:, :, 1], gate[:, :, 0], st[:, 12:14], ALU.mult))
            src = B.read(dve, ("rank", l))
            for i in range(2):
                marked(rank, i, lambda tt: src[:, tt * EXPERTS:(tt + 1) * EXPERTS])
            ins = V.tensor_reduce(st[:, 14:15], src[:, TT * EXPERTS:(TT + 1) * EXPERTS], AX.X, ALU.max)
            B.release(ins, ("rank", l))
            B.taken(dve, ("rank", l))

        def count_rounds(dve, V, l, step):
            step(dve, V.tensor_scalar(rt[:, 10, 0, 0:ROUNDS - 1], c("limits"), st[:, 14:15], None, ALU.is_lt))
            step(dve, V.tensor_reduce(st[:, 15:16], rt[:, 10, 0, 0:ROUNDS - 1], AX.X, ALU.add))
            V.tensor_scalar(nrounds[:, :], st[:, 15:16], 1.0, None, ALU.add).then_inc(sem("rounds_known"), 1)

        def placing(V, later):
            over, pos, under = rt[:, 11, :, 0:2], rt[:, 12, :, 0:2], rt[:, 13, :, 0:2]
            V.tensor_scalar(over, rank[:, :, :], float(SLOTS), AWAY, ALU.is_ge, ALU.mult)
            ins = V.tensor_tensor(pos, base[:, :, :], rank[:, :, :], ALU.add)
            if later:
                yield V.tensor_scalar(under, rank[:, :, :], 0.0, AWAY, ALU.is_lt, ALU.mult)
                yield V.tensor_tensor(over, over, under, ALU.add)
            else:
                yield ins
            yield V.tensor_tensor(cur[:, :, :], pos, over, ALU.add)

        def place(dve, V, step):
            for ins in placing(V, False):
                step(dve, ins)

        def next_round(dve, V, l, r):
            s = sem(f"round_step{l}")
            n = (r - 1) * (PLACING + 1)
            V.tensor_scalar(rank[:, :, :], rank[:, :, :], float(SLOTS), None, ALU.subtract).then_inc(s, 1)
            dve.wait_ge(s, n + 1)
            for k, ins in enumerate(placing(V, True)):
                ins.then_inc(s, 1)
                dve.wait_ge(s, n + k + 2)

        def pick(dve, V, q, n):
            for tt in range(TT):
                ins = V.tensor_scalar(sel[:, tt, :], c("iota"), cur[:, tt, 0:1], None, ALU.is_equal)
            ins.then_inc(q.sel_step, 1)
            dve.wait_ge(q.sel_step, n * 2 + 1)
            for tt in range(TT):
                ins = V.scalar_tensor_tensor(out=sel[:, tt, :], in0=c("iota"), scalar=cur[:, tt, 1:2],
                                             in1=sel[:, tt, :], op0=ALU.is_equal, op1=ALU.add)
            ins.then_inc(q.sel_built, 1)
            for tt in range(TT):
                for i in range(2):
                    ins = V.tensor_scalar(wsel[:, 2 * tt + i, :], c("iota"), cur[:, tt, i:i + 1],
                                          gate[:, tt, i:i + 1], ALU.is_equal, ALU.mult)
            ins.then_inc(q.wsel_built, 1)
            dve.wait_ge(q.wsel_built, n + 1)
            V.tensor_scalar(cur[:, :, :], cur[:, :, :], float(P), None, ALU.subtract).then_inc(q.sel_step, 1)
            dve.wait_ge(q.sel_step, n * 2 + 2)
            V.memset(st[:, 9:10], 0.0)

        def dve_lot(dve, V, q, it, n):
            l = q.l
            gain = par[:, PAR[f"gffn{l}"][0]:PAR[f"gffn{l}"][1]]
            for hf in range(2):
                dve.wait_ge(q.gathered, it * 2 + (hf + 1))
                ks = slice(4 * hf, 4 * hf + 4)
                V.tensor_tensor(xg[:, ks, :], bank[(3, 2)[hf]][:, :].rearrange("p (k s) -> p k s", k=4),
                                gain[:, ks].unsqueeze(2).broadcast_to([P, 4, P]), ALU.mult).then_inc(q.x_ready, 1)
            dve.wait_ge(q.w_turned, it + 1)
            V.tensor_copy(wT[:, :], bank[4][:, 0:T]).then_inc(q.w_ready, 1)
            pick(dve, V, q, n)
            dve.wait_ge(q.silu_ready, it + 1)
            V.tensor_tensor(hT[:, :, :], sil[:, :, :], bank[2][:, 2 * P:4 * P].rearrange("p (j s) -> p j s", j=2),
                            ALU.mult).then_inc(q.h_ready, 1)
            dve.wait_ge(q.freed[RING - 1], q.free_base[RING - 1] + 1 + it)
            V.tensor_copy(ys[:, 1, :], bank[5][:, :]).then_inc(q.y1_ready, 1)
            for hf in range(2):
                for tt in range(TT):
                    dve.wait_ge(q.combined, it * 4 + (2 * hf + tt + 1))
                    dst = h[:, tt, hf * HALF:(hf + 1) * HALF]
                    V.tensor_tensor(dst, dst, bank[6 + tt][:, :], ALU.add).then_inc(q.added, 1)

        def keep_warm(n, o):
            for _ in range(n):
                nc.tensor.matmul(o[:, 0:T], ident, con[:, 0:T], start=True, stop=True)

        def pe_lot(pe, q, it, it2, odd, n):
            def mm(o, lhsT, rhs, start, stop, **kw):
                return nc.tensor.matmul(o, lhsT, rhs, start=start, stop=stop, **kw)

            pe.wait_ge(q.sel_built, n + 1)
            for hf in range(2):
                for k in range(4):
                    for tt in range(TT):
                        src = u[:, tt, :].rearrange("p (d k) -> p k d", k=KD)[:, 4 * hf + k, :]
                        ins = mm(bank[(3, 2)[hf]][:, k * P:(k + 1) * P], src, sel[:, tt, :], tt == 0, tt == TT - 1)
                ins.then_inc(q.gathered, 1)
            def turn_w():
                pe.wait_ge(q.wsel_built, n + 1)
                for tt in range(TT):
                    for i in range(2):
                        ins = mm(bank[4][:, tt * P:(tt + 1) * P], wsel[:, 2 * tt + i, :], ident, i == 0, i == 1)
                ins.then_inc(q.w_turned, 1)

            def total(e):
                pe.wait_ge(q.part_ready, it * LOT + (e + 1))
                for j in range(4):
                    ins = mm(bank[2][:, j * P + e * SLOTS:j * P + (e + 1) * SLOTS],
                             part[:, e % 2, j * P:(j + 1) * P], c("stack"), True, True)
                ins.then_inc(q.summed, 1)

            for e in range(LOT):
                s, before = q.use(e, odd, it, it2)
                pe.wait_ge(q.landed[s], q.land_base[s] + (before + 1) * 32)
                if e >= 2:
                    pe.wait_ge(q.part_ready, it * LOT + (e - 1))
                w = gate_up(e, odd).rearrange("p (w k f) -> p k w f", w=2, k=KD)
                for k in range(KD):
                    if e == 0 and k % 4 == 0:
                        pe.wait_ge(q.x_ready, it * 2 + (k // 4 + 1))
                    cg = SLOTS * (k % 4)
                    ins = mm(bank[e % 2][cg:cg + SLOTS, :].rearrange("p (w f) -> p w f", w=2),
                             xg[:, k, e * SLOTS:(e + 1) * SLOTS], w[:, k], k < 4, k >= 4)
                ins.then_inc(q.freed[s], 1)
                if e == 0:
                    turn_w()
                else:
                    total(e - 1)
            total(LOT - 1)
            pe.wait_ge(q.h_ready, it + 1)
            pe.wait_ge(q.w_ready, it + 1)
            for pair in range(LOT // 2):
                s = LOT + pair
                pe.wait_ge(q.landed[s], q.land_base[s] + (it + 1) * 32)
                w = ring[:, s, :].rearrange("p (e j n) -> p e j n", e=2, j=2)
                for hf in range(2):
                    for j in range(2):
                        for e in (2 * pair, 2 * pair + 1):
                            ins = mm(bank[4 + hf][e * SLOTS:(e + 1) * SLOTS, :], hT[:, j, e * SLOTS:(e + 1) * SLOTS],
                                     w[:, e % 2, j, hf * HALF:(hf + 1) * HALF], j == 0, j == 1)
                    if hf == 1:
                        ins.then_inc(q.freed[s], 1)
                    elif pair == 1:
                        ins.then_inc(q.y_done, 1)
            for hf in range(2):
                pe.wait_ge((q.y0_ready, q.y1_ready)[hf], it + 1)
                for tt in range(TT):
                    if hf:
                        pe.wait_ge(q.added, it * 4 + (tt + 1))
                    mm(bank[6 + tt][:, :], wT[:, tt * P:(tt + 1) * P], ys[:, hf, :], True, True)\
                        .then_inc(q.combined, 1)

        block = ctx.enter_context(nc.Block())

        @block.sync
        def _(sp):
            def up_loads(q, it, it2, odd, g, experts=range(LOT), first=False):
                for e in experts:
                    s, n = q.use(e, odd, it, it2)
                    if first:
                        B.read(sp, ("s", q.l, 2 * HEADS - 1))
                    else:
                        sp.wait_ge(q.freed[s], q.free_base[s] + n)
                    half = gate_up(e, odd).rearrange("p (w n) -> p w n", w=2)
                    for w, src in enumerate((w_gate, w_up)):
                        one = src[q.l, bass.ds(g * LOT + e, 1)].rearrange("e (p k) f -> p (e k f)", k=KD)
                        sp.dma_start(half[:, w, :], one).then_inc(q.landed[s], 16)

            def down_loads(q, it, g):
                for pair in range(LOT // 2):
                    s = LOT + pair
                    sp.wait_ge(q.freed[s], q.free_base[s] + it)
                    half = ring[:, s, :].rearrange("p (e j n) -> p e j n", e=2, j=2)
                    for e in range(2):
                        one = w_down[q.l, bass.ds(g * LOT + 2 * pair + e, 1)]
                        sp.dma_start(half[:, e], one.rearrange("e (j p) d -> p (e j) d", p=P))\
                          .then_inc(q.landed[s], 16)

            def expert_loads(q, it, it2, odd, g):
                up_loads(q, it, it2, odd, g)
                down_loads(q, it, g)

            def first_ahead(l):
                up_loads(main[l], LOTS * l + 1, LOTS // 2 * l, 1, 1, experts=(0,), first=True)

            def experts_from_first(l):
                it, it2 = LOTS * l, LOTS // 2 * l
                down_loads(main[l], it, 0)
                up_loads(main[l], it + 1, it2, 1, 1, experts=range(1, LOT))
                down_loads(main[l], it + 1, 1)
                with sp.Fori(1, LOTS // 2) as g2:
                    for odd in range(2):
                        expert_loads(main[l], it + g2 * 2 + odd, it2 + g2, odd, g2 * 2 + odd)

            def more_rounds(l):
                sp.wait_ge(sem("rounds_known"), l + 1)
                r_end = sp.value_load(nrounds[0:1, 0:1], min_val=1, max_val=ROUNDS)
                with sp.If(r_end > 1):
                    for s in range(RING + 1):
                        sp.wait_ge(main[l].freed[s], main[l].free_base[s] + runs[s] * (l + 1))
                    with sp.Fori(1, r_end) as r:
                        with sp.Fori(0, LOTS // 2) as g2:
                            for odd in range(2):
                                expert_loads(more[l], (r - 1) * LOTS + g2 * 2 + odd, (r - 1) * (LOTS // 2) + g2,
                                             odd, g2 * 2 + odd)
                    sp.wait_ge(sem("experts_added"), l + 1)
                with sp.Else():
                    sp.nop()

            for tt in range(TT):
                sp.dma_start(h[:, tt, :], x[0, tt * P:(tt + 1) * P, :]).then_inc(sem("x_loaded"), 16)
            sp.dma_start(par[:, 0:PAR_COLS - D], params[:, 0:PAR_COLS - D]).then_inc(sem("par_loaded"), 16)
            sp.dma_start(con[:, 0:P], consts[:, 0:P]).then_inc(sem("ident_loaded"), 16)
            half = SLOT_COLS // 2
            sp.dma_start(ring[:, 0, 0:half], stream[0, :, 0:half]).then_inc(sem("slot0_half_landed"), 16)
            sp.dma_start(ring[:, 0, half:], stream[0, :, half:]).then_inc(sem("slot0_landed"), 16)
            sp.dma_start(con[:, P:], consts[:, P:]).then_inc(sem("con_loaded"), 16)
            for s in (1, 2):
                sp.dma_start(ring[:, s, :], stream[s]).then_inc(sem(f"slot{s}_landed"), 16)
                if s == 1:
                    sp.dma_start(ring[:, 3, 0:1024], kvb).then_inc(sem("slot3_landed"), 16)
            for s in range(LOT, RING):
                sp.dma_start(ring[:, s, :], stream[s - 1]).then_inc(sem(f"slot{s}_landed"), 16)
            sp.dma_start(par[:, PAR_COLS - D:], params[:, PAR_COLS - D:]).then_inc(sem("gfinal_loaded"), 16)
            up_loads(main[0], 0, 0, 0, 0)
            first_ahead(0)
            experts_from_first(0)
            more_rounds(0)
            for s in range(RING):
                sp.wait_ge(sem(f"slot{s}_freed"), moe0[s] + runs[s])
                sp.dma_start(ring[:, s, :], stream[5 + s]).then_inc(sem(f"slot{s}_landed"), 16)
            up_loads(main[1], LOTS, LOTS // 2, 0, 0)
            for s in range(LOT, RING):
                sp.wait_ge(sem(f"slot{s}_freed"), moe0[s] + runs[s] + 1)
                sp.dma_start(ring[:, s, :], stream[11 + s - LOT]).then_inc(sem(f"slot{s}_landed"), 16)
            first_ahead(1)
            experts_from_first(1)
            more_rounds(1)
            for tt in range(TT):
                sp.wait_ge(sem("final_ready"), tt + 1)
                sp.dma_start(out[0, tt * P:(tt + 1) * P, :], u[:, tt, :]).then_inc(sem("stored"), 16)
            sp.wait_ge(sem("stored"), 16 * TT)

        @block.gpsimd
        def _(pool):
            pool.wait_ge(sem("rows_step"), 1)
            B.taken(pool, "rows")
            for w in range(2):
                skewed = bias_rows[w].rearrange("h (q x) -> h q x", q=P)[:, :, 0:BLK]
                pool.dma_start(skewed, rows[:, w, :].unsqueeze(1).broadcast_to([HEADS, P, BLK]))\
                    .then_inc(sem("rows_stored"), 16)
            pool.wait_ge(sem("rows_stored"), 32)

            def spread(w):
                for seg, (a, n) in enumerate(((0, T), (T, P))):
                    src_ap = bass.AP(bias_rows.tensor, w * HEADS * P * (BLK + 1) + P - 1 + seg * P,
                                     [[BLK, P], [P * (BLK + 1), HEADS], [1, n]])
                    pool.dma_start(bias[:, :, a:a + n], src_ap).then_inc(sem("bias_ready"), 16)

            spread(0)
            pool.wait_ge(sem("kr_parts"), 1)
            B.taken(pool, ("low", 3))
            src = [krt[HD:P, i, :].unsqueeze(1).broadcast_to([HD, HEADS, T]) for i in range(2)]
            nc.gpsimd.tensor_tensor(kT[HD:P, :, :], src[0], src[1], ALU.add).then_inc(sem("kr_ready"), 1)
            pool.wait_ge(sem("experts_added"), 1)
            spread(1)

        @block.scalar
        def _(act):
            step = Steps(sem("act_step"))
            act.dma_start(tab[:, :], table).then_inc(sem("tab_loaded"), 16)
            act.dma_start(hot[:, :], onehot).then_inc(sem("tab_loaded"), 16)
            act.dma_start(msk[:, :, :], masks).then_inc(sem("tab_loaded"), 16)
            act.dma_start(rw[:, :, :, :], router_w).then_inc(sem("par_loaded"), 16)

            def norm_half(i):
                act.wait_ge(sem("eps_ready"), 1)
                nc.scalar.activation(st[:, 6:7], st[:, 8:9], ACT.Sqrt)
                h_complete(act, i)
                act.wait_ge(sem("h_read"), i)
                nc.scalar.activation(junk[:, :], h[:, 0, :], ACT.Square,
                                     accum_out=st[:, 0:1]).then_inc(sem("ss_act"), 1)
                act.wait_ge(sem("ss_act"), i + 1)
                act.wait_ge(sem("ss_dve"), i + 1)
                nc.scalar.activation(st[:, 2:4], st[:, 0:2], ACT.Sqrt, bias=st[:, 8:9],
                                     scale=1.0 / D).then_inc(sem("std_ready"), 1)

            def normed_tile0(i):
                act.wait_ge(sem("rstd_ready"), i + 1)
                nc.scalar.activation(u[:, 0, :], h[:, 0, :], ACT.Copy, scale=st[:, 4:5])\
                  .then_inc(sem("u0_ready"), 1)

            def uT_banks(l, which):
                for b in (0, 2):
                    src = B.read(act, ("uT", l, which, b))
                    for j in range(2):
                        k = 2 * b + j
                        ins = nc.scalar.activation(uT[:, k, :], src[:, j * T:(j + 1) * T], ACT.Copy,
                                                   scale=pcol(f"g{which}{l}", k))
                    B.release(ins, ("uT", l, which, b))

            for l in range(DEPTH):
                norm_half(2 * l)
                normed_tile0(2 * l)
                if l == 0:
                    act.wait_ge(sem("par_loaded"), 32)
                uT_banks(l, "mix")
                if l == 0:
                    for i in range(2):
                        src = B.read(act, ("swq", i))
                        ins = nc.scalar.activation(swq[:, 2 * i:2 * i + 2, :],
                                                   src[:, :].rearrange("p (c t) -> p c t", c=2), ACT.Copy)
                        B.release(ins, ("swq", i))
                        if i == 0:
                            src = B.read(act, "ssq")
                            nc.scalar.activation(lowr[:, 0, :], src[:, 0:T], ACT.Sqrt, bias=st[:, 8:9], scale=1.0 / MLA_QR)
                            ins = nc.scalar.activation(lowr[:, 1, :], src[:, T:2 * T], ACT.Sqrt, bias=st[:, 8:9],
                                                       scale=1.0 / MLA_KVR)
                            B.release(ins, "ssq")
                    for i in range(4):
                        src = B.read(act, ("mk", i))
                        for j in range(2):
                            ins = nc.scalar.activation(kT[0:HD, 2 * i + j, :], src[HD * j:HD * (j + 1), 0:T], ACT.Copy)
                        B.release(ins, ("mk", i))
                else:
                    in1_reads(act, nc.scalar, 1)

                for i in range(2 * HEADS + 2):
                    if i < 2 * HEADS:
                        j = i % 3
                        if not is_sb(l, i):
                            act.wait_ge(sem("max_ready"), 2 * HEADS * l + i + 1)
                            if i >= 3:
                                B.read(act, ("t", l, i - 3))
                            nc.scalar.activation(pr[:, j, 0:T], sc[:, j, 0:T], ACT.Exp, bias=nm[:, j, 0:1],
                                                 accum_out=nm[:, j, 2:3])
                            ins = nc.scalar.activation(pr[:, j, T:BLK], sc[:, j, T:BLK], ACT.Exp,
                                                       bias=nm[:, j, 1:2], accum_out=nm[:, j, 3:4])
                            if l == 0 and i >= HEADS:
                                hh = swa_head(i)
                                ins = nc.scalar.activation(nm[:, j, 4:6], nm[:, j, 0:2], ACT.Exp,
                                                           bias=pcol("sinks", hh))
                            ins.then_inc(sem("exp_ready"), 1)
                        else:
                            B.taken(act, ("s", l, i))
                            B.read(act, ("t", l, i - 3))
                            nc.scalar.activation(pr[:, j, :], sc[:, j, :], ACT.Sigmoid, scale=-1.0)\
                              .then_inc(sem("left_ready"), 1)
                            nc.scalar.activation(sc[:, j, :], sc[:, j, :], ACT.Sigmoid)\
                              .then_inc(sem("share_ready"), 1)
                    if i >= 2:
                        n = i - 2
                        src = B.read(act, ("t", l, n))
                        if n >= 2:
                            pv_done(act, l, n - 2)
                        ins = nc.scalar.activation(pt[:, n % 2, :], src[:, 0:BLK], ACT.Copy)
                        B.release(ins, ("t", l, n))

                norm_half(2 * l + 1)
                normed_tile0(2 * l + 1)
                uT_banks(l, "ffn")
                src = B.read(act, ("route parts", l))
                nc.scalar.activation(part[0:NR, 0, T:2 * T], src[HD:HD + NR, 0:T], ACT.Copy)\
                  .then_inc(sem("logits1_ready"), 1)
                act.wait_ge(sem("glog_ready"), l + 1)
                nc.scalar.activation(rt[:, 1, :, 0:GROUPS], rt[:, 1, :, 0:GROUPS], ACT.Exp)\
                  .then_inc(sem("gexp_ready"), 1)
                act.wait_ge(sem("gap_ready"), l + 1)
                nc.scalar.activation(st[:, 12:14], st[:, 10:12], ACT.Exp).then_inc(sem("gapexp_ready"), 1)

                with act.Fori(0, LOTS // 2) as g2:
                    for odd in range(2):
                        act_lot(act, main[l], LOTS * l + g2 * 2 + odd, LOTS // 2 * l + g2, odd)
                act.wait_ge(sem("rounds_known"), l + 1)
                r_end = act.value_load(nrounds[0:1, 0:1], min_val=1, max_val=ROUNDS)
                with act.If(r_end > 1):
                    with act.Fori(1, r_end) as r:
                        with act.Fori(0, LOTS // 2) as g2:
                            for odd in range(2):
                                act_lot(act, more[l], (r - 1) * LOTS + g2 * 2 + odd,
                                        (r - 1) * (LOTS // 2) + g2, odd)
                with act.Else():
                    act.nop()
            norm_half(2 * DEPTH)

        @block.vector
        def _(dve):
            step = Steps(sem("dve_step"))
            V = nc.vector
            step(dve, V.memset(st[:, 8:9], EPS))
            V.memset(st[:, 9:10], 0.0).then_inc(sem("eps_ready"), 1)

            def bias_over_distances():
                dve.wait_ge(sem("par_loaded"), 32)
                dve.wait_ge(sem("tab_loaded"), 48)
                step(dve, V.tensor_scalar(nsink[:, :], pcol("sinks"), -1.0, None, ALU.mult))
                src = B.read(dve, "rows")
                for w in range(2):
                    ins = V.scalar_tensor_tensor(out=rows[:, w, :], in0=src[0:HEADS, 0:BLK], scalar=1.0 / HEAD_SCALE,
                                                 in1=msk[:, w, :], op0=ALU.mult, op1=ALU.add)
                    if w == 0:
                        ins.then_inc(sem("rows_step"), 1)
                B.release(ins, "rows")

            def roots(i):
                h_complete(dve, i)
                V.tensor_tensor_reduce(u[:, 1, :], h[:, 1, :], h[:, 1, :], 1.0, 0.0, ALU.mult, ALU.add,
                                       st[:, 1:2]).then_inc(sem("ss_dve"), 1)
                dve.wait_ge(sem("std_ready"), i + 1)
                V.reciprocal(st[:, 4:6], st[:, 2:4]).then_inc(sem("rstd_ready"), 1)
                dve.wait_ge(sem("rstd_ready"), i + 1)
                dve.wait_ge(sem("ss_dve"), i + 1)

            def norm_turn(i, l, which):
                roots(i)
                V.tensor_scalar(u[:, 1, :], h[:, 1, :], st[:, 5:6], None, ALU.mult).then_inc(sem("u1_ready"), 1)
                if i == 0:
                    bias_over_distances()
                for b in (1, 3):
                    src = B.read(dve, ("uT", l, which, b))
                    for j in range(2):
                        k = 2 * b + j
                        ins = V.tensor_scalar(uT[:, k, :], src[:, j * T:(j + 1) * T], pcol(f"g{which}{l}", k),
                                              None, ALU.mult)
                    B.release(ins, ("uT", l, which, b))
                dve.wait_ge(sem("u0_ready"), i + 1)
                dve.wait_ge(sem("u1_ready"), i + 1)
                dve.sem_inc(sem("h_read"), 1)

            for l in range(DEPTH):
                norm_turn(2 * l, l, "mix")
                if l == 0:
                    for i in range(3):
                        src = B.read(dve, ("low", i))
                        ins = V.tensor_copy(low[:, i, :], src[:, 0:T])
                        B.release(ins, ("low", i))
                        B.taken(dve, ("low", i))
                        V.tensor_tensor(lowsq[:, i, :], low[:, i, :], low[:, i, :], ALU.mult)\
                         .then_inc(sem("lowsq_ready"), 1)
                    src = B.read(dve, ("low", 3))
                    dve.wait_ge(sem("con_loaded"), 16)
                    V.tensor_tensor(krt[HD:P, 0, :], src[0:HD, 0:T], c("kcos", slice(HD, P)), ALU.mult)\
                     .then_inc(sem("kr_parts"), 1)
                    ins = V.tensor_tensor(krt[HD:P, 1, :], src[HD:P, 0:T], c("ksin", slice(HD, P)), ALU.mult)
                    B.release(ins, ("low", 3))
                    B.taken(dve, "ssq")
                    step(dve, V.reciprocal(lowr[:, :, :], lowr[:, :, :]))
                    for i in range(3):
                        g = pcol("gkv", 0) if i == 2 else pcol("gq", i)
                        V.scalar_tensor_tensor(out=low[:, i, :], in0=low[:, i, :], scalar=g,
                                               in1=lowr[:, i // 2, :], op0=ALU.mult, op1=ALU.mult)\
                         .then_inc(sem("lown_ready"), 1)
                    src = B.read(dve, "swk")
                    ins = V.tensor_copy(swk[:, :], src[:, 0:T])
                    B.release(ins, "swk")
                    src = B.read(dve, "swv")
                    ins = V.tensor_copy(v2[:, :, 0:P], src[:, 0:2 * P].rearrange("p (t n) -> p t n", t=TT))
                    B.release(ins, "swv")
                    for i in range(TT):
                        src = B.read(dve, ("mv", i))
                        ins = V.tensor_copy(v1[:, i, :], src[:, :])
                        B.release(ins, ("mv", i))
                    for i in range(4):
                        src = B.read(dve, ("mq", i))
                        ins = V.tensor_tensor(qT[:, 2 * i:2 * i + 2, :], src[:, :].rearrange("p (c t) -> p c t", c=2),
                                              c("qrope").unsqueeze(1).broadcast_to([P, 2, T]), ALU.mult)
                        B.release(ins, ("mq", i))
                else:
                    in1_reads(dve, V, 0)

                for i in range(2 * HEADS + 6):
                    if i < 2 * HEADS:
                        j = i % 3
                        src = B.read(dve, ("s", l, i))
                        if i >= 3 and not is_sb(l, i - 3):
                            dve.wait_ge(sem("exp_ready"), 2 * HEADS * l + i - 2)
                        if l == 0 and i < HEADS:
                            scale, add = MLA_SCALE, c("causal")
                        elif l == 0:
                            scale, add = HEAD_SCALE, bias[:, swa_head(i), :]
                            dve.wait_ge(sem("bias_ready"), 32)
                        elif i < HEADS:
                            scale, add = HEAD_SCALE, bias[:, i, :]
                            dve.wait_ge(sem("bias_ready"), 64)
                        else:
                            scale, add = HEAD_SCALE, c("strict")
                        if is_sb(l, i):
                            ins = V.scalar_tensor_tensor(out=sc[:, j, :], in0=src[:, 0:BLK], scalar=scale, in1=add,
                                                         op0=ALU.mult, op1=ALU.add)
                            B.release(ins, ("s", l, i))
                        else:
                            for seg, (c0, c1) in enumerate(((0, T), (T, BLK))):
                                ins = V.tensor_tensor_reduce(sc[:, j, c0:c1], src[:, c0:c1], add[:, c0:c1], scale,
                                                             -3e38, ALU.add, ALU.max, nm[:, j, 8 + seg:9 + seg])
                            B.release(ins, ("s", l, i))
                            B.taken(dve, ("s", l, i))
                            sink = nsink[:, swa_head(i):swa_head(i) + 1] if l == 0 and i >= HEADS else None
                            ins = V.tensor_scalar(nm[:, j, 0:2], nm[:, j, 8:10], -1.0, sink, ALU.mult,
                                                  *(() if sink is None else (ALU.min,)))
                            ins.then_inc(sem("max_ready"), 1)
                    n = i - 1
                    if is_sb(l, n) and n < 2 * HEADS:
                        j = n % 3
                        if n == HEADS:
                            step(dve, V.memset(after[:, BLK:BLK + 1], 1.0))
                        dve.wait_ge(sem("left_ready"), n - HEADS + 1)
                        if n > HEADS:
                            dve.wait_ge(sem("sb_ready"), n - HEADS)
                        step(dve, V.tensor_tensor_scan(after[:, 0:BLK][:, ::-1], pr[:, j, ::-1],
                                                       c("restart")[:, ::-1], 1.0, ALU.mult, ALU.max))
                        dve.wait_ge(sem("share_ready"), n - HEADS + 1)
                        V.tensor_tensor(pr[:, j, :], sc[:, j, :], after[:, 1:BLK + 1], ALU.mult)\
                         .then_inc(sem("sb_ready"), 1)
                    elif 0 <= n < 2 * HEADS:
                        j = n % 3
                        dve.wait_ge(sem("exp_ready"), 2 * HEADS * l + n + 1)
                        if l == 0 and n >= HEADS:
                            step(dve, V.tensor_tensor(nm[:, j, 2:4], nm[:, j, 2:4], nm[:, j, 4:6], ALU.add))
                        step(dve, V.reciprocal(nm[:, j, 6:8], nm[:, j, 2:4]))
                        V.tensor_scalar(pr[:, j, 0:T], pr[:, j, 0:T], nm[:, j, 6:7], None, ALU.mult)
                        V.tensor_scalar(pr[:, j, T:BLK], pr[:, j, T:BLK], nm[:, j, 7:8], None, ALU.mult)\
                         .then_inc(sem("p_ready"), 1)
                    n = i - 4
                    if n >= 1 and n % 2 == 1 and n < 2 * HEADS:
                        src = B.read(dve, ("o", l, n // 2))
                        ins = V.tensor_copy(oT[:, n // 2, :], src[:, 0:T])
                        B.release(ins, ("o", l, n // 2))

                for i in range(4):
                    src = B.read(dve, ("out", l, i))
                    tt, hf = i // 2, i % 2
                    dst = h[:, tt, hf * HALF:(hf + 1) * HALF]
                    ins = V.tensor_tensor(dst, dst, src[:, :], ALU.add)
                    B.release(ins, ("out", l, i))

                norm_turn(2 * l + 1, l, "ffn")
                route(dve, V, l, step)
                place(dve, V, step)
                pick(dve, V, main[l], BUILDS * l)
                count_rounds(dve, V, l, step)
                with dve.Fori(0, LOTS) as g:
                    dve_lot(dve, V, main[l], LOTS * l + g, BUILDS * l + g + 1)
                dve.wait_ge(sem("rounds_known"), l + 1)
                r_end = dve.value_load(nrounds[0:1, 0:1], min_val=1, max_val=ROUNDS)
                with dve.If(r_end > 1):
                    with dve.Fori(1, r_end) as r:
                        next_round(dve, V, l, r)
                        pick(dve, V, more[l], (r - 1) * BUILDS)
                        with dve.Fori(0, LOTS) as g:
                            dve_lot(dve, V, more[l], (r - 1) * LOTS + g, (r - 1) * BUILDS + g + 1)
                        dve.wait_ge(more[l].added, r * (LOTS * 4))
                    V.memset(st[:, 9:10], 0.0).then_inc(sem("experts_added"), 1)
                with dve.Else():
                    dve.wait_ge(main[l].added, LOTS * (l + 1) * 4)
                    V.memset(st[:, 9:10], 0.0).then_inc(sem("experts_added"), 1)

            roots(2 * DEPTH)
            dve.wait_ge(sem("gfinal_loaded"), 16)
            for tt in range(TT):
                V.scalar_tensor_tensor(out=u[:, tt, :], in0=h[:, tt, :], scalar=st[:, 4 + tt:5 + tt],
                                       in1=pcol("gfinal"), op0=ALU.mult, op1=ALU.mult)\
                 .then_inc(sem("final_ready"), 1)


        @block.tensor
        def _(pe):
            spent = []

            def carry(ins):
                if spent:
                    ins.then_inc(sem(f"slot{spent.pop()}_freed"), 1)
                return ins

            def mm(o, lhsT, rhs, start, stop, **kw):
                return carry(nc.tensor.matmul(o, lhsT, rhs, start=start, stop=stop, **kw))

            pe.wait_ge(sem("tab_loaded"), 48)
            o = B.begin(pe, "rows")
            B.written(mm(o[0:HEADS, 0:BLK], tab[:, :], hot[:, :], True, True), "rows")

            def turn_u(i, l, which):
                for tt in range(TT):
                    pe.wait_ge(sem(f"u{tt}_ready"), i + 1)
                    if i == 0 and tt == 0:
                        pe.wait_ge(sem("ident_loaded"), 16)
                    for b in range(4):
                        o = B.begin(pe, ("uT", l, which, b)) if tt == 0 else bank[B.at[("uT", l, which, b)][0]]
                        for j in range(2):
                            src = u[:, tt, :].rearrange("p (d k) -> p k d", k=KD)[:, 2 * b + j, :]
                            ins = carry(nc.tensor.transpose(o[:, j * T + tt * P:j * T + (tt + 1) * P], src, ident))
                        if tt == TT - 1:
                            B.written(ins, ("uT", l, which, b))

            def turned(l, which, k):
                if k % 2 == 0:
                    B.taken(pe, ("uT", l, which, k // 2))

            def featured(o, w, cols, M, first=None):
                for k in range(KD):
                    if first is not None:
                        turned(first, "mix", k)
                    ins = mm(o[0:M, :], w[:, k, cols:cols + M], uT[:, k, :], k == 0, k == KD - 1)
                return ins

            def tokened(o, w, tt, cols, n):
                for k in range(KD):
                    ins = mm(o, uT[:, k, tt * P:(tt + 1) * P], w[:, k, cols:cols + n], k == 0, k == KD - 1)
                return ins

            def slot_freed(s):
                spent.append(s)

            for l in range(DEPTH):
                turn_u(2 * l, l, "mix")
                if l == 0:
                    w = win(0)
                    outs = [B.begin(pe, ("low", i)) for i in range(4)]
                    for k in range(KD):
                        if k == 0:
                            pe.wait_ge(sem("slot0_half_landed"), 16)
                        if k == KD // 2:
                            arrived(pe, ("in", 0), 0)
                        turned(0, "mix", k)
                        for i in range(4):
                            ins = mm(outs[i][:, 0:T], w[:, k, i * P:(i + 1) * P], uT[:, k, :], k == 0, k == KD - 1)
                            if k == KD - 1:
                                B.written(ins, ("low", i))
                    slot_freed(0)
                    arrived(pe, ("in", 0), 1)
                    w = win(1)
                    for i in range(2):
                        o = B.begin(pe, ("swq", i))
                        for j in range(2):
                            ins = featured(o[:, j * T:(j + 1) * T], w, (2 * i + j) * P, P)
                        B.written(ins, ("swq", i))
                        if i == 0:
                            pe.wait_ge(sem("con_loaded"), 16)
                            pe.wait_ge(sem("lowsq_ready"), 3)
                            o = B.begin(pe, "ssq")
                            mm(o[:, 0:T], ones, lowsq[:, 0, :], True, False)
                            mm(o[:, 0:T], ones, lowsq[:, 1, :], False, True)
                            B.written(mm(o[:, T:2 * T], ones, lowsq[:, 2, :], True, True), "ssq")
                    slot_freed(1)
                    arrived(pe, ("in", 0), 2)
                    w = ring[:, 2, 0:KD * T].rearrange("p (k n) -> p k n", k=KD)
                    o = B.begin(pe, "swk")
                    B.written(featured(o[:, 0:T], w, 0, P), "swk")
                    o = B.begin(pe, "swv")
                    for tt in range(TT):
                        ins = tokened(o[:, tt * P:(tt + 1) * P], w, tt, P, P)
                    B.written(ins, "swv")
                    arrived(pe, ("in", 0), 3)
                    pe.wait_ge(sem("lown_ready"), 3)
                    for i in range(4):
                        o = B.begin(pe, ("mk", i))
                        B.written(mm(o[:, 0:T], ring[:, 3, i * P:(i + 1) * P], low[:, 2, :], True, True), ("mk", i))
                    for tt in range(TT):
                        o = B.begin(pe, ("mv", tt))
                        ins = mm(o[:, :], low[:, 2, tt * P:(tt + 1) * P], ring[:, 3, 512:1024], True, True)
                        B.written(ins, ("mv", tt))
                    slot_freed(3)
                    wq = ring[:, 2, KD * T:].rearrange("p (k n) -> p k n", k=2)
                    for i in range(4):
                        o = B.begin(pe, ("mq", i))
                        for j in range(2):
                            hh = 2 * i + j
                            for k in range(2):
                                ins = mm(o[:, j * T:(j + 1) * T], wq[:, k, hh * P:(hh + 1) * P], low[:, k, :],
                                         k == 0, k == 1)
                        B.written(ins, ("mq", i))
                    slot_freed(2)
                    pe.wait_ge(sem("kr_ready"), 1)
                    for key in [("mk", i) for i in range(4)] + [("mv", 0), ("mv", 1)]:
                        B.taken(pe, key)
                else:
                    n = 0
                    for s in range(RING):
                        arrived(pe, ("in", 1), s)
                        w = win(s)
                        for i in range(2):
                            o = B.begin(pe, ("in1", n))
                            if s % 3 == 2:
                                ins = tokened(o[:, :], w, i, 0, 512)
                            else:
                                for j in range(2):
                                    ins = featured(o[:, j * T:(j + 1) * T], w, (2 * i + j) * P, P,
                                                   first=l if n == 0 and j == 0 else None)
                            B.written(ins, ("in1", n))
                            n += 1
                        slot_freed(s)
                    for i in range(6):
                        B.taken(pe, ("in1", i))

                def operands(n):
                    if l == 0 and n < HEADS:
                        return qT[:, n, :], kT[:, n, :]
                    p0 = HD * (n % 2)
                    if l == 0:
                        return swq[p0:p0 + HD, (n - HEADS) // 2, :], swk[p0:p0 + HD, :]
                    return qT[p0:p0 + HD, n // 2, :], kT[p0:p0 + HD, n // 2, :]

                def values(n, tt):
                    if l == 0 and n >= HEADS:
                        return v2[:, tt, HD * (n % 2):HD * (n % 2) + HD]
                    return (v1 if n < HEADS else v2)[:, tt, (n % HEADS) * HD:(n % HEADS + 1) * HD]

                def logits(n):
                    if l == 0 and n < HEADS and n % 2 == 0:
                        B.taken(pe, ("mq", n // 2))
                    if n == HEADS:
                        for key in ([("swq", 0), ("swq", 1), "swk", "swv"] if l == 0
                                    else [("in1", i) for i in range(6, 12)]):
                            B.taken(pe, key)
                    q_, k_ = operands(n)
                    o = B.begin(pe, ("s", l, n))
                    mm(o[:, 0:T], q_[:, P:T], k_, True, True)
                    B.written(mm(o[:, T:BLK], q_[:, 0:P], k_[:, 0:P], True, True), ("s", l, n))

                logits(0)
                for i in range(2 * HEADS + 3):
                    if i + 1 < 2 * HEADS:
                        logits(i + 1)
                    n = i - 2
                    if 0 <= n < 2 * HEADS:
                        if is_sb(l, n):
                            pe.wait_ge(sem("sb_ready"), n - HEADS + 1)
                        else:
                            pe.wait_ge(sem("p_ready"), 2 * HEADS * l + n + 1)
                        w = pr[:, n % 3, :]
                        o = B.begin(pe, ("t", l, n))
                        nc.tensor.transpose(o[:, 0:P], w[:, T:BLK], ident)
                        nc.tensor.transpose(o[:, P:2 * P], w[:, 0:P], ident)
                        ins = nc.tensor.transpose(o[:, 2 * P:3 * P], w[:, P:2 * P], ident)
                        B.written(ins, ("t", l, n))
                    n = i - 3
                    if n >= 0:
                        B.taken(pe, ("t", l, n))
                        p0 = HD * (n % 2)
                        o = B.begin(pe, ("o", l, n // 2)) if n % 2 == 0 else bank[B.at[("o", l, n // 2)][0]]
                        mm(o[p0:p0 + HD, 0:T], values(n, 0), pt[:, n % 2, 0:T], True, True)
                        ins = mm(o[p0:p0 + HD, P:T], values(n, 1), pt[:, n % 2, T:BLK], False, True,
                                 skip_group_check=True)
                        if n % 2 == 0:
                            ins.then_inc(sem("pv_even"), 1)
                        else:
                            B.written(ins, ("o", l, n // 2))

                for i in range(4):
                    tt, hf = i // 2, i % 2
                    s = LOT + hf
                    if tt == 0:
                        arrived(pe, ("in", 0) if l == 0 else ("out", 1), s)
                    o = B.begin(pe, ("out", l, i))
                    for k in range(KD):
                        if i == 0:
                            B.taken(pe, ("o", l, k))
                        ins = mm(o[:, :], oT[:, k, tt * P:(tt + 1) * P], win(s)[:, k, :], k == 0, k == KD - 1)
                    B.written(ins, ("out", l, i))
                    if tt == 1:
                        slot_freed(s)

                turn_u(2 * l + 1, l, "ffn")
                o = B.begin(pe, ("route parts", l))
                for k in range(KD):
                    turned(l, "ffn", k)
                    p0 = HD * (k % 2)
                    ins = mm(o[p0:p0 + NR, 0:T], rw[:, l, k, :], uT[:, k, :], k < 2, k >= KD - 2)
                B.written(ins, ("route parts", l))
                o = B.begin(pe, ("route", l))
                pe.wait_ge(sem("logits0_ready"), l + 1)
                pe.wait_ge(sem("logits1_ready"), l + 1)
                for tt in range(TT):
                    for which in range(2):
                        ins = mm(o[:, tt * HD:tt * HD + NR], part[0:NR, 0, which * T + tt * P:which * T + (tt + 1) * P],
                                 ident[0:NR, 0:NR], which == 0, which == 1)
                B.written(ins, ("route", l))
                keep_warm(6, bank[7])
                pe.wait_ge(sem("members"), l + 1)
                o = B.begin(pe, ("rank", l))
                both = mem[:, :, :].rearrange("p t e -> p (t e)")
                mm(o[:, 0:2 * EXPERTS], c("earlier"), both, True, False)
                mm(o[:, EXPERTS:2 * EXPERTS], ones, mem[:, 0, :], False, True)
                mm(o[:, 2 * EXPERTS:3 * EXPERTS], ones, mem[:, 0, :], True, False)
                ins = mm(o[:, 2 * EXPERTS:3 * EXPERTS], ones, mem[:, 1, :], False, True)
                B.written(ins, ("rank", l))
                keep_warm(4, bank[7])
                for b in range(8):
                    pe.wait_ge(B.free[b], upto[l][b])

                with pe.Fori(0, LOTS // 2) as g2:
                    for odd in range(2):
                        pe_lot(pe, main[l], LOTS * l + g2 * 2 + odd, LOTS // 2 * l + g2, odd,
                               BUILDS * l + g2 * 2 + odd)
                pe.wait_ge(sem("rounds_known"), l + 1)
                r_end = pe.value_load(nrounds[0:1, 0:1], min_val=1, max_val=ROUNDS)
                with pe.If(r_end > 1):
                    for s in range(RING + 1):
                        pe.sem_inc(more[l].freed[s], 1)
                    pe.wait_ge(main[l].added, LOTS * (l + 1) * 4)
                    with pe.Fori(1, r_end) as r:
                        with pe.Fori(0, LOTS // 2) as g2:
                            for odd in range(2):
                                pe_lot(pe, more[l], (r - 1) * LOTS + g2 * 2 + odd,
                                       (r - 1) * (LOTS // 2) + g2, odd, (r - 1) * BUILDS + g2 * 2 + odd)
                with pe.Else():
                    pe.nop()
                pe.wait_ge(sem("experts_added"), l + 1)

def _stream(inp):
    def cols(w, parts):
        return np.ascontiguousarray(np.concatenate([w[:, a:b] for a, b in parts], 1)).reshape(P, -1)

    w0 = inp["w_in_even"][0]
    kr = MLA_QR + MLA_KVR
    half = ROPE // 2
    a, b = (kr, kr + half), (kr + half, kr + ROPE)
    qs = kr + ROPE
    slots = [cols(w0, [(0, kr), a, b, b, a, b, a, a, b])]
    heads = [(qs + HD * n, qs + HD * (n + 1)) for i in range(4) for n in (i, 4 + i)]
    slots.append(cols(w0, heads))
    ks = qs + HEADS * HD
    wq = inp["w_mla_qb"][0].reshape(2, P, HEADS, HD + ROPE)
    wq = np.concatenate([wq, wq[..., HD:]], -1).transpose(1, 0, 2, 3).reshape(P, -1)
    slots.append(np.concatenate([cols(w0, [(ks, ks + 256)]), wq], 1))
    wo = inp["w_out_even"][0].reshape(16, HD, D)
    order = list(range(8)) + [n for i in range(4) for n in (8 + i, 12 + i)]
    wo = wo[order].reshape(KD, P, D).transpose(1, 0, 2)
    slots += [wo[:, :, i * HALF:(i + 1) * HALF].reshape(P, -1) for i in range(2)]
    w1 = inp["w_in_odd"][0]
    slots += [cols(w1, [(512 * i, 512 * i + 512)]) for i in range(6)]
    wo = inp["w_out_odd"][0].reshape(KD, P, D).transpose(1, 0, 2)
    slots += [wo[:, :, i * HALF:(i + 1) * HALF].reshape(P, -1) for i in range(2)]
    return np.ascontiguousarray(np.stack(slots))


def kernel(**inputs):
    import concourse.bacc as bacc
    from concourse.bass_utils import run_bass_kernel_spmd

    inp = {k: np.asarray(v) for k, v in inputs.items()}
    consts, at = shape_constants()
    onehot, masks = distance_constants()
    kv = inp["w_mla_kvb"][0].reshape(P, HEADS, 2 * HD)
    par = np.empty((P, PAR_COLS), np.float32)

    def put(name, v):
        par[:, PAR[name][0]:PAR[name][1]] = v

    for l in range(DEPTH):
        put(f"gmix{l}", inp["norm_mix"][l].reshape(P, KD))
        put(f"gffn{l}", inp["norm_ffn"][l].reshape(P, KD))
        put(f"rbias{l}", np.concatenate([inp["moe_b_group"][l], inp["moe_b_router"][l]])[None])
    put("gq", inp["g_mla_q"][0].reshape(2, P).T)
    put("gkv", inp["g_mla_kv"][0].reshape(1, P).T)
    put("sinks", inp["swa_sinks"][0][None])
    put("gfinal", inp["norm_final"][None])
    rw = np.concatenate([inp["moe_w_group"], inp["moe_w_router"]], -1).reshape(DEPTH, P, KD, GROUPS + EXPERTS)
    arrays = {
        "in_x": inp["x"], "in_stream": _stream(inp),
        "in_kvb": np.ascontiguousarray(np.concatenate([kv[:, :, :HD].reshape(P, -1), kv[:, :, HD:].reshape(P, -1)], 1)),
        "in_router": np.ascontiguousarray(rw.transpose(1, 0, 2, 3)), "in_params": par,
        "in_table": inp["rel_bias_table"], "in_consts": consts, "in_onehot": onehot, "in_masks": masks,
        "in_gate": inp["moe_w_gate"], "in_up": inp["moe_w_up"], "in_down": inp["moe_w_down"],
    }
    arrays = {k: np.ascontiguousarray(v) for k, v in arrays.items()}
    nc = bacc.Bacc("TRN2", target_bir_lowering=False, num_devices=1)
    args = [nc.dram_tensor(k, v.shape, mybir.dt.from_np(v.dtype), kind="ExternalInput").ap() for k, v in arrays.items()]
    out = nc.dram_tensor("out", (1, T, D), F32, kind="ExternalOutput").ap()
    trunk(nc, *args, out, at)
    r = run_bass_kernel_spmd(nc, [arrays], core_ids=[0])
    return r.results[0]["out"]
```
